# Optimizing a Trainium2 kernel written in Bass

```python
import jax, jax.numpy as jnp
from jax import lax
import numpy as np

D_MODEL = 2048
BATCH = 1
SEQ = 512
DEPTH = 1
DEC_BATCH = 8
DEC_SEQ = 1
PAST_LEN = 4096
PAGE_SIZE = 128

MIX_WIDTH = D_MODEL
POOL_WIDTH = D_MODEL // 4
POOL_WINDOWS = (2, 4, 8, 16)
POOL_GROUPS = len(POOL_WINDOWS)
POOL_GROUP_DIM = POOL_WIDTH // POOL_GROUPS
POOL_STATE = max(POOL_WINDOWS) - 1
CONV_WIDTH = D_MODEL // 4
CONV_K = 3
ATT_WIDTH = MIX_WIDTH - POOL_WIDTH - CONV_WIDTH
HEAD_DIM = 128
N_HEADS = ATT_WIDTH // HEAD_DIM
D_FF = ((8 * D_MODEL // 3 + 255) // 256) * 256
FFN_K = 3
QBLOCK = 128
EPS = 1e-6
D_IN = POOL_WIDTH + 3 * CONV_WIDTH + 3 * ATT_WIDTH + N_HEADS

kernel_name = "hybrid_pool_conv_fox_step"

def rms_norm(x, g):
    x32 = x.astype(jnp.float32)
    y = x32 * lax.rsqrt(jnp.mean(x32 * x32, axis=-1, keepdims=True) + EPS)
    return (y * g.astype(jnp.float32)).astype(x.dtype)

def causal_dwconv(z, prev, w):
    t = z.shape[1]
    zz = jnp.concatenate([prev.astype(z.dtype), z], axis=1)
    out = w[0] * zz[:, 0:t]
    for j in range(1, w.shape[0]):
        out = out + w[j] * zz[:, j:j + t]
    return out, zz[:, zz.shape[1] - (w.shape[0] - 1):]

def causal_pool_mix(u, prev, pool_w, pool_scale):
    b, t, _ = u.shape
    p = prev.shape[1]
    zz = jnp.concatenate([prev.astype(u.dtype), u], axis=1)
    cs = jnp.pad(jnp.cumsum(zz.astype(jnp.float32), axis=1), ((0, 0), (1, 0), (0, 0)))
    hi = p + jnp.arange(t) + 1
    means = []
    for g, win in enumerate(POOL_WINDOWS):
        lo = jnp.maximum(hi - win, 0)
        sl = slice(g * POOL_GROUP_DIM, (g + 1) * POOL_GROUP_DIM)
        cnt = (hi - lo).astype(jnp.float32)[None, :, None]
        means.append((cs[:, hi, sl] - cs[:, lo, sl]) / cnt)
    pooled = (jnp.concatenate(means, axis=-1) - u.astype(jnp.float32)).astype(u.dtype)
    y = jnp.einsum('btgc,gcd->btgd', pooled.reshape(b, t, POOL_GROUPS, POOL_GROUP_DIM), pool_w)
    y = y.reshape(b, t, POOL_WIDTH) * pool_scale
    return y, zz[:, zz.shape[1] - POOL_STATE:]

def fox_attend(q, k, v, c_q, c_k, q_pos, k_pos):
    s = jnp.einsum('bqhd,bkhd->bhqk', q, k, preferred_element_type=jnp.float32) * (HEAD_DIM ** -0.5)
    s = s + jnp.transpose(c_q, (0, 2, 1))[:, :, :, None] - jnp.transpose(c_k, (0, 2, 1))[:, :, None, :]
    mask = k_pos[None, :] <= q_pos[:, None]
    s = jnp.where(mask[None, None], s, -jnp.inf)
    p = jax.nn.softmax(s, axis=-1)
    return jnp.einsum('bhqk,bkhd->bqhd', p.astype(v.dtype), v)

def fox_prompt(q, k, v, logf):
    b, s, h, d = q.shape
    c = jnp.cumsum(logf.astype(jnp.float32), axis=1)
    nb = s // QBLOCK
    qb = q.reshape(b, nb, QBLOCK, h, d).transpose(1, 0, 2, 3, 4)
    cb = c.reshape(b, nb, QBLOCK, h).transpose(1, 0, 2, 3)
    starts = jnp.arange(nb) * QBLOCK
    k_pos = jnp.arange(s)

    def block(args):
        qi, ci, st = args
        return fox_attend(qi, k, v, ci, c, st + jnp.arange(QBLOCK), k_pos)

    o = lax.map(block, (qb, cb, starts))
    return o.transpose(1, 0, 2, 3, 4).reshape(b, s, h * d)

def fox_sample(q, k_new, v_new, logf_new, k_past, v_past, logf_past):
    b, t, h, d = q.shape
    p = k_past.shape[1]
    k = jnp.concatenate([k_past.astype(k_new.dtype), k_new], axis=1)
    v = jnp.concatenate([v_past.astype(v_new.dtype), v_new], axis=1)
    logf = jnp.concatenate([logf_past.astype(jnp.float32), logf_new.astype(jnp.float32)], axis=1)
    c = jnp.cumsum(logf, axis=1)
    o = fox_attend(q, k, v, c[:, p:], c, p + jnp.arange(t), jnp.arange(p + t))
    return o.reshape(b, t, h * d)

def hybrid_layer(x, prev_pool, prev_conv, prev_ffn, attn_fn, norm1_g, w_in, b_f, pool_w, pool_scale, conv_w,
                 q_norm_g, k_norm_g, out_norm_g, w_o, norm2_g, w_up, ffn_conv_w, ffn_conv_b, w_down):
    b, t, _ = x.shape
    xn = rms_norm(x, norm1_g)
    proj = xn @ w_in
    o1 = POOL_WIDTH
    o2 = o1 + CONV_WIDTH
    o3 = o2 + CONV_WIDTH
    o4 = o3 + CONV_WIDTH
    o5 = o4 + ATT_WIDTH
    o6 = o5 + ATT_WIDTH
    o7 = o6 + ATT_WIDTH
    u_pool, h_b, h_c, h_x, q, k, v, f_logit = jnp.split(proj, [o1, o2, o3, o4, o5, o6, o7], axis=-1)
    y_pool, pool_state = causal_pool_mix(u_pool, prev_pool, pool_w, pool_scale)
    conv_out, conv_state = causal_dwconv(h_c * h_x, prev_conv, conv_w)
    y_conv = h_b * conv_out
    q = rms_norm(q.reshape(b, t, N_HEADS, HEAD_DIM), q_norm_g)
    k = rms_norm(k.reshape(b, t, N_HEADS, HEAD_DIM), k_norm_g)
    v = v.reshape(b, t, N_HEADS, HEAD_DIM)
    logf = jax.nn.log_sigmoid(f_logit.astype(jnp.float32) + b_f.astype(jnp.float32))
    y_att = attn_fn(q, k, v, logf)
    g_pool, g_conv, g_att = jnp.split(out_norm_g, [POOL_WIDTH, POOL_WIDTH + CONV_WIDTH])
    mix = jnp.concatenate([rms_norm(y_pool, g_pool), rms_norm(y_conv, g_conv), rms_norm(y_att, g_att)], axis=-1)
    x = x + mix @ w_o
    xn2 = rms_norm(x, norm2_g)
    a, gate = jnp.split(xn2 @ w_up, 2, axis=-1)
    a_conv, ffn_state = causal_dwconv(a, prev_ffn, ffn_conv_w)
    x = x + (jax.nn.silu(a_conv + ffn_conv_b) * gate) @ w_down
    return x, pool_state, conv_state, ffn_state, k, v, logf

def setup_inputs(seed: int = 0) -> dict:
    key = jax.random.key(seed)
    ks = jax.random.split(key, 32)
    f32 = jnp.float32
    n_pages = PAST_LEN // PAGE_SIZE
    n_used = DEC_BATCH * n_pages
    n_pool = n_used + max(1, n_used // 4)
    nrm = lambda k, shape: jax.random.normal(k, shape, f32)
    perm = jax.random.permutation(ks[0], n_pool)[:n_used]
    page_table = perm.reshape(DEC_BATCH, n_pages).astype(jnp.int32)
    return {
        "x_prompt": nrm(ks[1], (BATCH, SEQ, D_MODEL)),
        "x_sample": nrm(ks[2], (DEC_BATCH, DEC_SEQ, D_MODEL)),
        "cache_k": nrm(ks[3], (DEPTH, n_pool, PAGE_SIZE, N_HEADS, HEAD_DIM)),
        "cache_v": nrm(ks[4], (DEPTH, n_pool, PAGE_SIZE, N_HEADS, HEAD_DIM)),
        "cache_logf": jax.nn.log_sigmoid(2.5 + nrm(ks[5], (DEPTH, n_pool, PAGE_SIZE, N_HEADS))),
        "state_pool": nrm(ks[6], (DEPTH, DEC_BATCH, POOL_STATE, POOL_WIDTH)),
        "state_conv": nrm(ks[7], (DEPTH, DEC_BATCH, CONV_K - 1, CONV_WIDTH)),
        "state_ffn": nrm(ks[8], (DEPTH, DEC_BATCH, FFN_K - 1, D_FF)),
        "page_table": page_table,
        "norm1_g": 1.0 + 0.05 * nrm(ks[9], (DEPTH, D_MODEL)),
        "w_in": nrm(ks[10], (DEPTH, D_MODEL, D_IN)) * D_MODEL ** -0.5,
        "b_f": jax.random.uniform(ks[11], (DEPTH, N_HEADS), f32, 1.0, 4.0),
        "pool_w": nrm(ks[12], (DEPTH, POOL_GROUPS, POOL_GROUP_DIM, POOL_GROUP_DIM)) * POOL_GROUP_DIM ** -0.5,
        "pool_scale": 1.0 + 0.05 * nrm(ks[13], (DEPTH, POOL_WIDTH)),
        "conv_w": nrm(ks[14], (DEPTH, CONV_K, CONV_WIDTH)) * CONV_K ** -0.5,
        "q_norm_g": 1.0 + 0.05 * nrm(ks[15], (DEPTH, HEAD_DIM)),
        "k_norm_g": 1.0 + 0.05 * nrm(ks[16], (DEPTH, HEAD_DIM)),
        "out_norm_g": 1.0 + 0.05 * nrm(ks[17], (DEPTH, MIX_WIDTH)),
        "w_o": nrm(ks[18], (DEPTH, MIX_WIDTH, D_MODEL)) * MIX_WIDTH ** -0.5,
        "norm2_g": 1.0 + 0.05 * nrm(ks[19], (DEPTH, D_MODEL)),
        "w_up": nrm(ks[20], (DEPTH, D_MODEL, 2 * D_FF)) * D_MODEL ** -0.5,
        "ffn_conv_w": nrm(ks[21], (DEPTH, FFN_K, D_FF)) * FFN_K ** -0.5,
        "ffn_conv_b": 0.02 * nrm(ks[22], (DEPTH, D_FF)),
        "w_down": nrm(ks[23], (DEPTH, D_FF, D_MODEL)) * D_FF ** -0.5,
    }

def reference(x_prompt, x_sample, cache_k, cache_v, cache_logf, state_pool, state_conv, state_ffn, page_table,
              norm1_g, w_in, b_f, pool_w, pool_scale, conv_w, q_norm_g, k_norm_g, out_norm_g, w_o, norm2_g,
              w_up, ffn_conv_w, ffn_conv_b, w_down):
    b, _, _ = x_prompt.shape
    db = x_sample.shape[0]
    past = page_table.shape[1] * PAGE_SIZE
    dt = x_prompt.dtype
    yp, ys = x_prompt, x_sample
    kp_l, vp_l, fp_l, pp_l, cp_l, ffp_l = [], [], [], [], [], []
    ks_l, vs_l, fs_l, ps_l, cs_l, ffs_l = [], [], [], [], [], []
    for l in range(DEPTH):
        w = (norm1_g[l], w_in[l], b_f[l], pool_w[l], pool_scale[l], conv_w[l], q_norm_g[l], k_norm_g[l],
             out_norm_g[l], w_o[l], norm2_g[l], w_up[l], ffn_conv_w[l], ffn_conv_b[l], w_down[l])
        yp, ps, cs, ffs, kk, vv, ff = hybrid_layer(
            yp, jnp.zeros((b, 0, POOL_WIDTH), dt), jnp.zeros((b, CONV_K - 1, CONV_WIDTH), dt),
            jnp.zeros((b, FFN_K - 1, D_FF), dt), fox_prompt, *w)
        kp_l.append(kk); vp_l.append(vv); fp_l.append(ff); pp_l.append(ps); cp_l.append(cs); ffp_l.append(ffs)
        k_past = cache_k[l, page_table].reshape(db, past, N_HEADS, HEAD_DIM)
        v_past = cache_v[l, page_table].reshape(db, past, N_HEADS, HEAD_DIM)
        f_past = cache_logf[l, page_table].reshape(db, past, N_HEADS)
        attn_s = lambda q, k, v, f, kp=k_past, vp=v_past, fpst=f_past: fox_sample(q, k, v, f, kp, vp, fpst)
        ys, ps, cs, ffs, kk, vv, ff = hybrid_layer(ys, state_pool[l], state_conv[l], state_ffn[l], attn_s, *w)
        ks_l.append(kk); vs_l.append(vv); fs_l.append(ff); ps_l.append(ps); cs_l.append(cs); ffs_l.append(ffs)
    return (yp, ys,
            jnp.stack(kp_l), jnp.stack(vp_l), jnp.stack(fp_l), jnp.stack(pp_l), jnp.stack(cp_l), jnp.stack(ffp_l),
            jnp.stack(ks_l), jnp.stack(vs_l), jnp.stack(fs_l), jnp.stack(ps_l), jnp.stack(cs_l), jnp.stack(ffs_l))


_drawn_inputs = setup_inputs


def setup_inputs(seed=0):
    import zlib

    import numpy as np

    out = dict(_drawn_inputs(seed))
    spreads = {}
    factors = {'pool_scale': 2.98, 'ffn_conv_b': 7.335}
    for name, (base, spread) in spreads.items():
        noise = np.random.default_rng([zlib.crc32(name.encode()), seed]).standard_normal(out[name].shape)
        drawn = base * np.exp(spread * noise) if base else spread * noise
        out[name] = __import__('jax').numpy.asarray(drawn.astype(out[name].dtype))
    for name, factor in factors.items():
        out[name] = (out[name] * factor).astype(out[name].dtype)
    return out
```

```python
import concourse.bass as bass
import numpy as np
from concourse import mybir
from contextlib import ExitStack

F32 = mybir.dt.float32
F32R = mybir.dt.float32r
I32 = mybir.dt.int32
ALU = mybir.AluOpType
ACT = mybir.ActivationFunctionType
AX = mybir.AxisListType
P = 128

D_MODEL = 2048
SEQ = 512
DEC = 8
T = SEQ + DEC
HALF = T // 2
HEADS = 8
HD = 128
PAST = 4096
PAGES = PAST // P
POOL_G = 4
POOL_STATE = 15
CONV_T = 4
D_FF = 5632
KT = D_MODEL // P
FT = D_FF // P
FG = 4
GROUPS = FT // FG
EPS = 1e-6
SCALE = HD ** -0.5
MASKED = -1e30

T_U, T_B, T_C, T_X, T_Q, T_K, T_V, T_F = 0, 4, 8, 12, 16, 24, 32, 40
G1, G2, GO, PS, CW, QG, KG, FW, FB = 0, 16, 32, 48, 52, 64, 65, 66, 198
PARAM_ROWS = 66
RAW = 4096
CHUNK = 1024
RING = 4
K_PER_CHUNK = [5, 5, 5, 5, 4, 4, 4, 0]
V_PER_CHUNK = [4, 4, 5, 5, 5, 5, 4, 0]


class Count:

    def __init__(self, sem):
        self.sem, self.base, self.n = sem, 0, 0

    def inc(self, ins):
        ins.then_inc(self.sem, 1)
        self.n += 1
        return ins

    def value(self):
        return self.base + self.n

    def loop(self, i, start, per):
        self.base, self.n = i * per + start, 0

    def after(self, value):
        self.base, self.n = value, 0


def hybrid_layer_kernel(nc, a, o):
    ctx = ExitStack()
    with ctx:
        def sb(name, shape, dt=F32):
            return ctx.enter_context(nc.sbuf_tensor("t_" + name, shape, dt))

        def sem(name):
            return ctx.enter_context(nc.semaphore(name))

        xh = sb("xh", [P, KT, T], F32R)
        xl = sb("xl", [P, KT, T], F32R)
        r1 = sb("r1", [P, KT * T])
        xT = r1[:, :].rearrange("p (k t) -> p k t", k=KT)
        kring = r1[:, 0:RING * 1024].rearrange("p (s n) -> p s n", s=RING)
        vring = r1[:, RING * 1024:2 * RING * 1024].rearrange("p (s n) -> p s n", s=RING)
        wraw = sb("wraw", [P, 2, RAW])
        wh = sb("wh", [P, 4, CHUNK], F32R)
        wl = sb("wl", [P, 4, CHUNK], F32R)
        stg = sb("stg", [P, 2, T])
        ident = sb("ident", [P, P])
        ones = sb("ones", [P, P])
        cmask = sb("cmask", [P, P])
        par = sb("par", [P, 242])
        rc = sb("rc", [P, 16])
        epsc = sb("epsc", [P, 1])
        projS = sb("projS", [P, 40, DEC])
        bf = sb("bf", [HEADS, 1])
        ptr = sb("ptr", [1, DEC * PAGES], I32)
        pti = sb("pti", [P, 2], I32)
        fraw = sb("fraw", [P, KT, HEADS])
        S = sb("S", [P, PAGES, HEADS])
        pr = sb("pr", [P, PAGES, HEADS])
        tri = pr[:, 0:P // HEADS, :].rearrange("p g h -> p (g h)")
        sel = S[0:DEC, :, :].rearrange("p g h -> p (g h)")
        qS = sb("qS", [P, HEADS, DEC])
        sm = sb("sm", [P, HEADS, DEC])
        kSn = sb("kSn", [P, HEADS, DEC])
        maxall = sb("maxall", [P, DEC, HEADS])
        denall = sb("denall", [P, DEC, HEADS])
        ocomb = sb("ocomb", [P, DEC, HEADS])
        mx8 = sb("mx8", [P, HEADS])
        mx1 = sb("mx1", [HEADS, 1])
        mxb = sb("mxb", [P, HEADS])
        diag = sb("diag", [HEADS, HEADS])
        ps8 = sb("ps8", [P, HEADS])
        lfT = sb("lfT", [P, 4, HEADS])
        cqT = sb("cqT", [P, 4, HEADS])
        lfS = sb("lfS", [DEC, HEADS])
        tot = sb("tot", [P, 2, HEADS])
        cqh = sb("cqh", [P, 4])
        rmax = sb("rmax", [P, 4])
        rsum = sb("rsum", [P, 4])
        with nc.sbuf_tensor("t_work", [P, 8192], F32) as work:
            pass
        hh = sb("hh", [P, FG, T], F32R)
        hl = sb("hl", [P, FG, T], F32R)
        xr = work[:, :].rearrange("p (s n) -> p s n", s=4)
        rb = work[:, 7672:8192]
        lf = work[:, 0:2048].rearrange("p (c n) -> p c n", c=2)
        Eb = work[:, 2048:4096].rearrange("p (g h) -> p g h", h=HEADS)
        qmask = work[0:DEC, 0:1024]
        junk = work[:, 4096:5120]
        qrows = work[0:DEC, 5120:6144]
        qcur = work[:, 6144:7168]
        osb = work[0:HEADS, 7168:8192]
        shifts = work[:, 1024:1280].rearrange("p (g h) -> p g h", h=HEADS)
        ps = ctx.enter_context(nc.psum_tensor("ps", [P, 8, 512], F32))

        def acc(t):
            return ps[:, 2 * (t % 2):2 * (t % 2) + 2, 0:HALF]

        def two(ap):
            return ap.rearrange("p (c t) -> p c t", c=2)

        scr = nc.dram_tensor("scr_proj", (40, P, SEQ), F32, kind="Internal").ap()
        scrx = nc.dram_tensor("scr_x", (KT, P, T), F32, kind="Internal").ap()
        scrc = nc.dram_tensor("scr_c", (HEADS, SEQ), F32, kind="Internal").ap()

        def sems(names):
            return [sem(x) for x in names.split()]

        const_ready, prow_loaded, small_loaded, par_full, par_ready = sems(
            "const_ready param_rows_loaded small_loaded params_transposed params_ready")
        xs_loaded, x_full, x_moved_act, x_moved_dve, x_spilled = sems(
            "x_sample_loaded x_transposed x_moved_by_act x_moved_by_dve x_spilled")
        x_loaded = [sem(f"x_block{j}_loaded") for j in range(4)]
        n_sq, n_sum, n_rb, n_tmp, n_hi, n_lo = sems(
            "norm_square_ready norm_square_summed norm_rstd_ready norm_scaled_ready norm_head_ready norm_rest_ready")
        w_loaded = [sem(f"weights_loaded{j}") for j in range(2)]
        w_hi, w_lo, w_used = sems("weight_head_ready weight_rest_ready weight_chunk_used")
        acc_free = [sem(f"accumulators{j}_free") for j in range(2)]
        tile_kept, act_seq, dve_seq = sems("sample_columns_kept act_sequence dve_sequence")
        tile_spilled = [sem(f"tile_spilled{j}") for j in range(2)]
        f_loaded, f_full, f_z, f_nz, f_soft, f_log, f_cum, f_cols, f_kept, f_stored = sems(
            "f_weights_loaded f_full f_z_ready f_negabs_ready f_softplus_ready "
            "logf_ready logf_summed logf_columns_full logf_columns_kept logf_stored")
        e_loaded, e_scan, e_tail, e_tails, e_bias, e_full, e_kept = sems(
            "page_logf_loaded page_logf_summed tails_full tails_ready biases_ready biases_transposed biases_kept")
        q_sq, q_sum, q_rs, q_n, q_tr, q_rows = sems(
            "q_square_ready q_square_summed q_rstd_ready q_normed q_rows_full q_rows_ready")
        k_loaded = [sem(f"k_page_loaded{j}") for j in range(RING)]
        v_loaded = [sem(f"v_page_loaded{j}") for j in range(RING)]
        k_used, v_used = sems("k_page_used v_page_used")
        q_mask, q_bc, q_cur = sems("q_row_masked q_broadcast_full q_current_ready")
        c_se, c_mx, c_mT, c_m1, c_dg, c_mb, c_sub, c_mk, c_p, c_ps, c_den, c_dk = sems(
            "scores_biased page_max_ready page_max_transposed sequence_max_ready sequence_max_diagonal max_broadcast_full "
            "scores_shifted max_kept probs_ready probs_summed den_full den_kept")
        o_rows, o_cols, o_kept = sems("o_rows_ready o_columns_full o_columns_kept")
        s_e, s_x, s_sq, s_sum, s_rs, s_kn, s_pd, s_sc, s_done = sems(
            "own_exponents_ready own_exp_ready k_square_ready k_square_summed k_rstd_ready k_normed qk_product_ready qk_sum_full sample_mixed")
        r_full, r_copied, r_stored = sems("rows_full rows_copied rows_stored")
        p_loaded, p_states, p_tr, p_stT, p_pooled, p_mm, p_y = sems(
            "pool_inputs_loaded mixer_states_loaded states_transposed states_ready pooled_ready pool_mixed pool_y_ready")
        v_in, v_done = sems("conv_inputs_loaded conv_done")
        h_loaded = sems("head_loaded head_decays_loaded")
        h_stored = sems("head_keys_stored head_values_stored")
        h_rowfree, h_ln, h_free, h_sq, h_sum, h_rs, h_qk, h_rowsF, h_rowsC = sems(
            "head_rows_free head_log_ready head_inputs_free head_squares_ready head_squares_summed head_rstd_ready head_qk_normed head_rows_full "
            "head_rows_copied")
        h_cq, h_bias, h_sc, h_mx, h_ri, h_S, h_t, h_e, h_pn, h_pT, h_pC, h_O, h_done = sems(
            "head_decays_ready head_bias_ready head_scores_ready head_max_ready head_sum_inverted head_scores_full head_scores_shifted head_exp_ready head_probs_ready head_probs_transposed "
            "head_probs_copied head_out_full head_out_ready")
        res_loaded, x2_ready = sems("residual_loaded x2_ready")
        g_states, g_tr, g_stT, g_cur, g_kept, g_cv, g_silu, g_h, g_hi, g_lo, g_half, g_y = sems(
            "ffn_states_loaded ffn_states_full ffn_states_ready ffn_columns_ready a_kept conv_ready "
            "silu_ready hidden_ready hidden_head hidden_rest down_tile_full y_added")
        g_t0, g_t1, g_lo_own = sems("tap0_done tap1_done hidden_slot_free")
        z_full, z_ffn, z_act, z_rows = sems("out_full ffn_rows_full ffn_rows_copied out_rows_ready")
        z_stored = [sem(f"out_stored{j}") for j in range(2)]
        states_copied = sem("states_copied")

        w_in_v = a["w_in"].rearrange("l (k p) n -> p (l k) n", p=P)
        w_o_v = a["w_o"].rearrange("l (k p) n -> p (l k) n", p=P)
        w_up_v = a["w_up"].rearrange("l (k p) n -> p (l k) n", p=P)
        w_down_v = a["w_down"].rearrange("l (k p) n -> p (l k) n", p=P)
        k_pages = a["cache_k"].rearrange("l g t h d -> (l g) t (h d)")
        v_pages = a["cache_v"].rearrange("l g t h d -> (l g) t (h d)")
        lf_pages = a["cache_logf"].rearrange("l g t h -> (l g) (t h)")
        N_POOL = k_pages.shape[0]

        R_Q, R_IN, R_O, R_F = 0, 4, 20, 28
        T_IN, T_O, T_FF = 8, 40, 56
        N_CONST = 28
        PRIME = RING

        def step(eng, count, ins):
            count.inc(ins)
            eng.wait_ge(count.sem, count.value())

        lgv = work[0:HEADS, 6144:6144 + T]
        fz = work[0:HEADS, 7168:7168 + T]
        fn = junk[0:HEADS, 0:T]
        Pc = work[:, 2048:4096].rearrange("p (c n) -> p c n", c=2)
        lfE = work[:, 0:2048].rearrange("p (c h t) -> p c h t", c=2, h=HEADS)
        ub = work[:, 0:2112].rearrange("p (g t) -> p g t", g=POOL_G)
        shA, shB = work[:, 2112:2640], work[:, 2640:3168]
        pooled = work[:, 3168:3688]
        strow = work[0:120, 3688:4200]
        cstrow = work[0:16, 4200:4712]
        poolw = work[:, 4712:5224].rearrange("p (g d) -> p g d", g=POOL_G)
        stT = work[:, 5224:5704].rearrange("p (g b) -> p g b", g=POOL_G)
        cstT = work[:, 5704:5768].rearrange("p (g b) -> p g b", g=CONV_T)
        rows1 = work[0:16, 5768:6792]
        rows2 = work[0:16, 6792:7816]
        tmp5 = [work[:, 7816 + 64 * i:7880 + 64 * i] for i in range(5)]
        c3 = work[:, 0:1536].rearrange("p (c t) -> p c t", c=3)
        ct, cz = work[:, 1536:2056], work[:, 2056:2570]
        zs4 = work[:, 2570:2602]
        zl4 = work[:, 2602:2610]
        krs = stg[0:DEC, :, :].rearrange("p a b -> p (a b)")[:, 0:1024]
        vrs = work[0:DEC, 0:1024]
        qkv = work[:, 0:1536].rearrange("p (c t) -> p c t", c=3)
        cb = work[:, 1536:2048]
        qk = work[:, 2048:3072].rearrange("p (c t) -> p c t", c=2)
        sqs = work[:, 3072:4096].rearrange("p (c t) -> p c t", c=2)
        probs2 = sqs
        shifted = work[:, 4096:5120].rearrange("p (c t) -> p c t", c=2)
        pT = work[:, 5120:7168].rearrange("p (k t) -> p k t", k=4)
        krow, vrow = work[:, 7168:7680], work[:, 7680:8192]
        xres = work[:, 0:4 * T].rearrange("p (m t) -> p m t", m=4)
        abuf = work[:, 4160:5204].rearrange("p (s t) -> p s t", s=2)
        cv = work[:, 5204:6244].rearrange("p (s t) -> p s t", s=2)
        fcur = work[:, 6244:6260].rearrange("p (j i) -> p j i", j=4)
        stfT = work[:, 6260:6964].rearrange("p (s f) -> p s f", s=2 * DEC)
        ast = work[:, 6964:7404].rearrange("p (s f) -> p s f", s=DEC + 2)
        stcur = work[:, 7404:7468].rearrange("p (s i) -> p s i", s=2 * DEC)
        strows = work[0:FT, 2080:2080 + 2 * DEC * P].rearrange("p (s n) -> p s n", s=2 * DEC)
        astrows = work[0:FT, 4160:4160 + (DEC + 2) * P].rearrange("p (s n) -> p s n", s=DEC + 2)
        orow = work[:, 0:4096].rearrange("p (s n) -> p s n", s=2)

        def transposed_probs(pe, tr, h, i):
            pe.wait_ge(h_pn, h * 4 + (i + 1))
            if i >= 2:
                pe.wait_ge(h_pC, h * 4 + (i - 1))
            for k in range(i + 1):
                last = tr(ps[:, 6 + i % 2, k * P:(k + 1) * P], probs2[:, i % 2, k * P:(k + 1) * P], P)
            last.then_inc(h_pT, 1)

        def copy_probs(act, copy, h, i):
            act.wait_ge(h_pT, h * 4 + (i + 1))
            copy(pT[:, 0:i + 1, i * P:(i + 1) * P],
                 ps[:, 6 + i % 2, 0:(i + 1) * P].rearrange("p (k t) -> p k t", t=P)).then_inc(h_pC, 1)

        def normalize(dve, h, i):
            dve.wait_ge(h_e, h * 4 + (i + 1))
            dve.reciprocal(rsum[:, i:i + 1], rsum[:, i:i + 1]).then_inc(h_ri, 1)
            dve.wait_ge(h_ri, h * 4 + (i + 1))
            pb = probs2[:, i % 2, 0:(i + 1) * P]
            dve.tensor_scalar(pb, pb, rsum[:, i:i + 1], None, ALU.mult).then_inc(h_pn, 1)

        block = ctx.enter_context(nc.Block())

        @block.gpsimd
        def _(pool):
            cst = Count(const_ready)
            cst.inc(pool.memset(ident[:, :], 0.0))
            cst.inc(pool.memset(ones[:, :], 1.0))
            cst.inc(pool.memset(cmask[:, :], 0.0))
            cst.inc(pool.memset(tri[:, :], 1.0))
            cst.inc(pool.memset(sel[:, :], 1.0))
            for t in range(16):
                cst.inc(pool.memset(rc[:, t:t + 1], 1.0 / (t + 1)))
            cst.inc(pool.memset(epsc[:, :], EPS))
            pool.wait_ge(const_ready, cst.value())
            cst.inc(pool.affine_select(out=ident[:, :], in_=ident[:, :], compare_op=ALU.not_equal, fill=1.0,
                                       base=0, pattern=[[-1, P]], channel_multiplier=1))
            cst.inc(pool.affine_select(out=cmask[:, :], in_=cmask[:, :], compare_op=ALU.is_ge, fill=MASKED,
                                       base=0, pattern=[[-1, P]], channel_multiplier=1))
            cst.inc(pool.affine_select(out=tri[:, :], in_=tri[:, :], compare_op=ALU.is_ge, fill=0.0,
                                       base=0, pattern=[[-1, P]], channel_multiplier=1))
            pool.wait_ge(const_ready, cst.value())
            tv = tri.rearrange("p (a c) -> p a c", c=PAGES)
            cst.inc(pool.affine_select(out=tv, in_=tv, compare_op=ALU.is_ge, fill=0.0, base=PAGES - 1,
                                       pattern=[[PAGES, P // PAGES], [0, PAGES]], channel_multiplier=-1))
            sv = sel.rearrange("p (a c) -> p a c", c=PAGES)
            cst.inc(pool.affine_select(out=sv, in_=sv, compare_op=ALU.is_equal, fill=0.0, base=0,
                                       pattern=[[-1, DEC], [0, PAGES]], channel_multiplier=1))
            assert cst.value() <= N_CONST, cst.value()
            cst.inc(pool.memset(mx8[:, :], 0.0))
            pool.wait_ge(x_moved_act, 9)
            pool.wait_ge(x_moved_dve, 8)
            pool.dma_start(scrx.rearrange("k p t -> p k t"), xT).then_inc(x_spilled, 16)
            pool.wait_ge(small_loaded, 48)
            pool.wait_ge(n_lo, KT)
            for c in range(2):
                pool.indirect_dma_start(lf[:, c, :], None, lf_pages,
                                        bass.IndirectOffsetOnAxis(ap=pti[:, c:c + 1], axis=0)).then_inc(e_loaded, 16)
            pool.dma_start(o["pool_sample"][0, :, 0:POOL_STATE - 1, :],
                           a["state_pool"][0, :, 1:POOL_STATE, :]).then_inc(states_copied, 16)
            pool.dma_start(o["conv_sample"][0, :, 0:1, :], a["state_conv"][0, :, 1:2, :]).then_inc(states_copied, 16)
            pool.dma_start(o["ffn_sample"][0, :, 0:1, :], a["state_ffn"][0, :, 1:2, :]).then_inc(states_copied, 16)
            pool.wait_ge(f_cum, 1)
            pool.dma_start(scrc, junk[0:HEADS, 0:SEQ]).then_inc(f_stored, 16)
            pool.wait_ge(f_kept, 3)
            pool.dma_start(o["logf_prompt"][0, 0].rearrange("(j p) h -> p j h", p=P), lfT[:, :, :]).then_inc(f_stored, 16)
            pool.dma_start(o["logf_sample"][0, :, 0, :], lfS[:, :]).then_inc(f_stored, 16)

            pool.wait_ge(r_copied, 1)
            pool.dma_start(o["k_sample"][0, :, 0].rearrange("b h d -> b (h d)"), krs).then_inc(r_stored, 16)
            pool.wait_ge(r_copied, 2)
            pool.dma_start(o["v_sample"][0, :, 0].rearrange("b h d -> b (h d)"), vrs).then_inc(r_stored, 16)
            pool.wait_ge(r_copied, 3)
            pool.dma_start(o["pool_prompt"][0, 0], rows1[0:POOL_STATE, 0:512]).then_inc(r_stored, 16)
            pool.wait_ge(r_copied, 4)
            pool.dma_start(o["pool_sample"][0, :, POOL_STATE - 1, :], rows1[0:DEC, 512:1024]).then_inc(r_stored, 16)
            pool.wait_ge(r_copied, 5)
            pool.dma_start(o["conv_prompt"][0, 0], rows2[0:2, 0:512]).then_inc(r_stored, 16)
            pool.wait_ge(r_copied, 6)
            pool.dma_start(o["conv_sample"][0, :, 1, :], rows2[0:DEC, 512:1024]).then_inc(r_stored, 16)

            pool.wait_ge(z_act, 3)
            for b in range(DEC):
                pool.dma_start(o["ffn_sample"][0, b, 1, :].rearrange("(t n) -> t n", n=P),
                               astrows[:, b, :]).then_inc(states_copied, 16)
            for j in range(2):
                pool.dma_start(o["ffn_prompt"][0, 0, j, :].rearrange("(t n) -> t n", n=P),
                               astrows[:, DEC + j, :]).then_inc(states_copied, 16)
            pool.wait_ge(states_copied, 16 * 13)
            pool.wait_ge(f_stored, 48)
            pool.wait_ge(r_stored, 96)

        @block.sync
        def _(sp):
            sp.dma_start(xr[0:DEC, 3, :], a["x_sample"].rearrange("b t d -> (b t) d")).then_inc(xs_loaded, 16)
            xp = a["x_prompt"].rearrange("b (j p) d -> (b j) p d", p=P)
            for j in range(3):
                sp.dma_start(xr[:, j, :], xp[j]).then_inc(x_loaded[j], 16)
            pv = stg[:, :, :].rearrange("p a b -> p (a b)")

            def rows(lo, n, ap):
                at, row = (0, lo) if lo < P else (lo // P, lo % P)
                sp.dma_start(pv[row:row + n, at * P:(at + 1) * P], ap).then_inc(prow_loaded, 16)

            rows(G1, 16, a["norm1_g"][0].rearrange("(k p) -> k p", p=P))
            rows(G2, 16, a["norm2_g"][0].rearrange("(k p) -> k p", p=P))
            rows(GO, 16, a["out_norm_g"][0].rearrange("(k p) -> k p", p=P))
            rows(PS, 4, a["pool_scale"][0].rearrange("(k p) -> k p", p=P))
            for j in range(3):
                rows(CW + 4 * j, 4, a["conv_w"][0, j].rearrange("(k p) -> k p", p=P))
            rows(QG, 1, a["q_norm_g"])
            rows(KG, 1, a["k_norm_g"])
            for j in range(2):
                rows(P + j * FT, FT, a["ffn_conv_w"][0, j].rearrange("(k p) -> k p", p=P))
            rows(2 * P, FT, a["ffn_conv_w"][0, 2].rearrange("(k p) -> k p", p=P))
            rows(2 * P + FT, FT, a["ffn_conv_b"][0].rearrange("(k p) -> k p", p=P))
            sp.dma_start(bf[:, :], a["b_f"].rearrange("l h -> h l"),
                         allow_slow_non_contiguous=True).then_inc(small_loaded, 16)
            sp.dma_start(ptr[:, :], a["page_table"].rearrange("(o b) g -> o (b g)", o=1)).then_inc(small_loaded, 16)
            sp.dma_start(pti[:, :], a["page_table"].rearrange("(c b) g -> (b g) c", c=2),
                         allow_slow_non_contiguous=True).then_inc(small_loaded, 16)
            sp.wait_ge(x_full, 1)
            sp.dma_start(xr[:, 3, :], xp[3]).then_inc(x_loaded[3], 16)
            sp.dma_start(fraw[:, :, :], w_in_v[:, :, T_F * P:T_F * P + HEADS]).then_inc(f_loaded, 16)

            def load_raw(n, slot, source, col, k=KT, width=2 * P):
                sp.wait_ge(w_lo, n * 4 - 4)
                sp.dma_start(wraw[:, slot, :].rearrange("p (k n) -> p k n", k=k),
                             source[:, :, bass.ds(col, width)]).then_inc(w_loaded[slot], 16)

            for n in range(2):
                sp.dma_start(wraw[:, n, :].rearrange("p (k n) -> p k n", k=KT),
                             w_in_v[:, :, (T_Q + 2 * n) * P:(T_Q + 2 * n + 2) * P]).then_inc(w_loaded[n], 16)
            for n in range(2, 4):
                load_raw(n, n % 2, w_in_v, (T_Q + 2 * n) * P)
            for n in range(4, 6):
                load_raw(n, n % 2, w_in_v, 2 * (n - R_IN) * P)

            def page(ring, pages, loads, used, r, p):
                g = sp.value_load(ptr[0:1, bass.ds(r * PAGES + p, 1)], min_val=0, max_val=N_POOL - 1)
                sp.wait_ge(used, r * PAGES + (p + 1))
                sp.dma_start(ring[:, p % RING, :],
                             pages[bass.ds(g, 1), :, :].rearrange("a p n -> (a p) n")).then_inc(loads[p % RING], 16)

            sp.wait_ge(small_loaded, 48)
            sp.wait_ge(n_lo, KT)
            sp.wait_ge(x_spilled, 16)

            def round_loads(r, weights, keys, values):
                kp, vp = 0, 0
                for c in range(8):
                    if weights and c % 4 == 1:
                        weights(c // 4)
                    for n in range(max(K_PER_CHUNK[c], V_PER_CHUNK[c])):
                        if keys and n < K_PER_CHUNK[c]:
                            page(kring, k_pages, k_loaded, k_used, r, kp)
                            kp += 1
                        if values and n < V_PER_CHUNK[c]:
                            page(vring, v_pages, v_loaded, v_used, r - 1, vp)
                            vp += 1

            def next_in(r):
                def load(m):
                    s = r + 1
                    load_raw(r * 2 + (R_IN + 2 + m), m, w_in_v, s * (4 * P) + (s // 4) * (8 * P) + 2 * m * P)
                return load

            def first_o(m):
                load_raw(R_O + m, m, w_o_v, 2 * m * P)

            round_loads(0, next_in(0), True, False)
            with sp.Fori(1, DEC - 1) as r:
                round_loads(r, next_in(r), True, True)
            round_loads(DEC - 1, first_o, True, True)
            round_loads(DEC, None, False, True)

            sp.wait_ge(s_done, 1)
            sp.wait_ge(r_stored, 32)
            sp.dma_start(ub[:, :, 16:528], scr[T_U:T_U + 4].rearrange("g p t -> p g t")).then_inc(p_loaded, 16)
            sp.dma_start(strow[:, :], a["state_pool"].rearrange("l b t c -> (l b t) c")).then_inc(p_states, 16)
            sp.dma_start(cstrow[:, :], a["state_conv"].rearrange("l b t c -> (l b t) c")).then_inc(p_states, 16)
            sp.dma_start(poolw, a["pool_w"].rearrange("l g c d -> c (l g) d")).then_inc(p_states, 16)
            sp.wait_ge(p_y, 2 * POOL_G)
            sp.wait_ge(r_full, 4)
            for j in range(CONV_T):
                if j:
                    sp.wait_ge(v_done, j)
                src = scr[T_B:T_B + 12].rearrange("(c g) p t -> g p c t", c=3)
                sp.dma_start(c3, src[j]).then_inc(v_in, 16)
            sp.wait_ge(v_done, CONV_T)
            sp.wait_ge(r_stored, 96)
            src = scr[T_Q:T_Q + 24].rearrange("(c h) p t -> h p c t", c=3)
            sp.sem_inc(h_rowfree, 1)
            with sp.Fori(0, HEADS) as h:
                sp.wait_ge(h_free, h + 1)
                sp.dma_start(qkv, src[bass.ds(h, 1)].rearrange("a p c t -> (a p) c t")).then_inc(h_loaded[0], 16)
                sp.dma_start(cb, scrc[bass.ds(h, 1), :].broadcast_to([P, SEQ])).then_inc(h_loaded[1], 16)
                for n, (name, row) in enumerate((("k_prompt", krow), ("v_prompt", vrow))):
                    sp.wait_ge(h_rowsC, h * 2 + (n + 1))
                    dst = o[name].rearrange("l b (j p) h d -> p (l b j) h d", p=P)
                    sp.dma_start(dst[:, :, bass.ds(h, 1), :].rearrange("p j a d -> p (j a) d"),
                                 row.rearrange("p (j d) -> p j d", j=4)).then_inc(h_stored[n], 16)
                for n in range(2):
                    sp.wait_ge(h_stored[n], h * 16 + 16)
                sp.sem_inc(h_rowfree, 1)
            for n in range(2):
                sp.wait_ge(h_stored[n], 16 * HEADS)
            sp.wait_ge(h_done, HEADS)
            sp.wait_ge(h_free, HEADS + 1)
            sp.dma_start(strows, a["state_ffn"].rearrange("l b j (t n) -> t (l b j) n", n=P)).then_inc(g_states, 16)

            def o_body(i, weights):
                sp.wait_ge(x2_ready, i * 4 + 1)
                sp.dma_start(xres, scrx.rearrange("(i m) p t -> i p m t", m=4)[bass.ds(i, 1)]
                             .rearrange("a p m t -> (a p) m t")).then_inc(res_loaded, 16)
                for m in range(2):
                    weights(i, m)

            with sp.Fori(0, 3) as i:
                o_body(i, lambda i, m: load_raw(i * 2 + (R_O + 2 + m), m, w_o_v, i * (4 * P) + (2 + m) * 2 * P))
            o_body(3, lambda i, m: load_raw(R_F + m, m, w_up_v, m * D_FF))
            def down(i, n, m):
                sp.wait_ge(w_lo, n * 4 - 4)
                rows_ = w_down_v[:, bass.ds(i * FG, FG), 1024 * m:1024 * (m + 1)]
                sp.dma_start(wraw[:, m, :].rearrange("p (k n) -> p k n", k=FG), rows_).then_inc(w_loaded[m], 16)

            def ffn_body(i, more):
                n = i * 6 + R_F
                load_raw(n + 2, 0, w_up_v, i * (FG * P) + 2 * P)
                load_raw(n + 3, 1, w_up_v, i * (FG * P) + (D_FF + 2 * P))
                down(i, n + 4, 0)
                down(i, n + 5, 1)
                if more:
                    load_raw(n + 6, 0, w_up_v, i * (FG * P) + FG * P)
                    load_raw(n + 7, 1, w_up_v, i * (FG * P) + (FG * P + D_FF))

            with sp.Fori(0, GROUPS - 1) as i:
                ffn_body(i, True)
            ffn_body(GROUPS - 1, False)
            yp = o["y_prompt"].rearrange("b (j p) d -> (b j) p d", p=P)
            for j in range(4):
                sp.wait_ge(z_rows, 4 * (j + 1))
                sp.dma_start(yp[j], orow[:, j % 2, :]).then_inc(z_stored[j % 2], 16)
            sp.wait_ge(z_rows, 20)
            sp.dma_start(o["y_sample"].rearrange("b t d -> (b t) d"), orow[0:DEC, 0, :]).then_inc(z_stored[0], 16)
            sp.wait_ge(z_stored[0], 48)
            sp.wait_ge(z_stored[1], 32)

        norm_groups = [(0, KT, G1, D_MODEL), (0, 4, GO, 512), (4, 8, GO + 4, 512), (8, 16, GO + 8, 1024),
                       (0, KT, G2, D_MODEL)]
        norm_first = [0, 16, 20, 24, 32]

        @block.tensor
        def _(pe):
            def mm(out, lhsT, rhs, start=True, stop=True):
                return pe.matmul(out, lhsT, rhs, start=start, stop=stop)

            def tr(out, in_, n):
                return pe.transpose(out, in_, ident[0:n, 0:n])

            pe.sem_inc(w_used, 4)
            pe.sem_inc(v_used, PRIME)
            pe.wait_ge(const_ready, N_CONST)
            pe.wait_ge(prow_loaded, 13 * 16)
            pv = stg[:, :, :].rearrange("p a b -> p (a b)")
            tr(ps[:, 7, 0:66], pv[0:66, 0:P], 66)
            tr(ps[:, 7, 66:154], pv[0:88, P:2 * P], 88)
            tr(ps[:, 7, 154:242], pv[0:88, 2 * P:3 * P], 88).then_inc(par_full, 1)
            pe.wait_ge(xs_loaded, 16)
            for k in range(KT):
                last = tr(ps[:, 6, k * DEC:(k + 1) * DEC], xr[0:DEC, 3, k * P:(k + 1) * P], DEC)
            last.then_inc(x_full, 1)
            for i in range(16):
                j, g = divmod(i, 4)
                if g == 0:
                    pe.wait_ge(x_loaded[j], 16)
                if i >= 4:
                    pe.wait_ge(*((x_moved_act, 1 + (i - 4) // 2 + 1) if i % 2 == 0 else (x_moved_dve, (i - 4) // 2 + 1)))
                for k in range(4):
                    last = tr(ps[:, i % 4, k * P:(k + 1) * P], xr[:, j, (4 * g + k) * P:(4 * g + k + 1) * P], P)
                last.then_inc(x_full, 1)

            def norm(group):
                lo, hi, _, _ = norm_groups[group]
                if group:
                    pe.wait_ge(n_rb, group)
                for t in range(lo, hi):
                    n = norm_first[group] + t - lo
                    pe.wait_ge(n_sq, n + 1)
                    for c in range(2):
                        last = mm(ps[:, 4 + c, 0:HALF], ones[:, :], stg[:, n % 2, c * HALF:(c + 1) * HALF],
                                  t == lo, t == hi - 1)
                    last.then_inc(n_sum, 1)

            norm(0)

            pe.wait_ge(n_lo, KT)
            pe.wait_ge(f_loaded, 16)
            for k in range(KT):
                for x in (xh, xl):
                    for c in range(2):
                        last = mm(ps[0:HEADS, 4 + c, 0:HALF], fraw[:, k, :],
                                  x[:, k, c * HALF:(c + 1) * HALF].bitcast(F32),
                                  k == 0 and x is xh, k == KT - 1 and x is xl)
            last.then_inc(f_full, 1)

            def chunk(g, c, t, u, half):
                if half == 0:
                    pe.wait_ge(acc_free[u % 2], t)
                pe.wait_ge(w_lo, g + (c + 1))
                s = c % 4
                for k in range(8):
                    kt = 8 * half + k
                    block_h = wh[:, s, k * P:(k + 1) * P]
                    block_l = wl[:, s, k * P:(k + 1) * P]
                    for w, x in ((block_h, xh), (block_h, xl), (block_l, xh)):
                        for b in range(2):
                            last = mm(ps[:, 2 * (u % 2) + b, 0:HALF], w, x[:, kt, b * HALF:(b + 1) * HALF],
                                      kt == 0 and w is block_h and x is xh, kt == KT - 1 and w is block_l)
                last.then_inc(w_used, 1)

            def tile(g, t0, u):
                for half in range(2):
                    chunk(g, 2 * u + half, t0 // 2 + (u // 2 + 1), u, half)

            for u in range(4):
                tile(0, 0, u)
            pe.wait_ge(f_cum, 1)
            for j in range(4):
                tr(ps[:, 4, j * HEADS:(j + 1) * HEADS], lgv[:, j * P:(j + 1) * P], HEADS)
                tr(ps[:, 4, 32 + j * HEADS:32 + (j + 1) * HEADS], junk[0:HEADS, j * P:(j + 1) * P], HEADS)
            tr(ps[0:DEC, 4, 64:72], lgv[:, SEQ:T], HEADS).then_inc(f_cols, 1)
            pe.wait_ge(f_kept, 3)
            pe.wait_ge(e_scan, 1)
            for c in range(2):
                mm(ps[:, 5, c * HEADS:(c + 1) * HEADS], tri[:, :], Pc[:, c, 1024 - HEADS:1024], True, False)
                last = mm(ps[:, 5, c * HEADS:(c + 1) * HEADS], sel[:, c * P:(c + 1) * P], lfS[:, :], False, True)
            last.then_inc(e_tail, 1)
            pe.wait_ge(e_bias, 1)
            for i in range(4):
                if i >= 2:
                    pe.wait_ge(e_kept, i - 1)
                for n in range(4):
                    c, h = divmod(4 * i + n, HEADS)
                    last = tr(ps[:, 4 + i % 2, n * P:(n + 1) * P], lfE[:, c, h, :], P)
                last.then_inc(e_full, 1)
            for u in range(4):
                tile(8, 4, u)
            pe.wait_ge(q_sq, 1)
            mm(ps[:, 6, 0:64], ones[:, :], sm[:, :, :].rearrange("p h b -> p (h b)")).then_inc(q_sum, 1)
            pe.wait_ge(q_n, 1)
            for h in range(HEADS):
                last = tr(ps[0:DEC, 6 + h // 4, (h % 4) * P:(h % 4 + 1) * P], qS[:, h, :], P)
            last.then_inc(q_tr, 1)

            def broadcast_q(s, half):
                if half == 0:
                    pe.wait_ge(q_mask, s + 1)
                if half or not (isinstance(s, int) and s == 0):
                    pe.wait_ge(q_cur, 2 * s + half)
                mm(ps[:, 6, :], ones[0:DEC, :], qmask[:, half * 512:(half + 1) * 512]).then_inc(q_bc, 1)

            def value_page(r, p):
                pe.wait_ge(v_loaded[p % RING], r * (16 * PAGES // RING) + 16 * (p // RING + 1))
                for c in range(2):
                    last = mm(ps[0:HEADS, 4 + c, :], pr[:, p, :], vring[:, p % RING, c * 512:(c + 1) * 512],
                              p == 0, p == PAGES - 1)
                last.then_inc(v_used, 1)

            def round_(r, keys, more, values):
                p = 0
                for c in range(8):
                    if c == 7:
                        if more:
                            broadcast_q(r + 1, 0)
                        if keys:
                            pe.wait_ge(c_mx, r + 1)
                            if values:
                                pe.wait_ge(c_dk, r)
                            tr(ps[0:HEADS, 7, 0:P], mx8[:, :], P).then_inc(c_mT, 1)
                    if keys:
                        u, half = divmod(c, 2)
                        chunk(r * 8 + 4 * R_IN, c, r * 2 + (T_IN // 2 + u // 2 + 1), u, half)
                    if values and c == 0:
                        pe.wait_ge(c_p, r)
                        pe.wait_ge(o_rows, r)
                    if values and c == 1:
                        pe.wait_ge(c_ps, r)
                        pe.wait_ge(o_kept, r)
                        mm(ps[:, 7, 136:144], ones[:, :], ps8[:, :]).then_inc(c_den, 1)
                    for _ in range(V_PER_CHUNK[c] if values else 0):
                        value_page(r - 1, p)
                        p += 1
                if more:
                    broadcast_q(r + 1, 1)
                if keys:
                    pe.wait_ge(c_dg, r + 1)
                if values:
                    pe.wait_ge(o_rows, r + 1)
                    pe.wait_ge(c_dk, r)
                    for h in range(HEADS):
                        last = mm(ps[:, 7, 144 + h:145 + h], osb[:, h * P:(h + 1) * P], ident[0:HEADS, h:h + 1])
                    last.then_inc(o_cols, 1)
                if keys:
                    mm(ps[:, 7, P:P + HEADS], ones[0:HEADS, :], diag[:, :]).then_inc(c_mb, 1)

            broadcast_q(0, 0)
            broadcast_q(0, 1)
            round_(0, True, True, False)
            with pe.Fori(1, DEC - 1) as r:
                round_(r, True, True, True)
            round_(DEC - 1, True, False, True)
            round_(DEC, False, False, True)

            pe.wait_ge(o_kept, DEC + 1)
            for b in range(2):
                pe.wait_ge(acc_free[b], T_O // 2 + 1)
            pe.wait_ge(s_sq, 1)
            mm(ps[:, 6, 0:64], ones[:, :], sm[:, :, :].rearrange("p h b -> p (h b)")).then_inc(s_sum, 1)
            pe.wait_ge(s_pd, 1)
            mm(ps[:, 6, 64:128], ones[:, :], tmp5[0]).then_inc(s_sc, 1)
            for h in range(HEADS):
                last = tr(ps[0:DEC, 2 + h // 4, (h % 4) * P:(h % 4 + 1) * P], kSn[:, h, :], P)
            last.then_inc(r_full, 1)
            for h in range(HEADS):
                last = tr(ps[0:DEC, 4 + h // 4, (h % 4) * P:(h % 4 + 1) * P], projS[:, T_V + h, :], P)
            last.then_inc(r_full, 1)

            pe.wait_ge(p_states, 48)
            for g in range(POOL_G):
                tr(ps[:, 0, g * 120:(g + 1) * 120], strow[:, g * P:(g + 1) * P], 120)
                last = tr(ps[:, 1, g * 16:(g + 1) * 16], cstrow[:, g * P:(g + 1) * P], 16)
            last.then_inc(p_tr, 1)
            pe.wait_ge(r_copied, 2)
            for g in range(POOL_G):
                pe.wait_ge(p_pooled, g + 1)
                if g >= 2:
                    pe.wait_ge(p_y, 2 * (g - 1))
                b = 2 + 2 * (g % 2)
                mm(ps[:, b, :], poolw[:, g, :], pooled[:, 0:SEQ])
                mm(ps[:, b + 1, 0:DEC], poolw[:, g, :], pooled[:, SEQ:T]).then_inc(p_mm, 1)
            pe.wait_ge(s_done, 1)
            for g in range(POOL_G):
                last = tr(ps[0:POOL_STATE, 6, g * P:(g + 1) * P], ub[:, g, 528 - POOL_STATE:528], P)
            last.then_inc(r_full, 1)
            for g in range(POOL_G):
                last = tr(ps[0:DEC, 7, g * P:(g + 1) * P], projS[:, T_U + g, :], P)
            last.then_inc(r_full, 1)
            pe.wait_ge(v_done, CONV_T)
            pe.wait_ge(p_stT, 1)
            for j in range(CONV_T):
                last = tr(ps[0:2, 0, j * P:(j + 1) * P], zl4[:, 2 * j:2 * j + 2], P)
            last.then_inc(r_full, 1)
            for j in range(CONV_T):
                last = tr(ps[0:DEC, 1, j * P:(j + 1) * P], zs4[:, DEC * j:DEC * (j + 1)], P)
            last.then_inc(r_full, 1)
            pe.wait_ge(r_copied, 6)

            with pe.Fori(0, HEADS) as h:
                pe.wait_ge(h_sq, h + 1)
                for c in range(2):
                    last = mm(ps[:, c, :], ones[:, :], sqs[:, c, :])
                last.then_inc(h_sum, 1)
                pe.wait_ge(h_qk, h + 1)
                for j in range(4):
                    last = tr(ps[:, 2, j * P:(j + 1) * P], qk[:, 1, j * P:(j + 1) * P], P)
                last.then_inc(h_rowsF, 1)
                for j in range(4):
                    last = tr(ps[:, 3, j * P:(j + 1) * P], qkv[:, 2, j * P:(j + 1) * P], P)
                last.then_inc(h_rowsF, 1)
                for i in range(4):
                    n = (i + 1) * P
                    if i >= 2:
                        pe.wait_ge(h_t, h * 4 + (i - 1))
                    mm(ps[:, 4 + i % 2, 0:n], qk[:, 0, i * P:(i + 1) * P], qk[:, 1, 0:n]).then_inc(h_S, 1)
                    if i >= 1:
                        transposed_probs(pe, tr, h, i - 1)
                transposed_probs(pe, tr, h, 3)
                pe.wait_ge(h_pC, h * 4 + 4)
                pe.wait_ge(h_rowsC, h * 2 + 2)
                for k in range(4):
                    last = mm(ps[:, 0, k * P:SEQ], vrow[:, k * P:(k + 1) * P], pT[:, k, k * P:SEQ], k == 0, k == 3)
                last.then_inc(h_O, 1)
                pe.wait_ge(h_done, h + 1)

            for group in (1, 2, 3):
                norm(group)
            pe.wait_ge(n_lo, 32)
            with pe.Fori(0, 4) as i:
                for u in range(4):
                    for half in range(2):
                        chunk(i * 8 + 4 * R_O, 2 * u + half, i * 2 + (T_O // 2 + u // 2 + 1), u, half)
            pe.wait_ge(g_states, 16)
            pe.wait_ge(n_rb, 4)
            for s in range(2 * DEC):
                last = tr(ps[:, 6 + s // 11, (s % 11) * FT:(s % 11 + 1) * FT], strows[:, s, :], FT)
            last.then_inc(g_tr, 1)
            norm(4)
            pe.wait_ge(n_lo, 48)

            def ffn(i, t):
                g = i * 24 + 4 * R_F
                for u in range(8):
                    for half in range(2):
                        chunk(g, 2 * u + half, i * 12 + (T_FF // 2 + u // 2 + 1), u, half)
                for c in range(8):
                    pe.wait_ge(w_lo, g + (16 + c + 1))
                    if c == 0:
                        pe.wait_ge(g_lo, i * 4 + 4)
                    for m in range(2):
                        pe.wait_ge(acc_free[m], i * 12 + (T_FF // 2 + 4 + c + 1))
                        for k in range(FG):
                            at = k * 256 + m * P
                            block_h = wh[:, c % 4, at:at + P]
                            block_l = wl[:, c % 4, at:at + P]
                            for w, x in ((block_h, hh), (block_h, hl), (block_l, hh)):
                                for b in range(2):
                                    last = mm(ps[:, 2 * m + b, 0:HALF], w, x[:, k, b * HALF:(b + 1) * HALF],
                                              k == 0 and w is block_h and x is hh, k == FG - 1 and w is block_l)
                        last.then_inc(g_half if m == 0 else w_used, 1)

            with pe.Fori(0, GROUPS) as i:
                ffn(i, 0)

            pe.wait_ge(g_kept, FT)
            for s in range(DEC + 2):
                last = tr(ps[0:FT, 4 + s // 4, (s % 4) * P:(s % 4 + 1) * P], ast[:, s, :], P)
            last.then_inc(z_ffn, 1)
            pe.wait_ge(g_y, GROUPS)
            for i in range(20):
                j, q = divmod(i, 4)
                if i >= 4:
                    pe.wait_ge(z_rows, i - 3)
                n = P if j < 4 else DEC
                for k in range(4):
                    last = tr(ps[0:n, i % 4, k * P:(k + 1) * P], xT[:, 4 * q + k, j * P:j * P + n], P)
                last.then_inc(z_full, 1)


        @block.scalar
        def _(act):
            seq = Count(act_seq)

            def copy(out, in_):
                return act.activation(out, in_, ACT.Copy)

            for b in range(2):
                act.sem_inc(acc_free[b], 1)
            act.sem_inc(o_rows, 1)
            act.sem_inc(g_hi, 2)
            act.wait_ge(par_full, 1)
            copy(par[:, :], ps[:, 7, 0:242]).then_inc(par_ready, 1)
            act.wait_ge(x_full, 1)
            copy(xT[:, :, SEQ:T], ps[:, 6, 0:KT * DEC].rearrange("p (k b) -> p k b", k=KT)).then_inc(x_moved_act, 1)
            for i in range(0, 16, 2):
                j, g = divmod(i, 4)
                act.wait_ge(x_full, i + 2)
                copy(xT[:, 4 * g:4 * g + 4, j * P:(j + 1) * P],
                     ps[:, i % 4, :].rearrange("p (k t) -> p k t", k=4)).then_inc(x_moved_act, 1)

            def norm(group):
                lo, hi, _, width = norm_groups[group]
                n0 = norm_first[group]
                for t in range(lo, hi):
                    n = n0 + t - lo
                    if t - lo >= 2:
                        act.wait_ge(n_sum, n - 1)
                    elif group:
                        act.wait_ge(n_lo, n0)
                    if group == 4:
                        act.wait_ge(x2_ready, t + 2)
                    act.activation(stg[:, n % 2, :], xT[:, t, :], ACT.Square).then_inc(n_sq, 1)
                act.wait_ge(n_sum, n0 + hi - lo)
                step(act, seq, act.activation(two(rb), ps[:, 4:6, 0:HALF], ACT.Ln, bias=epsc[:, :], scale=1.0 / width))
                act.activation(rb, rb, ACT.Exp, scale=-0.5).then_inc(n_rb, 1)
                for t in range(lo, hi):
                    n = n0 + t - lo
                    act.wait_ge(n_tmp, n + 1)
                    copy(xh[:, t, :], stg[:, n % 2, :]).then_inc(n_hi, 1)

            act.wait_ge(x_moved_dve, 8)
            act.wait_ge(x_moved_act, 9)
            norm(0)

            def raw_chunk(c, down):
                raw, q = wraw[:, (c // 4) % 2, :], c % 4
                if down:
                    return raw.rearrange("p (k n) -> p k n", k=FG)[:, :, q * 256:(q + 1) * 256]
                m, half = divmod(q, 2)
                return raw.rearrange("p (k n) -> p k n", k=KT)[:, half * 8:half * 8 + 8, m * P:(m + 1) * P]

            def blocks(buf, c, down):
                return buf[:, c % 4, :].rearrange("p (k n) -> p k n", k=FG if down else 8)

            def head(g, c, down=False):
                if c % 4 == 0:
                    act.wait_ge(w_loaded[(c // 4) % 2], g * 2 + 16 * (c // 8 + 1))
                act.wait_ge(w_used, g + (c + 1))
                copy(blocks(wh, c, down), raw_chunk(c, down)).then_inc(w_hi, 1)

            for c in range(4):
                head(0, c)

            def move_tile(t, u, dst, used):
                s = u % 2
                act.wait_ge(w_used, used)
                if not (isinstance(t, int) and t + u < 2):
                    act.wait_ge(tile_spilled[s], t * 8 + 16 * (u // 2))
                    act.wait_ge(tile_kept, t + (u - 1))
                act.activation(two(stg[:, s, :]), ps[:, 2 * s:2 * s + 2, 0:HALF], ACT.Copy).then_inc(acc_free[s], 1)
                act.wait_ge(acc_free[s], t // 2 + (u // 2 + 2))
                copy(projS[:, bass.ds(dst, 1), :], stg[:, s:s + 1, SEQ:T]).then_inc(tile_kept, 1)
                act.dma_start(scr[bass.ds(dst, 1)].rearrange("a p t -> (a p) t"), stg[:, s, 0:SEQ]).then_inc(tile_spilled[s], 16)

            act.wait_ge(f_nz, 1)
            step(act, seq, act.activation(fn, fn, ACT.Exp))
            act.activation(fn, fn, ACT.Ln, bias=1.0).then_inc(f_soft, 1)
            for i in range(2):
                for u in range(4):
                    for c in (2 * u, 2 * u + 1):
                        head(8 * i, 4 + c)
                    move_tile(4 * i, u, T_Q + 4 * i + u, 4 + 8 * i + 2 * u + 2)
                if i == 0:
                    act.wait_ge(f_cols, 1)
                    copy(lfT[:, :, :], ps[:, 4, 0:32].rearrange("p (j h) -> p j h", j=4)).then_inc(f_kept, 1)
                    copy(cqT[:, :, :], ps[:, 4, 32:64].rearrange("p (j h) -> p j h", j=4)).then_inc(f_kept, 1)
                    copy(lfS[:, :], ps[0:DEC, 4, 64:72]).then_inc(f_kept, 1)
                    for n in range(4):
                        act.wait_ge(e_full, n + 1)
                        c, h = divmod(4 * n, HEADS)
                        copy(Eb[:, c * P:(c + 1) * P, h:h + 4].rearrange("p g h -> p h g"),
                             ps[:, 4 + n % 2, :].rearrange("p (h g) -> p h g", h=4)).then_inc(e_kept, 1)

            def rstd64(summed, done):
                act.wait_ge(summed, 1)
                v = sm[:, :, :].rearrange("p h b -> p (h b)")
                step(act, seq, act.activation(v, ps[:, 6, 0:64], ACT.Ln, bias=epsc[:, :], scale=1.0 / HD))
                act.activation(v, v, ACT.Exp, scale=-0.5).then_inc(done, 1)

            rstd64(q_sum, q_rs)
            act.wait_ge(q_tr, 1)
            copy(qrows.rearrange("p (c n) -> p c n", c=2), ps[0:DEC, 6:8, :]).then_inc(q_rows, 1)

            def take_q(s, half):
                act.wait_ge(q_bc, s * 2 + (half + 1))
                if half == 0:
                    act.wait_ge(k_used, s * PAGES + PRIME)
                copy(qcur[:, half * 512:(half + 1) * 512], ps[:, 6, :]).then_inc(q_cur, 1)

            def round_(r, keys, more, values):
                g = r * 8 + 4 * R_IN
                for u in range(4):
                    for c in (2 * u, 2 * u + 1):
                        if c == 7:
                            if more:
                                take_q(r + 1, 0)
                            if values:
                                act.wait_ge(v_used, r * PAGES + PRIME)
                                copy(osb.rearrange("p (c n) -> p c n", c=2), ps[0:HEADS, 4:6, :]).then_inc(o_rows, 1)
                        if keys:
                            head(g, 4 + c)
                    if keys:
                        move_tile(r * 4 + T_IN, u, r * 4 + (r // 4) * 8 + u, g + (4 + 2 * u + 2))
                if more:
                    take_q(r + 1, 1)
                if keys:
                    act.wait_ge(c_sub, r + 1)
                    act.activation(pr[:, :, :], shifts, ACT.Exp).then_inc(c_p, 1)

            take_q(0, 0)
            take_q(0, 1)
            round_(0, True, True, False)
            with act.Fori(1, DEC - 1) as r:
                round_(r, True, True, True)
            round_(DEC - 1, True, False, True)
            round_(DEC, False, False, True)

            rstd64(s_sum, s_rs)
            v = [t.rearrange("p (h b) -> p h b", h=HEADS) for t in tmp5]
            act.wait_ge(s_e, 1)
            act.activation(tmp5[2], tmp5[2], ACT.Exp).then_inc(s_x, 1)
            act.activation(tmp5[3], tmp5[3], ACT.Exp).then_inc(s_x, 1)
            act.wait_ge(r_full, 1)
            for b in range(2):
                act.wait_ge(tile_spilled[b], 16 * 20)
            copy(krs.rearrange("p (c n) -> p c n", c=2), ps[0:DEC, 2:4, :]).then_inc(r_copied, 1)
            act.wait_ge(r_full, 2)
            copy(vrs.rearrange("p (c n) -> p c n", c=2), ps[0:DEC, 4:6, :]).then_inc(r_copied, 1)
            act.wait_ge(p_tr, 1)
            copy(stT, ps[:, 0, 0:480].rearrange("p (g b) -> p g b", g=POOL_G)).then_inc(p_stT, 1)
            copy(cstT, ps[:, 1, 0:64].rearrange("p (g b) -> p g b", g=CONV_T)).then_inc(p_stT, 1)
            for g in range(POOL_G):
                act.wait_ge(p_mm, g + 1)
                b = 2 + 2 * (g % 2)
                act.activation(xT[:, g, 0:SEQ], ps[:, b, :], ACT.Copy, scale=par[:, PS + g:PS + g + 1]).then_inc(p_y, 1)
                act.activation(xT[:, g, SEQ:T], ps[:, b + 1, 0:DEC], ACT.Copy,
                               scale=par[:, PS + g:PS + g + 1]).then_inc(p_y, 1)
            for n, (out, in_) in enumerate(((rows1[0:POOL_STATE, 0:512], ps[0:POOL_STATE, 6, :]),
                                            (rows1[0:DEC, 512:1024], ps[0:DEC, 7, :]),
                                            (rows2[0:2, 0:512], ps[0:2, 0, :]),
                                            (rows2[0:DEC, 512:1024], ps[0:DEC, 1, :]))):
                act.wait_ge(r_full, 3 + n)
                copy(out, in_).then_inc(r_copied, 1)

            with act.Fori(0, HEADS) as h:
                act.wait_ge(h_sum, h + 1)
                act.activation(sqs, ps[:, 0:2, :], ACT.Ln, bias=epsc[:, :], scale=1.0 / HD).then_inc(h_ln, 1)
                act.wait_ge(h_ln, h + 1)
                act.activation(sqs, sqs, ACT.Exp, scale=-0.5).then_inc(h_rs, 1)
                for n, row in enumerate((krow, vrow)):
                    act.wait_ge(h_rowsF, h * 2 + (n + 1))
                    if n == 0:
                        act.wait_ge(h_rowfree, h + 1)
                    copy(row, ps[:, 2 + n, :]).then_inc(h_rowsC, 1)
                for i in range(4):
                    act.wait_ge(h_t, h * 4 + (i + 1))
                    act.activation(probs2[:, i % 2, 0:(i + 1) * P], shifted[:, i % 2, 0:(i + 1) * P], ACT.Exp,
                                   accum_out=rsum[:, i:i + 1]).then_inc(h_e, 1)
                    if i >= 1:
                        copy_probs(act, copy, h, i - 1)
                copy_probs(act, copy, h, 3)
                act.wait_ge(h_O, h + 1)
                copy(xT[:, bass.ds(h + 8, 1), 0:SEQ], ps[:, 0:1, :]).then_inc(h_done, 1)
            act.wait_ge(h_done, HEADS)
            for n in range(2):
                act.wait_ge(h_stored[n], 16 * HEADS)

            for group in (1, 2, 3):
                norm(group)

            with act.Fori(0, 4) as i:
                for c in range(8):
                    head(i * 8 + 4 * R_O, 4 + c)
            act.wait_ge(g_tr, 1)
            copy(stfT[:, 0:11, :], ps[:, 6, 0:484].rearrange("p (s f) -> p s f", f=FT)).then_inc(g_stT, 1)
            copy(stfT[:, 11:16, :], ps[:, 7, 0:220].rearrange("p (s f) -> p s f", f=FT)).then_inc(g_stT, 1)
            norm(4)

            def ffn(i, more):
                g = i * 24 + 4 * R_F
                for u in range(8):
                    for c in (2 * u, 2 * u + 1):
                        head(g, 4 + c, down=4 + c >= 16)
                    act.wait_ge(w_used, g + (4 + 2 * u + 2))
                    pair, gate, n = u // 4, (u // 2) % 2, u % 2
                    if not gate:
                        act.wait_ge(g_cv, i * 4 + (2 * pair + n + 1))
                        act.activation(abuf[:, n, 2:2 + T].rearrange("p (c t) -> p c t", c=2),
                                       ps[:, 2 * n:2 * n + 2, 0:HALF], ACT.Copy).then_inc(acc_free[n], 1)
                    else:
                        tile = 2 * pair + n
                        act.wait_ge(g_cv, i * 4 + (tile + 3))
                        act.activation(cv[:, n, :], cv[:, n, :], ACT.Silu, bias=fcur[:, 3, tile:tile + 1])\
                           .then_inc(g_silu, 1)
                        act.wait_ge(g_h, i * 4 + (tile + 1))
                        copy(hh[:, tile, :], cv[:, n, :]).then_inc(g_hi, 1)
                for c in range(8):
                    if c < 4:
                        head(g, 20 + c, down=True)
                    elif more:
                        head(g, 20 + c)

            with act.Fori(0, GROUPS - 1) as i:
                ffn(i, True)
            ffn(GROUPS - 1, False)
            for n, (lo, hi) in enumerate(((0, 4), (4, 8), (8, 10))):
                act.wait_ge(z_ffn, 1)
                copy(astrows[:, lo:hi, :], ps[0:FT, 4 + n, 0:(hi - lo) * P].rearrange("p (s n) -> p s n", n=P))\
                    .then_inc(z_act, 1)


        @block.vector
        def _(dve):
            seq = Count(dve_seq)

            def tt(out, in0, in1, op):
                return dve.tensor_tensor(out, in0, in1, op)

            def fma(out, in0, scalar, in1):
                return dve.scalar_tensor_tensor(out, in0, scalar, in1, ALU.mult, ALU.add)

            dve.sem_inc(k_used, PRIME)
            dve.sem_inc(x2_ready, 1)
            dve.sem_inc(h_free, 1)
            dve.sem_inc(o_kept, 1)
            dve.sem_inc(g_cv, 2)
            for i in range(1, 16, 2):
                j, g = divmod(i, 4)
                dve.wait_ge(x_full, i + 2)
                dve.tensor_copy(xT[:, 4 * g:4 * g + 4, j * P:(j + 1) * P],
                                ps[:, i % 4, :].rearrange("p (k t) -> p k t", k=4)).then_inc(x_moved_dve, 1)

            def norm(group):
                lo, hi, gcol, _ = norm_groups[group]
                n0 = norm_first[group]
                dve.wait_ge(n_rb, group + 1)

                def rest(t):
                    n = n0 + t - lo
                    dve.wait_ge(n_hi, n + 1)
                    tt(xl[:, t, :], stg[:, n % 2, :], xh[:, t, :].bitcast(F32), ALU.subtract).then_inc(n_lo, 1)

                for t in range(lo, hi):
                    n = n0 + t - lo
                    if t - lo >= 2:
                        dve.wait_ge(n_lo, n - 1)
                    dve.scalar_tensor_tensor(stg[:, n % 2, :], xT[:, t, :], par[:, gcol + t - lo:gcol + t - lo + 1], rb,
                                             ALU.mult, ALU.mult).then_inc(n_tmp, 1)
                    if t > lo:
                        rest(t - 1)
                rest(hi - 1)

            dve.wait_ge(par_ready, 1)
            dve.wait_ge(x_moved_act, 9)
            dve.wait_ge(x_moved_dve, 8)
            norm(0)

            def raw_chunk(c, down):
                raw, q = wraw[:, (c // 4) % 2, :], c % 4
                if down:
                    return raw.rearrange("p (k n) -> p k n", k=FG)[:, :, q * 256:(q + 1) * 256]
                m, half = divmod(q, 2)
                return raw.rearrange("p (k n) -> p k n", k=KT)[:, half * 8:half * 8 + 8, m * P:(m + 1) * P]

            def blocks(buf, c, down):
                return buf[:, c % 4, :].rearrange("p (k n) -> p k n", k=FG if down else 8)

            def rest(g, c, down=False):
                dve.wait_ge(w_hi, g + (c + 1))
                tt(blocks(wl, c, down), raw_chunk(c, down), blocks(wh, c, down).bitcast(F32),
                   ALU.subtract).then_inc(w_lo, 1)

            for c in range(4):
                rest(0, c)

            dve.wait_ge(small_loaded, 48)
            dve.wait_ge(f_full, 1)
            step(dve, seq, dve.tensor_scalar(two(fz), ps[0:HEADS, 4:6, 0:HALF], bf[:, :], None, ALU.add))
            dve.scalar_tensor_tensor(fn, fz, -1.0, fz, ALU.mult, ALU.min).then_inc(f_nz, 1)
            dve.wait_ge(f_soft, 1)
            step(dve, seq, dve.scalar_tensor_tensor(lgv, fz, 0.0, fn, ALU.min, ALU.subtract))
            dve.tensor_tensor_scan(out=junk[0:HEADS, 0:SEQ], data0=lgv[:, 0:SEQ], data1=lgv[:, 0:SEQ], initial=0.0,
                                   op0=ALU.add, op1=ALU.bypass).then_inc(f_cum, 1)
            for i in range(2):
                for c in range(8):
                    rest(8 * i, 4 + c)
                if i == 0:
                    dve.wait_ge(e_loaded, 32)
                    lf4 = work[:, 0:2048].rearrange("p (c t h) -> p c t h", c=2, h=HEADS)
                    P4 = work[:, 2048:4096].rearrange("p (c t h) -> p c t h", c=2, h=HEADS)
                    for c in range(2):
                        for h in range(HEADS):
                            last = dve.tensor_tensor_scan(out=P4[:, c, :, h], data0=lf4[:, c, :, h],
                                                          data1=lf4[:, c, :, h], initial=0.0,
                                                          op0=ALU.add, op1=ALU.bypass)
                    last.then_inc(e_scan, 1)
                    dve.wait_ge(e_tail, 1)
                    step(dve, seq, dve.tensor_copy(tot[:, :, :], ps[:, 5, 0:16].rearrange("p (c h) -> p c h", c=2)))
                    for c in range(2):
                        for h in range(HEADS):
                            last = dve.tensor_scalar(lfE[:, c, h, :], P4[:, c, :, h], -1.0, tot[:, c, h:h + 1],
                                                     ALU.mult, ALU.add)
                    last.then_inc(e_bias, 1)
            dve.wait_ge(tile_kept, 8)
            tt(sm[:, :, :], projS[:, T_Q:T_Q + HEADS, :], projS[:, T_Q:T_Q + HEADS, :], ALU.mult).then_inc(q_sq, 1)
            dve.wait_ge(q_rs, 1)
            dve.scalar_tensor_tensor(qS[:, :, :], projS[:, T_Q:T_Q + HEADS, :], par[:, QG:QG + 1], sm[:, :, :],
                                     ALU.mult, ALU.mult).then_inc(q_n, 1)
            dve.wait_ge(q_rows, 1)
            dve.wait_ge(f_stored, 48)
            dve.wait_ge(e_kept, 4)

            def key_page(r, p):
                dve.wait_ge(k_loaded[p % RING], r * (16 * PAGES // RING) + 16 * (p // RING + 1))
                dve.wait_ge(k_used, r * PAGES + (p + PRIME))
                for h in range(HEADS):
                    last = dve.tensor_tensor_reduce(
                        out=junk[:, h * HD:(h + 1) * HD], in0=kring[:, p % RING, h * HD:(h + 1) * HD],
                        in1=qcur[:, h * HD:(h + 1) * HD], scale=SCALE, scalar=0.0, op0=ALU.mult, op1=ALU.add,
                        accum_out=S[:, p, h:h + 1])
                last.then_inc(k_used, 1)

            def mask_q(s):
                if not (isinstance(s, int) and s == 0):
                    dve.wait_ge(q_bc, s * 2)
                dve.tensor_scalar(qmask, qrows, ident[0:DEC, bass.ds(s, 1)], None, ALU.mult).then_inc(q_mask, 1)

            def round_(r, keys, more, values):
                g = r * 8 + 4 * R_IN
                if values:
                    dve.wait_ge(c_p, r)
                    dve.tensor_reduce(ps8[:, :], pr[:, :, :].rearrange("p g h -> p h g"), AX.X, ALU.add).then_inc(c_ps, 1)
                if keys:
                    dve.wait_ge(q_cur, r * 2 + 2)
                p = 0
                for c in range(8):
                    if c == 5 and more:
                        mask_q(r + 1)
                    if c == 2 and values:
                        dve.wait_ge(c_den, r)
                        dve.tensor_copy(denall[:, bass.ds(r - 1, 1), :], ps[:, 7:8, 136:144]).then_inc(c_dk, 1)
                    if c == 7 and keys:
                        dve.wait_ge(k_used, r * PAGES + (PAGES + PRIME))
                        if values:
                            dve.wait_ge(c_p, r)
                        tt(shifts, S[:, :, :], Eb[:, bass.ds(r * PAGES, PAGES), :], ALU.add).then_inc(c_se, 1)
                        dve.wait_ge(c_se, r + 1)
                        dve.tensor_reduce(mx8[:, :], shifts.rearrange("p g h -> p h g"), AX.X, ALU.max).then_inc(c_mx, 1)
                        dve.wait_ge(c_mT, r + 1)
                        dve.tensor_reduce(mx1[:, :], ps[0:HEADS, 7, 0:P], AX.X, ALU.max).then_inc(c_m1, 1)
                        dve.wait_ge(c_m1, r + 1)
                        dve.tensor_scalar(diag[:, :], ident[0:HEADS, 0:HEADS], mx1[:, :], None, ALU.mult).then_inc(c_dg, 1)
                    for _ in range(min(3, K_PER_CHUNK[c]) if keys else 0):
                        key_page(r, p)
                        p += 1
                    if keys:
                        rest(g, 4 + c)
                    for _ in range(K_PER_CHUNK[c] - 3 if keys else 0):
                        key_page(r, p)
                        p += 1
                if keys:
                    dve.wait_ge(c_mb, r + 1)
                    dve.tensor_copy(mxb[:, :], ps[:, 7, P:P + HEADS]).then_inc(c_mk, 1)
                if values:
                    dve.wait_ge(o_cols, r)
                    dve.tensor_copy(ocomb[:, bass.ds(r - 1, 1), :], ps[:, 7:8, 144:152]).then_inc(o_kept, 1)
                if keys:
                    dve.wait_ge(c_mk, r + 1)
                    tt(shifts, shifts, mxb[:, :].unsqueeze(1).broadcast_to([P, PAGES, HEADS]),
                       ALU.subtract).then_inc(c_sub, 1)
                    dve.tensor_copy(maxall[:, bass.ds(r, 1), :], mxb[:, :].unsqueeze(1))

            mask_q(0)
            round_(0, True, True, False)
            with dve.Fori(1, DEC - 1) as r:
                round_(r, True, True, True)
            round_(DEC - 1, True, False, True)
            round_(DEC, False, False, True)

            kv = projS[:, T_K:T_K + HEADS, :]
            dve.wait_ge(tile_kept, 40)
            tt(sm[:, :, :], kv, kv, ALU.mult).then_inc(s_sq, 1)
            dve.wait_ge(s_rs, 1)
            dve.scalar_tensor_tensor(kSn[:, :, :], kv, par[:, KG:KG + 1], sm[:, :, :], ALU.mult, ALU.mult).then_inc(s_kn, 1)
            dve.wait_ge(s_kn, 1)
            t3 = [t.rearrange("p (h b) -> p h b", h=HEADS) for t in tmp5]
            hb = [t[:, :, :].rearrange("p b h -> p h b") for t in (maxall, denall, ocomb)]
            tt(t3[0], qS[:, :, :], kSn[:, :, :], ALU.mult).then_inc(s_pd, 1)
            dve.wait_ge(s_sc, 1)
            own = ps[:, 6, 64:128].rearrange("p (h b) -> p h b", h=HEADS)
            dve.wait_ge(c_dk, DEC)
            step(dve, seq, dve.tensor_scalar(t3[4], own, SCALE, None, ALU.mult))
            step(dve, seq, tt(t3[1], t3[4], hb[0], ALU.max))
            tt(t3[2], hb[0], t3[1], ALU.subtract)
            tt(t3[3], t3[4], t3[1], ALU.subtract).then_inc(s_e, 1)
            dve.wait_ge(s_x, 2)
            step(dve, seq, tt(t3[0], hb[1], t3[2], ALU.mult))
            step(dve, seq, tt(t3[0], t3[0], t3[3], ALU.add))
            step(dve, seq, dve.reciprocal(t3[4], t3[0]))
            step(dve, seq, tt(t3[1], hb[2], t3[2], ALU.mult))
            step(dve, seq, tt(t3[3], t3[3], projS[:, T_V:T_V + HEADS, :], ALU.mult))
            step(dve, seq, tt(t3[1], t3[1], t3[3], ALU.add))
            tt(xT[:, 8:16, SEQ:T], t3[1], t3[4], ALU.mult).then_inc(s_done, 1)

            dve.wait_ge(r_stored, 32)
            dve.memset(ub[:, :, 0:16], 0.0)
            dve.memset(shA[:, 0:16], 0.0)
            step(dve, seq, dve.memset(shB[:, 0:16], 0.0))
            dve.wait_ge(p_loaded, 16)
            dve.wait_ge(p_stT, 2)
            n_mm = 0
            for g in range(POOL_G):
                win = 2 << g
                cur = ub[:, g, :]
                for n in range(g + 1):
                    nxt = shA if n % 2 == 0 else shB
                    sh = 1 << n
                    step(dve, seq, tt(nxt[:, 16:528], cur[:, 16:528], cur[:, 16 - sh:528 - sh], ALU.add))
                    cur = nxt
                if g:
                    dve.wait_ge(p_mm, g)
                step(dve, seq, tt(pooled[:, 0:win], cur[:, 16:16 + win], rc[:, 0:win], ALU.mult))
                step(dve, seq, tt(pooled[:, 0:win], pooled[:, 0:win], ub[:, g, 16:16 + win], ALU.subtract))
                step(dve, seq, dve.scalar_tensor_tensor(pooled[:, win:SEQ], cur[:, 16 + win:528], 1.0 / win,
                                                        ub[:, g, 16 + win:528], ALU.mult, ALU.subtract))
                old = stT[:, g, :].rearrange("p (b t) -> p b t", b=DEC)[:, :, POOL_STATE + 1 - win:POOL_STATE]
                step(dve, seq, dve.tensor_reduce(pooled[:, SEQ:T], old, AX.X, ALU.add))
                step(dve, seq, tt(pooled[:, SEQ:T], pooled[:, SEQ:T], projS[:, T_U + g, :], ALU.add))
                dve.scalar_tensor_tensor(pooled[:, SEQ:T], pooled[:, SEQ:T], 1.0 / win, projS[:, T_U + g, :],
                                         ALU.mult, ALU.subtract).then_inc(p_pooled, 1)

            def tap(j, t):
                return par[:, CW + 4 * j + t:CW + 4 * j + t + 1]

            step(dve, seq, dve.memset(cz[:, 0:2], 0.0))
            dve.wait_ge(p_y, 2 * POOL_G)
            for t in range(CONV_T):
                dve.wait_ge(v_in, 16 * (t + 1))
                cs = cstT[:, t, :].rearrange("p (b j) -> p b j", j=2)
                zs = zs4[:, DEC * t:DEC * (t + 1)]
                tt(zs, projS[:, T_C + t, :], projS[:, T_X + t, :], ALU.mult)
                step(dve, seq, tt(cz[:, 2:514], c3[:, 1, :], c3[:, 2, :], ALU.mult))
                dve.tensor_copy(zl4[:, 2 * t:2 * t + 2], cz[:, 512:514])
                dve.tensor_scalar(ct[:, SEQ:T], cs[:, :, 0], tap(0, t), None, ALU.mult)
                step(dve, seq, dve.tensor_scalar(ct[:, 0:SEQ], cz[:, 0:512], tap(0, t), None, ALU.mult))
                fma(ct[:, SEQ:T], cs[:, :, 1], tap(1, t), ct[:, SEQ:T])
                step(dve, seq, fma(ct[:, 0:SEQ], cz[:, 1:513], tap(1, t), ct[:, 0:SEQ]))
                fma(ct[:, SEQ:T], zs, tap(2, t), ct[:, SEQ:T])
                step(dve, seq, fma(ct[:, 0:SEQ], cz[:, 2:514], tap(2, t), ct[:, 0:SEQ]))
                tt(xT[:, 4 + t, SEQ:T], ct[:, SEQ:T], projS[:, T_B + t, :], ALU.mult)
                tt(xT[:, 4 + t, 0:SEQ], ct[:, 0:SEQ], c3[:, 0, :], ALU.mult).then_inc(v_done, 1)
                dve.wait_ge(v_done, t + 1)

            with dve.Fori(0, HEADS) as h:
                dve.wait_ge(h_loaded[0], h * 16 + 16)
                dve.wait_ge(h_loaded[1], h * 16 + 16)
                tt(sqs, qkv[:, 0:2, :], qkv[:, 0:2, :], ALU.mult).then_inc(h_sq, 1)
                dve.tensor_copy(cqh[:, :], cqT[:, :, bass.ds(h, 1)].rearrange("p j a -> p (j a)")).then_inc(h_cq, 1)
                dve.wait_ge(h_rs, h + 1)
                for n, gcol in enumerate((QG, KG)):
                    last = dve.scalar_tensor_tensor(qk[:, n, :], qkv[:, n, :], par[:, gcol:gcol + 1], sqs[:, n, :],
                                                    ALU.mult, ALU.mult)
                last.then_inc(h_qk, 1)
                dve.wait_ge(h_cq, h + 1)
                for i in range(4):
                    n = (i + 1) * P
                    t = shifted[:, i % 2, 0:n]
                    if i >= 2:
                        dve.wait_ge(h_e, h * 4 + (i - 1))
                    dve.tensor_scalar(t, cb[:, 0:n], -1.0, cqh[:, i:i + 1], ALU.mult, ALU.add).then_inc(h_bias, 1)
                    dve.wait_ge(h_bias, h * 8 + (2 * i + 1))
                    d = shifted[:, i % 2, n - P:n]
                    tt(d, d, cmask[:, :], ALU.add).then_inc(h_bias, 1)
                    dve.wait_ge(h_bias, h * 8 + (2 * i + 2))
                    dve.wait_ge(h_S, h * 4 + (i + 1))
                    fma(t, ps[:, 4 + i % 2, 0:n], SCALE, t).then_inc(h_sc, 1)
                    dve.wait_ge(h_sc, h * 4 + (i + 1))
                    dve.tensor_reduce(rmax[:, i:i + 1], t, AX.X, ALU.max).then_inc(h_mx, 1)
                    dve.wait_ge(h_mx, h * 4 + (i + 1))
                    dve.tensor_scalar(t, t, rmax[:, i:i + 1], None, ALU.subtract).then_inc(h_t, 1)
                    if i >= 1:
                        normalize(dve, h, i - 1)
                normalize(dve, h, 3)
                dve.wait_ge(h_rowsF, h * 2 + 2)
                dve.wait_ge(h_pT, h * 4 + 4)
                dve.sem_inc(h_free, 1)

            for group in (1, 2, 3):
                norm(group)

            with dve.Fori(0, 4) as i:
                g = i * 8 + 4 * R_O
                for u in range(4):
                    for c in (2 * u, 2 * u + 1):
                        rest(g, 4 + c)
                    dve.wait_ge(w_used, g + (4 + 2 * u + 2))
                    if u == 0:
                        dve.wait_ge(res_loaded, i * 16 + 16)
                    b = 2 * (u % 2)
                    tt(two(xres[:, u, :]), ps[:, b:b + 2, 0:HALF], two(xres[:, u, :]), ALU.add).then_inc(acc_free[u % 2], 1)
                    dve.wait_ge(acc_free[u % 2], i * 2 + (T_O // 2 + u // 2 + 2))
                    dve.tensor_copy(xT[:, bass.ds(i * 4 + u, 1), :], xres[:, u:u + 1, :]).then_inc(x2_ready, 1)
            dve.wait_ge(x2_ready, KT + 1)
            norm(4)

            fw = par[:, FW:FW + 4 * FT].rearrange("p (j f) -> p j f", j=4)
            dve.memset(abuf[:, :, 0:2], 0.0).then_inc(g_cur, 1)
            dve.wait_ge(g_stT, 2)

            def conv(i, tile, n, u):
                dve.wait_ge(acc_free[n], i * 12 + (T_FF // 2 + u // 2 + 2))
                A = abuf[:, n, :]
                w = [fcur[:, j, tile:tile + 1] for j in range(3)]
                old = stcur.rearrange("p (b j) f -> p b j f", j=2)[:, :, :, tile]
                dve.tensor_copy(ast[:, 0:DEC, bass.ds(i * 4 + tile, 1)], A[:, 514:522].unsqueeze(2))
                dve.tensor_copy(ast[:, DEC:DEC + 2, bass.ds(i * 4 + tile, 1)], A[:, 512:514].unsqueeze(2)).then_inc(g_kept, 1)
                dve.wait_ge(g_hi, i * 4 + (tile + 1))
                dve.wait_ge(g_lo_own, i * 4 + (tile + 1))
                C = cv[:, n, :]
                dve.tensor_scalar(C[:, SEQ:T], old[:, :, 0], w[0], None, ALU.mult)
                dve.tensor_scalar(C[:, 0:SEQ], A[:, 0:512], w[0], None, ALU.mult).then_inc(g_t0, 1)
                dve.wait_ge(g_t0, i * 4 + (tile + 1))
                fma(C[:, SEQ:T], old[:, :, 1], w[1], C[:, SEQ:T])
                fma(C[:, 0:SEQ], A[:, 1:513], w[1], C[:, 0:SEQ]).then_inc(g_t1, 1)
                dve.wait_ge(g_t1, i * 4 + (tile + 1))
                fma(C[:, SEQ:T], A[:, 514:522], w[2], C[:, SEQ:T])
                fma(C[:, 0:SEQ], A[:, 2:514], w[2], C[:, 0:SEQ]).then_inc(g_cv, 1)

            def ffn(i, more):
                g = i * 24 + 4 * R_F
                dve.tensor_copy(fcur, fw[:, :, bass.ds(i * FG, FG)])
                dve.tensor_copy(stcur, stfT[:, :, bass.ds(i * FG, FG)]).then_inc(g_cur, 1)
                dve.wait_ge(g_cur, i + 2)
                for u in range(8):
                    for c in (2 * u, 2 * u + 1):
                        rest(g, 4 + c, down=4 + c >= 16)
                    pair, gate, n = u // 4, (u // 2) % 2, u % 2
                    tile = 2 * pair + n
                    if not gate:
                        conv(i, tile, n, u)
                    else:
                        dve.wait_ge(w_used, g + (4 + 2 * u + 2))
                        dve.wait_ge(g_silu, i * 4 + (tile + 1))
                        dve.tensor_tensor(two(cv[:, n, :]), ps[:, 2 * n:2 * n + 2, 0:HALF], two(cv[:, n, :]),
                                          ALU.mult).then_inc(acc_free[n], 1)
                        dve.wait_ge(acc_free[n], i * 12 + (T_FF // 2 + u // 2 + 2))
                        dve.sem_inc(g_h, 1)
                        dve.wait_ge(g_hi, i * 4 + (tile + 3))
                        tt(hl[:, tile, :], cv[:, n, :], hh[:, tile, :].bitcast(F32), ALU.subtract).then_inc(g_lo, 1)
                        dve.wait_ge(g_lo, i * 4 + (tile + 1))
                        dve.sem_inc(g_lo_own, 1)
                for c in range(8):
                    for m in range(2):
                        dve.wait_ge(*((g_half, i * 8 + (c + 1)) if m == 0 else (w_used, g + (4 + 16 + c + 1))))
                        y = two(xT[:, 2 * c + m, :])
                        tt(y, ps[:, 2 * m:2 * m + 2, 0:HALF], y, ALU.add).then_inc(acc_free[m], 1)
                    if c < 4:
                        rest(g, 20 + c, down=True)
                    elif more:
                        rest(g, 20 + c)
                dve.wait_ge(acc_free[0], i * 12 + (T_FF // 2 + 13))
                dve.wait_ge(acc_free[1], i * 12 + (T_FF // 2 + 13))
                dve.sem_inc(g_y, 1)

            dve.sem_inc(g_lo_own, 2)
            with dve.Fori(0, GROUPS - 1) as i:
                ffn(i, True)
            ffn(GROUPS - 1, False)
            for i in range(20):
                j, q = divmod(i, 4)
                dve.wait_ge(z_full, i + 1)
                if q == 0 and j >= 2:
                    dve.wait_ge(z_stored[j % 2], 16 * (j // 2))
                n = P if j < 4 else DEC
                dve.tensor_copy(orow[0:n, j % 2, q * 512:(q + 1) * 512], ps[0:n, i % 4, :]).then_inc(z_rows, 1)



_OUTS = [("y_prompt", (1, SEQ, D_MODEL)), ("y_sample", (DEC, 1, D_MODEL)),
         ("k_prompt", (1, 1, SEQ, HEADS, HD)), ("v_prompt", (1, 1, SEQ, HEADS, HD)),
         ("logf_prompt", (1, 1, SEQ, HEADS)), ("pool_prompt", (1, 1, POOL_STATE, 512)),
         ("conv_prompt", (1, 1, 2, 512)), ("ffn_prompt", (1, 1, 2, D_FF)),
         ("k_sample", (1, DEC, 1, HEADS, HD)), ("v_sample", (1, DEC, 1, HEADS, HD)),
         ("logf_sample", (1, DEC, 1, HEADS)), ("pool_sample", (1, DEC, POOL_STATE, 512)),
         ("conv_sample", (1, DEC, 2, 512)), ("ffn_sample", (1, DEC, 2, D_FF))]


def kernel(**inputs):
    import concourse.bacc as bacc
    from concourse.bass_utils import run_bass_kernel_spmd

    nc = bacc.Bacc("TRN2", target_bir_lowering=False, num_devices=1)
    arrays, a, o = {}, {}, {}
    for name, value in inputs.items():
        v = np.ascontiguousarray(value)
        arrays[f"in_{name}"] = v
        a[name] = nc.dram_tensor(f"in_{name}", v.shape, mybir.dt.from_np(v.dtype), kind="ExternalInput").ap()
    for name, shape in _OUTS:
        o[name] = nc.dram_tensor(f"out_{name}", shape, F32, kind="ExternalOutput").ap()
    hybrid_layer_kernel(nc, a, o)
    r = run_bass_kernel_spmd(nc, [arrays], core_ids=[0])
    return tuple(r.results[0][f"out_{name}"] for name, _ in _OUTS)
```

```python
import concourse.bass as bass
import numpy as np
from concourse import mybir
from contextlib import ExitStack

F32 = mybir.dt.float32
F32R = mybir.dt.float32r
I32 = mybir.dt.int32
ALU = mybir.AluOpType
ACT = mybir.ActivationFunctionType
AX = mybir.AxisListType
P = 128

D_MODEL = 2048
SEQ = 512
DEC = 8
T = SEQ + DEC
HALF = T // 2
HEADS = 8
HD = 128
PAST = 4096
PAGES = PAST // P
POOL_G = 4
POOL_STATE = 15
CONV_T = 4
D_FF = 5632
KT = D_MODEL // P
FT = D_FF // P
FG = 4
GROUPS = FT // FG
EPS = 1e-6
SCALE = HD ** -0.5
MASKED = -1e30

T_U, T_B, T_C, T_X, T_Q, T_K, T_V, T_F = 0, 4, 8, 12, 16, 24, 32, 40
G1, G2, GO, PS, CW, QG, KG, FW, FB = 0, 16, 32, 48, 52, 64, 65, 66, 198
PARAM_ROWS = 66
RAW = 4096
CHUNK = 1024
RING = 4
K_PER_CHUNK = [5, 5, 5, 5, 4, 4, 4, 0]
V_PER_CHUNK = [4, 4, 5, 5, 5, 5, 4, 0]


class Count:

    def __init__(self, sem):
        self.sem, self.base, self.n = sem, 0, 0

    def inc(self, ins):
        ins.then_inc(self.sem, 1)
        self.n += 1
        return ins

    def value(self):
        return self.base + self.n

    def loop(self, i, start, per):
        self.base, self.n = i * per + start, 0

    def after(self, value):
        self.base, self.n = value, 0


def hybrid_layer_kernel(nc, a, o):
    ctx = ExitStack()
    with ctx:
        def sb(name, shape, dt=F32):
            return ctx.enter_context(nc.sbuf_tensor("t_" + name, shape, dt))

        def sem(name):
            return ctx.enter_context(nc.semaphore(name))

        with nc.sbuf_tensor("t_aux0", [P, KT * T], F32) as aux0:
            pass
        xh = sb("xh", [P, KT, T], F32R)
        with nc.sbuf_tensor("t_aux1", [P, KT * T], F32) as aux1:
            pass
        xl = sb("xl", [P, KT, T], F32R)
        r1 = sb("r1", [P, KT * T])
        xT = r1[:, :].rearrange("p (k t) -> p k t", k=KT)
        kring = r1[:, 0:RING * 1024].rearrange("p (s n) -> p s n", s=RING)
        vring = r1[:, KT * T - RING * 1024:KT * T].rearrange("p (s n) -> p s n", s=RING)
        wraw = sb("wraw", [P, 2, RAW])
        wh = sb("wh", [P, 4, CHUNK], F32R)
        wl = sb("wl", [P, 4, CHUNK], F32R)
        stg = sb("stg", [P, 2, T])
        ident = sb("ident", [P, P])
        ones = sb("ones", [P, P])
        cmask = sb("cmask", [P, P])
        par = sb("par", [P, 242])
        rc = sb("rc", [P, 16])
        epsc = sb("epsc", [P, 1])
        projS = sb("projS", [P, 40, DEC])
        bf = sb("bf", [HEADS, 1])
        ptr = sb("ptr", [1, DEC * PAGES], I32)
        pti = sb("pti", [P, 2], I32)
        fraw = sb("fraw", [P, KT, HEADS])
        S = sb("S", [P, PAGES, HEADS])
        pr = sb("pr", [P, PAGES, HEADS])
        tri = pr[:, 0:P // HEADS, :].rearrange("p g h -> p (g h)")
        sel = S[0:DEC, :, :].rearrange("p g h -> p (g h)")
        qS = sb("qS", [P, HEADS, DEC])
        sm = sb("sm", [P, HEADS, DEC])
        kSn = sb("kSn", [P, HEADS, DEC])
        maxall = sb("maxall", [P, DEC, HEADS])
        denall = sb("denall", [P, DEC, HEADS])
        ocomb = sb("ocomb", [P, DEC, HEADS])
        mx8 = sb("mx8", [P, HEADS])
        mx1 = sb("mx1", [HEADS, 1])
        mxb = sb("mxb", [P, HEADS])
        diag = sb("diag", [HEADS, HEADS])
        ps8 = sb("ps8", [P, HEADS])
        lfT = sb("lfT", [P, 4, HEADS])
        cqT = sb("cqT", [P, 4, HEADS])
        lfS = sb("lfS", [DEC, HEADS])
        tot = sb("tot", [P, 2, HEADS])
        cqh = sb("cqh", [P, 2, 4])
        rmax = sb("rmax", [P, 4])
        nmax = sb("nmax", [P, 4])
        qgs = sb("qgs", [P, 1])
        rsum = sb("rsum", [P, 4])
        with nc.sbuf_tensor("t_work", [P, 8192], F32) as work:
            pass
        hh = sb("hh", [P, FG, T], F32R)
        hl = sb("hl", [P, FG, T], F32R)
        xr = work[:, :].rearrange("p (s n) -> p s n", s=4)
        rb = work[:, 7672:8192]
        lf = work[:, 0:2048].rearrange("p (c n) -> p c n", c=2)
        Eb = work[:, 2048:4096].rearrange("p (g h) -> p g h", h=HEADS)
        qmask = work[0:DEC, 0:1024]
        junk = work[:, 4096:5120]
        qrows = work[0:DEC, 5120:6144]
        qcur = work[:, 6144:7168]
        osb = work[0:HEADS, 7168:8192]
        shifts = work[:, 1024:1280].rearrange("p (g h) -> p g h", h=HEADS)
        ps = ctx.enter_context(nc.psum_tensor("ps", [P, 8, 512], F32))

        def acc(t):
            return ps[:, 2 * (t % 2):2 * (t % 2) + 2, 0:HALF]

        def two(ap):
            return ap.rearrange("p (c t) -> p c t", c=2)

        scr = nc.dram_tensor("scr_proj", (40, P, SEQ), F32, kind="Internal").ap()
        scrx = nc.dram_tensor("scr_x", (KT, P, T), F32, kind="Internal").ap()
        scrc = nc.dram_tensor("scr_c", (HEADS, SEQ), F32, kind="Internal").ap()

        def sems(names):
            return [sem(x) for x in names.split()]

        const_ready, prow_loaded, small_loaded, par_full, par_ready = sems(
            "const_ready param_rows_loaded small_loaded params_transposed params_ready")
        xs_loaded, x_full, x_moved_act, x_moved_dve, x_spilled = sems(
            "x_sample_loaded x_transposed x_moved_by_act x_moved_by_dve x_spilled")
        x_loaded = [sem(f"x_block{j}_loaded") for j in range(4)]
        n_sq, n_sum, n_rb, n_tmp, n_hi, n_lo = sems(
            "norm_square_ready norm_square_summed norm_rstd_ready norm_scaled_ready norm_head_ready norm_rest_ready")
        w_loaded = [sem(f"weights_loaded{j}") for j in range(2)]
        w_hi, w_lo, w_used = sems("weight_head_ready weight_rest_ready weight_chunk_used")
        acc_free = [sem(f"accumulators{j}_free") for j in range(2)]
        tile_kept, act_seq, dve_seq = sems("sample_columns_kept act_sequence dve_sequence")
        tile_spilled = [sem(f"tile_spilled{j}") for j in range(2)]
        f_loaded, f_full, f_z, f_nz, f_soft, f_log, f_cum, f_cols, f_kept, f_stored = sems(
            "f_weights_loaded f_full f_z_ready f_negabs_ready f_softplus_ready "
            "logf_ready logf_summed logf_columns_full logf_columns_kept logf_stored")
        e_loaded, e_scan, e_tail, e_tails, e_bias, e_full, e_kept = sems(
            "page_logf_loaded page_logf_summed tails_full tails_ready biases_ready biases_transposed biases_kept")
        q_sq, q_sum, q_rs, q_n, q_tr, q_rows = sems(
            "q_square_ready q_square_summed q_rstd_ready q_normed q_rows_full q_rows_ready")
        k_loaded = [sem(f"k_page_loaded{j}") for j in range(RING)]
        v_loaded = [sem(f"v_page_loaded{j}") for j in range(RING)]
        k_used, v_used = sems("k_page_used v_page_used")
        q_mask, q_bc, q_cur = sems("q_row_masked q_broadcast_full q_current_ready")
        c_se, c_mx, c_mT, c_m1, c_dg, c_mb, c_sub, c_mk, c_p, c_ps, c_den, c_dk = sems(
            "scores_biased page_max_ready page_max_transposed sequence_max_ready sequence_max_diagonal max_broadcast_full "
            "scores_shifted max_kept probs_ready probs_summed den_full den_kept")
        o_rows, o_cols, o_kept = sems("o_rows_ready o_columns_full o_columns_kept")
        s_e, s_x, s_sq, s_sum, s_rs, s_kn, s_pd, s_sc, s_done = sems(
            "own_exponents_ready own_exp_ready k_square_ready k_square_summed k_rstd_ready k_normed qk_product_ready qk_sum_full sample_mixed")
        r_full, r_copied, r_stored = sems("rows_full rows_copied rows_stored")
        p_loaded, p_states, p_tr, p_stT, p_pooled, p_mm, p_y = sems(
            "pool_inputs_loaded mixer_states_loaded states_transposed states_ready pooled_ready pool_mixed pool_y_ready")
        v_in = [sem(f"conv_inputs{j}_loaded") for j in range(CONV_T)]
        v_done = sem("conv_done")
        h_loaded = sems("head_loaded head_decays_loaded")
        h_stored = sems("head_keys_stored head_values_stored")
        h_rowfree, h_ln, h_free, h_sq, h_sum, h_rs, h_qk, h_rowsF, h_rowsC = sems(
            "head_rows_free head_log_ready head_inputs_free head_squares_ready head_squares_summed head_rstd_ready head_qk_normed head_rows_full "
            "head_rows_copied")
        h_cq, h_bias, h_sc, h_mx, h_ri, h_S, h_t, h_e, h_pn, h_pT, h_pC, h_O, h_done = sems(
            "head_decays_ready head_bias_ready head_scores_ready head_max_ready head_sum_inverted head_scores_full head_scores_shifted head_exp_ready head_probs_ready head_probs_transposed "
            "head_probs_copied head_out_full head_out_ready")
        res_loaded, x2_ready = sems("residual_loaded x2_ready")
        g_states, g_tr, g_stT, g_cur, g_kept, g_cv, g_silu, g_h, g_hi, g_lo, g_half, g_y = sems(
            "ffn_states_loaded ffn_states_full ffn_states_ready ffn_columns_ready a_kept conv_ready "
            "silu_ready hidden_ready hidden_head hidden_rest down_tile_full y_added")
        g_t0, g_t1, g_lo_own = sems("tap0_done tap1_done hidden_slot_free")
        z_full, z_ffn, z_act, z_rows = sems("out_full ffn_rows_full ffn_rows_copied out_rows_ready")
        z_stored = [sem(f"out_stored{j}") for j in range(2)]
        states_copied = sem("states_copied")

        w_in_v = a["w_in"].rearrange("l (k p) n -> p (l k) n", p=P)
        w_o_v = a["w_o"].rearrange("l (k p) n -> p (l k) n", p=P)
        w_up_v = a["w_up"].rearrange("l (k p) n -> p (l k) n", p=P)
        w_down_v = a["w_down"].rearrange("l (k p) n -> p (l k) n", p=P)
        k_pages = a["cache_k"].rearrange("l g t h d -> (l g) t (h d)")
        v_pages = a["cache_v"].rearrange("l g t h d -> (l g) t (h d)")
        lf_pages = a["cache_logf"].rearrange("l g t h -> (l g) (t h)")
        N_POOL = k_pages.shape[0]

        R_Q, R_IN, R_O, R_F = 0, 4, 20, 28
        T_IN, T_O, T_FF = 8, 40, 56
        N_CONST = 28
        PRIME = RING

        def step(eng, count, ins):
            count.inc(ins)
            eng.wait_ge(count.sem, count.value())

        lgv = work[0:HEADS, 6144:6144 + T]
        fz = work[0:HEADS, 7168:7168 + T]
        fn = junk[0:HEADS, 0:T]
        Pc = work[:, 2048:4096].rearrange("p (c n) -> p c n", c=2)
        lfE = work[:, 0:2048].rearrange("p (c h t) -> p c h t", c=2, h=HEADS)
        ub = aux0[:, 0:2112].rearrange("p (g t) -> p g t", g=POOL_G)
        shA, shB = aux0[:, 2112:2640], aux0[:, 2640:3168]
        pooled = aux0[:, 3168:3688]
        strow = aux0[0:120, 3688:4200]
        cstrow = aux0[0:16, 4200:4712]
        poolw = aux0[:, 4712:5224].rearrange("p (g d) -> p g d", g=POOL_G)
        stT = aux0[:, 5224:5704].rearrange("p (g b) -> p g b", g=POOL_G)
        cstT = aux0[:, 5704:5768].rearrange("p (g b) -> p g b", g=CONV_T)
        rows1 = aux0[0:16, 5768:6792]
        rows2 = aux0[0:16, 6792:7816]
        c3 = aux1[:, 0:CONV_T * 1536].rearrange("p (g c t) -> p g c t", g=CONV_T, c=3)
        ct, cz = aux1[:, 6144:6664], aux1[:, 6664:7178]
        zs4 = aux1[:, 7178:7210]
        zl4 = aux1[:, 7210:7218]
        tmp5 = [work[:, 7816 + 64 * i:7880 + 64 * i] for i in range(5)]
        krs = stg[0:DEC, :, :].rearrange("p a b -> p (a b)")[:, 0:1024]
        vrs = work[0:DEC, 4608:5632]
        qkv = [x[:, 0:1536].rearrange("p (c t) -> p c t", c=3) for x in (aux0, aux1)]
        cb = [x[:, 1536:2048] for x in (aux0, aux1)]
        qk = [x[:, 2048:3072].rearrange("p (c t) -> p c t", c=2) for x in (aux0, aux1)]
        sqs = [x[:, 3072:4096].rearrange("p (c t) -> p c t", c=2) for x in (aux0, aux1)]
        krow = [x[:, 4096:4608] for x in (aux0, aux1)]
        vrow = [x[:, 4608:5120] for x in (aux0, aux1)]
        at = [0, P, 3 * P, 6 * P, 10 * P]
        shifted = [work[:, at[i]:at[i + 1]] for i in range(4)]
        probs2 = [work[:, 1280 + at[i]:1280 + at[i + 1]] for i in range(4)]
        pT = work[:, 2560:4608].rearrange("p (k t) -> p k t", k=4)
        xres = work[:, 0:4 * T].rearrange("p (m t) -> p m t", m=4)
        abuf = work[:, 4160:5204].rearrange("p (s t) -> p s t", s=2)
        cv = work[:, 5204:6244].rearrange("p (s t) -> p s t", s=2)
        fcur = work[:, 6244:6260].rearrange("p (j i) -> p j i", j=4)
        stfT = work[:, 6260:6964].rearrange("p (s f) -> p s f", s=2 * DEC)
        ast = work[:, 6964:7404].rearrange("p (s f) -> p s f", s=DEC + 2)
        stcur = work[:, 7404:7468].rearrange("p (s i) -> p s i", s=2 * DEC)
        strows = work[0:FT, 2080:2080 + 2 * DEC * P].rearrange("p (s n) -> p s n", s=2 * DEC)
        astrows = work[0:FT, 4160:4160 + (DEC + 2) * P].rearrange("p (s n) -> p s n", s=DEC + 2)
        orow = work[:, 0:4096].rearrange("p (s n) -> p s n", s=2)

        def transposed_probs(pe, tr, h, i):
            pe.wait_ge(h_pn, h * 4 + (i + 1))
            if i >= 2:
                pe.wait_ge(h_pC, h * 4 + (i - 1))
            for k in range(i + 1):
                last = tr(ps[:, 6 + i % 2, k * P:(k + 1) * P], probs2[i][:, k * P:(k + 1) * P], P)
            last.then_inc(h_pT, 1)

        def copy_probs(act, copy, h, i):
            act.wait_ge(h_pT, h * 4 + (i + 1))
            copy(pT[:, 0:i + 1, i * P:(i + 1) * P],
                 ps[:, 6 + i % 2, 0:(i + 1) * P].rearrange("p (k t) -> p k t", t=P)).then_inc(h_pC, 1)

        def normalize(dve, h, i):
            dve.wait_ge(h_e, h * 4 + (i + 1))
            dve.reciprocal(rsum[:, i:i + 1], rsum[:, i:i + 1]).then_inc(h_ri, 1)
            dve.wait_ge(h_ri, h * 4 + (i + 1))
            dve.tensor_scalar(probs2[i], probs2[i], rsum[:, i:i + 1], None, ALU.mult).then_inc(h_pn, 1)

        def attention(eng, step_):
            with eng.Fori(0, HEADS // 2 - 1) as j:
                step_(j * 2, 0, False)
                step_(j * 2 + 1, 1, False)
            step_(HEADS - 2, 0, False)
            step_(HEADS - 1, 1, True)

        block = ctx.enter_context(nc.Block())

        @block.gpsimd
        def _(pool):
            cst = Count(const_ready)
            cst.inc(pool.memset(ident[:, :], 0.0))
            cst.inc(pool.memset(ones[:, :], 1.0))
            cst.inc(pool.memset(cmask[:, :], 0.0))
            cst.inc(pool.memset(tri[:, :], 1.0))
            cst.inc(pool.memset(sel[:, :], 1.0))
            for t in range(16):
                cst.inc(pool.memset(rc[:, t:t + 1], 1.0 / (t + 1)))
            cst.inc(pool.memset(epsc[:, :], EPS))
            pool.wait_ge(const_ready, cst.value())
            cst.inc(pool.affine_select(out=ident[:, :], in_=ident[:, :], compare_op=ALU.not_equal, fill=1.0,
                                       base=0, pattern=[[-1, P]], channel_multiplier=1))
            cst.inc(pool.affine_select(out=cmask[:, :], in_=cmask[:, :], compare_op=ALU.is_ge, fill=MASKED,
                                       base=0, pattern=[[-1, P]], channel_multiplier=1))
            cst.inc(pool.affine_select(out=tri[:, :], in_=tri[:, :], compare_op=ALU.is_ge, fill=0.0,
                                       base=0, pattern=[[-1, P]], channel_multiplier=1))
            pool.wait_ge(const_ready, cst.value())
            tv = tri.rearrange("p (a c) -> p a c", c=PAGES)
            cst.inc(pool.affine_select(out=tv, in_=tv, compare_op=ALU.is_ge, fill=0.0, base=PAGES - 1,
                                       pattern=[[PAGES, P // PAGES], [0, PAGES]], channel_multiplier=-1))
            sv = sel.rearrange("p (a c) -> p a c", c=PAGES)
            cst.inc(pool.affine_select(out=sv, in_=sv, compare_op=ALU.is_equal, fill=0.0, base=0,
                                       pattern=[[-1, DEC], [0, PAGES]], channel_multiplier=1))
            assert cst.value() <= N_CONST, cst.value()
            cst.inc(pool.memset(mx8[:, :], 0.0))
            pool.wait_ge(x_moved_act, 9)
            pool.wait_ge(x_moved_dve, 8)
            pool.dma_start(scrx.rearrange("k p t -> p k t"), xT).then_inc(x_spilled, 16)
            pool.wait_ge(small_loaded, 48)
            pool.wait_ge(n_lo, KT)
            for c in range(2):
                pool.indirect_dma_start(lf[:, c, :], None, lf_pages,
                                        bass.IndirectOffsetOnAxis(ap=pti[:, c:c + 1], axis=0)).then_inc(e_loaded, 16)
            pool.dma_start(o["pool_sample"][0, :, 0:POOL_STATE - 1, :],
                           a["state_pool"][0, :, 1:POOL_STATE, :]).then_inc(states_copied, 16)
            pool.dma_start(o["conv_sample"][0, :, 0:1, :], a["state_conv"][0, :, 1:2, :]).then_inc(states_copied, 16)
            pool.dma_start(o["ffn_sample"][0, :, 0:1, :], a["state_ffn"][0, :, 1:2, :]).then_inc(states_copied, 16)
            pool.wait_ge(f_cum, 1)
            pool.dma_start(scrc, junk[0:HEADS, 0:SEQ]).then_inc(f_stored, 16)
            pool.wait_ge(f_kept, 3)
            pool.dma_start(o["logf_prompt"][0, 0].rearrange("(j p) h -> p j h", p=P), lfT[:, :, :]).then_inc(f_stored, 16)
            pool.dma_start(o["logf_sample"][0, :, 0, :], lfS[:, :]).then_inc(f_stored, 16)

            for n, (dst, src) in enumerate(((o["pool_prompt"][0, 0], rows1[0:POOL_STATE, 0:512]),
                                            (o["pool_sample"][0, :, POOL_STATE - 1, :], rows1[0:DEC, 512:1024]),
                                            (o["conv_prompt"][0, 0], rows2[0:2, 0:512]),
                                            (o["conv_sample"][0, :, 1, :], rows2[0:DEC, 512:1024]),
                                            (o["k_sample"][0, :, 0].rearrange("b h d -> b (h d)"), krs),
                                            (o["v_sample"][0, :, 0].rearrange("b h d -> b (h d)"), vrs))):
                pool.wait_ge(r_copied, n + 1)
                pool.dma_start(dst, src).then_inc(r_stored, 16)

            pool.wait_ge(z_act, 3)
            for b in range(DEC):
                pool.dma_start(o["ffn_sample"][0, b, 1, :].rearrange("(t n) -> t n", n=P),
                               astrows[:, b, :]).then_inc(states_copied, 16)
            for j in range(2):
                pool.dma_start(o["ffn_prompt"][0, 0, j, :].rearrange("(t n) -> t n", n=P),
                               astrows[:, DEC + j, :]).then_inc(states_copied, 16)
            pool.wait_ge(states_copied, 16 * 13)
            pool.wait_ge(f_stored, 48)
            pool.wait_ge(r_stored, 96)

        @block.sync
        def _(sp):
            sp.dma_start(xr[0:DEC, 3, :], a["x_sample"].rearrange("b t d -> (b t) d")).then_inc(xs_loaded, 16)
            xp = a["x_prompt"].rearrange("b (j p) d -> (b j) p d", p=P)
            for j in range(3):
                sp.dma_start(xr[:, j, :], xp[j]).then_inc(x_loaded[j], 16)
            pv = stg[:, :, :].rearrange("p a b -> p (a b)")

            def rows(lo, n, ap):
                at, row = (0, lo) if lo < P else (lo // P, lo % P)
                sp.dma_start(pv[row:row + n, at * P:(at + 1) * P], ap).then_inc(prow_loaded, 16)

            rows(G1, 16, a["norm1_g"][0].rearrange("(k p) -> k p", p=P))
            rows(G2, 16, a["norm2_g"][0].rearrange("(k p) -> k p", p=P))
            rows(GO, 16, a["out_norm_g"][0].rearrange("(k p) -> k p", p=P))
            rows(PS, 4, a["pool_scale"][0].rearrange("(k p) -> k p", p=P))
            for j in range(3):
                rows(CW + 4 * j, 4, a["conv_w"][0, j].rearrange("(k p) -> k p", p=P))
            rows(QG, 1, a["q_norm_g"])
            rows(KG, 1, a["k_norm_g"])
            for j in range(2):
                rows(P + j * FT, FT, a["ffn_conv_w"][0, j].rearrange("(k p) -> k p", p=P))
            rows(2 * P, FT, a["ffn_conv_w"][0, 2].rearrange("(k p) -> k p", p=P))
            rows(2 * P + FT, FT, a["ffn_conv_b"][0].rearrange("(k p) -> k p", p=P))
            sp.dma_start(bf[:, :], a["b_f"].rearrange("l h -> h l"),
                         allow_slow_non_contiguous=True).then_inc(small_loaded, 16)
            sp.dma_start(ptr[:, :], a["page_table"].rearrange("(o b) g -> o (b g)", o=1)).then_inc(small_loaded, 16)
            sp.dma_start(pti[:, :], a["page_table"].rearrange("(c b) g -> (b g) c", c=2),
                         allow_slow_non_contiguous=True).then_inc(small_loaded, 16)
            sp.wait_ge(x_full, 1)
            sp.dma_start(xr[:, 3, :], xp[3]).then_inc(x_loaded[3], 16)
            sp.dma_start(fraw[:, :, :], w_in_v[:, :, T_F * P:T_F * P + HEADS]).then_inc(f_loaded, 16)

            def load_raw(n, slot, source, col, k=KT, width=2 * P):
                sp.wait_ge(w_lo, n * 4 - 4)
                sp.dma_start(wraw[:, slot, :].rearrange("p (k n) -> p k n", k=k),
                             source[:, :, bass.ds(col, width)]).then_inc(w_loaded[slot], 16)

            for n in range(2):
                sp.dma_start(wraw[:, n, :].rearrange("p (k n) -> p k n", k=KT),
                             w_in_v[:, :, (T_Q + 2 * n) * P:(T_Q + 2 * n + 2) * P]).then_inc(w_loaded[n], 16)
            for n in range(2, 4):
                load_raw(n, n % 2, w_in_v, (T_Q + 2 * n) * P)
            for n in range(4, 6):
                load_raw(n, n % 2, w_in_v, 2 * (n - R_IN) * P)

            def page(ring, pages, loads, used, r, p):
                g = sp.value_load(ptr[0:1, bass.ds(r * PAGES + p, 1)], min_val=0, max_val=N_POOL - 1)
                sp.wait_ge(used, r * PAGES + (p + 1))
                sp.dma_start(ring[:, p % RING, :],
                             pages[bass.ds(g, 1), :, :].rearrange("a p n -> (a p) n")).then_inc(loads[p % RING], 16)

            sp.wait_ge(small_loaded, 48)
            sp.wait_ge(n_lo, KT)
            sp.wait_ge(x_spilled, 16)

            def round_loads(r, weights, keys, values):
                kp, vp = 0, 0
                for c in range(8):
                    if weights and c % 4 == 1:
                        weights(c // 4)
                    for n in range(max(K_PER_CHUNK[c], V_PER_CHUNK[c])):
                        if keys and n < K_PER_CHUNK[c]:
                            page(kring, k_pages, k_loaded, k_used, r, kp)
                            kp += 1
                        if values and n < V_PER_CHUNK[c]:
                            page(vring, v_pages, v_loaded, v_used, r - 1, vp)
                            vp += 1

            def next_in(r):
                def load(m):
                    s = r + 1
                    load_raw(r * 2 + (R_IN + 2 + m), m, w_in_v, s * (4 * P) + (s // 4) * (8 * P) + 2 * m * P)
                return load

            def first_o(m):
                load_raw(R_O + m, m, w_o_v, 2 * m * P)

            round_loads(0, next_in(0), True, False)
            with sp.Fori(1, DEC - 1) as r:
                round_loads(r, next_in(r), True, True)
            round_loads(DEC - 1, first_o, True, True)
            for p in range(RING):
                page(vring, v_pages, v_loaded, v_used, DEC - 1, p)
            sp.wait_ge(w_used, 4 * R_O + 4)
            for b in range(2):
                sp.wait_ge(tile_spilled[b], 16 * 20)
            sp.dma_start(strow[:, :], a["state_pool"].rearrange("l b t c -> (l b t) c")).then_inc(p_states, 16)
            sp.dma_start(cstrow[:, :], a["state_conv"].rearrange("l b t c -> (l b t) c")).then_inc(p_states, 16)
            sp.dma_start(poolw, a["pool_w"].rearrange("l g c d -> c (l g) d")).then_inc(p_states, 16)
            sp.dma_start(ub[:, :, 16:528], scr[T_U:T_U + 4].rearrange("g p t -> p g t")).then_inc(p_loaded, 16)
            mixed = scr[T_B:T_B + 12].rearrange("(c g) p t -> g p c t", c=3)
            for p in range(RING, PAGES):
                page(vring, v_pages, v_loaded, v_used, DEC - 1, p)
                if p % RING == 3 and p // RING <= CONV_T:
                    j = p // RING - 1
                    sp.dma_start(c3[:, j], mixed[j]).then_inc(v_in[j], 16)

            src = scr[T_Q:T_Q + 24].rearrange("(c h) p t -> h p c t", c=3)

            def load_head(h, b):
                sp.dma_start(qkv[b], src[bass.ds(h, 1)].rearrange("a p c t -> (a p) c t")).then_inc(h_loaded[0], 16)
                sp.dma_start(cb[b], scrc[bass.ds(h, 1), :].broadcast_to([P, SEQ])).then_inc(h_loaded[1], 16)

            def store_head(h, b):
                for n, (name, row) in enumerate((("v_prompt", vrow[b]), ("k_prompt", krow[b]))):
                    sp.wait_ge(h_rowsC, h * 2 + (n + 1))
                    dst = o[name].rearrange("l b (j p) h d -> p (l b j) h d", p=P)
                    sp.dma_start(dst[:, :, bass.ds(h, 1), :].rearrange("p j a d -> p (j a) d"),
                                 row.rearrange("p (j d) -> p j d", j=4)).then_inc(h_stored[n], 16)

            sp.wait_ge(p_y, 2 * POOL_G)
            sp.wait_ge(r_full, 2)
            load_head(0, 0)
            sp.wait_ge(v_done, CONV_T)
            for n in range(2):
                sp.wait_ge(h_loaded[n], 16)
            load_head(1, 1)
            sp.sem_inc(h_rowfree, 2)
            store_head(0, 0)

            def head_step(h, b, last):
                for n in range(2):
                    sp.wait_ge(h_stored[n], h * 16 + 16)
                sp.sem_inc(h_rowfree, 1)
                if not last:
                    store_head(h + 1, 1 - b)
                if not isinstance(h, int):
                    sp.wait_ge(h_free, h + 1)
                    load_head(h + 2, b)

            attention(sp, head_step)
            sp.wait_ge(h_done, HEADS + 1)
            sp.wait_ge(r_stored, 96)
            sp.dma_start(strows, a["state_ffn"].rearrange("l b j (t n) -> t (l b j) n", n=P)).then_inc(g_states, 16)

            def o_body(i, weights):
                sp.wait_ge(x2_ready, i * 4 + 1)
                sp.dma_start(xres, scrx.rearrange("(i m) p t -> i p m t", m=4)[bass.ds(i, 1)]
                             .rearrange("a p m t -> (a p) m t")).then_inc(res_loaded, 16)
                for m in range(2):
                    weights(i, m)

            with sp.Fori(0, 3) as i:
                o_body(i, lambda i, m: load_raw(i * 2 + (R_O + 2 + m), m, w_o_v, i * (4 * P) + (2 + m) * 2 * P))
            o_body(3, lambda i, m: load_raw(R_F + m, m, w_up_v, m * D_FF))
            def down(i, n, slot, m):
                sp.wait_ge(w_lo, n * 4 - 4)
                rows_ = w_down_v[:, bass.ds(i * FG, FG), 1024 * m:1024 * (m + 1)]
                sp.dma_start(wraw[:, slot, :].rearrange("p (k n) -> p k n", k=FG), rows_).then_inc(w_loaded[slot], 16)

            def ffn_body(i, more):
                n = i * 6 + R_F
                load_raw(n + 2, 0, w_up_v, i * (FG * P) + 2 * P)
                load_raw(n + 3, 1, w_up_v, i * (FG * P) + (D_FF + 2 * P))
                if more:
                    load_raw(n + 4, 0, w_up_v, i * (FG * P) + FG * P)
                    down(i, n + 5, 1, 0)
                    down(i, n + 6, 0, 1)
                    load_raw(n + 7, 1, w_up_v, i * (FG * P) + (FG * P + D_FF))
                else:
                    down(i, n + 4, 0, 0)
                    down(i, n + 5, 1, 1)

            with sp.Fori(0, GROUPS - 1) as i:
                ffn_body(i, True)
            ffn_body(GROUPS - 1, False)
            yp = o["y_prompt"].rearrange("b (j p) d -> (b j) p d", p=P)
            for j in range(4):
                sp.wait_ge(z_rows, 4 * (j + 1))
                sp.dma_start(yp[j], orow[:, j % 2, :]).then_inc(z_stored[j % 2], 16)
            sp.wait_ge(z_rows, 20)
            sp.dma_start(o["y_sample"].rearrange("b t d -> (b t) d"), orow[0:DEC, 0, :]).then_inc(z_stored[0], 16)
            sp.wait_ge(z_stored[0], 48)
            sp.wait_ge(z_stored[1], 32)

        norm_groups = [(0, KT, G1, D_MODEL), (0, 4, GO, 512), (4, 8, GO + 4, 512), (8, 16, GO + 8, 1024),
                       (0, KT, G2, D_MODEL)]
        norm_first = [0, 16, 20, 24, 32]

        @block.tensor
        def _(pe):
            def mm(out, lhsT, rhs, start=True, stop=True):
                return pe.matmul(out, lhsT, rhs, start=start, stop=stop)

            def tr(out, in_, n):
                return pe.transpose(out, in_, ident[0:n, 0:n])

            pe.sem_inc(w_used, 4)
            pe.sem_inc(v_used, PRIME)
            pe.wait_ge(const_ready, N_CONST)
            pe.wait_ge(prow_loaded, 13 * 16)
            pv = stg[:, :, :].rearrange("p a b -> p (a b)")
            tr(ps[:, 7, 0:66], pv[0:66, 0:P], 66)
            tr(ps[:, 7, 66:154], pv[0:88, P:2 * P], 88)
            tr(ps[:, 7, 154:242], pv[0:88, 2 * P:3 * P], 88).then_inc(par_full, 1)
            pe.wait_ge(xs_loaded, 16)
            for k in range(KT):
                last = tr(ps[:, 6, k * DEC:(k + 1) * DEC], xr[0:DEC, 3, k * P:(k + 1) * P], DEC)
            last.then_inc(x_full, 1)
            for i in range(16):
                j, g = divmod(i, 4)
                if g == 0:
                    pe.wait_ge(x_loaded[j], 16)
                if i >= 4:
                    pe.wait_ge(*((x_moved_act, 1 + (i - 4) // 2 + 1) if i % 2 == 0 else (x_moved_dve, (i - 4) // 2 + 1)))
                for k in range(4):
                    last = tr(ps[:, i % 4, k * P:(k + 1) * P], xr[:, j, (4 * g + k) * P:(4 * g + k + 1) * P], P)
                last.then_inc(x_full, 1)

            def norm(group):
                lo, hi, _, _ = norm_groups[group]
                if group:
                    pe.wait_ge(n_rb, group)
                for t in range(lo, hi):
                    n = norm_first[group] + t - lo
                    pe.wait_ge(n_sq, n + 1)
                    for c in range(2):
                        last = mm(ps[:, 4 + c, 0:HALF], ones[:, :], stg[:, n % 2, c * HALF:(c + 1) * HALF],
                                  t == lo, t == hi - 1)
                    last.then_inc(n_sum, 1)

            norm(0)

            pe.wait_ge(f_loaded, 16)
            for k in range(KT):
                pe.wait_ge(n_lo, k + 1)
                for x in (xh, xl):
                    for c in range(2):
                        last = mm(ps[0:HEADS, 4 + c, 0:HALF], fraw[:, k, :],
                                  x[:, k, c * HALF:(c + 1) * HALF].bitcast(F32),
                                  k == 0 and x is xh, k == KT - 1 and x is xl)
            last.then_inc(f_full, 1)

            def chunk(g, c, t, u, half, normed=None):
                if half == 0:
                    pe.wait_ge(acc_free[u % 2], t)
                pe.wait_ge(w_lo, g + (c + 1))
                s = c % 4
                for k in range(8):
                    kt = 8 * half + k
                    if normed is not None and u == 0:
                        pe.wait_ge(n_lo, normed + kt + 1)
                    block_h = wh[:, s, k * P:(k + 1) * P]
                    block_l = wl[:, s, k * P:(k + 1) * P]
                    for w, x in ((block_h, xh), (block_h, xl), (block_l, xh)):
                        for b in range(2):
                            last = mm(ps[:, 2 * (u % 2) + b, 0:HALF], w, x[:, kt, b * HALF:(b + 1) * HALF],
                                      kt == 0 and w is block_h and x is xh, kt == KT - 1 and w is block_l)
                last.then_inc(w_used, 1)

            def tile(g, t0, u):
                for half in range(2):
                    chunk(g, 2 * u + half, t0 // 2 + (u // 2 + 1), u, half)

            for u in range(4):
                tile(0, 0, u)
            pe.wait_ge(f_cum, 1)
            for j in range(4):
                tr(ps[:, 4, j * HEADS:(j + 1) * HEADS], lgv[:, j * P:(j + 1) * P], HEADS)
                tr(ps[:, 4, 32 + j * HEADS:32 + (j + 1) * HEADS], junk[0:HEADS, j * P:(j + 1) * P], HEADS)
            tr(ps[0:DEC, 4, 64:72], lgv[:, SEQ:T], HEADS).then_inc(f_cols, 1)
            pe.wait_ge(f_kept, 3)
            pe.wait_ge(e_scan, 1)
            for c in range(2):
                mm(ps[:, 5, c * HEADS:(c + 1) * HEADS], tri[:, :], Pc[:, c, 1024 - HEADS:1024], True, False)
                last = mm(ps[:, 5, c * HEADS:(c + 1) * HEADS], sel[:, c * P:(c + 1) * P], lfS[:, :], False, True)
            last.then_inc(e_tail, 1)
            pe.wait_ge(e_bias, 1)
            for i in range(4):
                if i >= 2:
                    pe.wait_ge(e_kept, i - 1)
                for n in range(4):
                    c, h = divmod(4 * i + n, HEADS)
                    last = tr(ps[:, 4 + i % 2, n * P:(n + 1) * P], lfE[:, c, h, :], P)
                last.then_inc(e_full, 1)
            for u in range(4):
                tile(8, 4, u)
            pe.wait_ge(q_sq, 1)
            mm(ps[:, 6, 0:64], ones[:, :], sm[:, :, :].rearrange("p h b -> p (h b)")).then_inc(q_sum, 1)
            pe.wait_ge(q_n, 1)
            for h in range(HEADS):
                last = tr(ps[0:DEC, 6 + h // 4, (h % 4) * P:(h % 4 + 1) * P], qS[:, h, :], P)
            last.then_inc(q_tr, 1)

            def broadcast_q(s, half):
                if half == 0:
                    pe.wait_ge(q_mask, s + 1)
                if half or not (isinstance(s, int) and s == 0):
                    pe.wait_ge(q_cur, 2 * s + half)
                mm(ps[:, 6, :], ones[0:DEC, :], qmask[:, half * 512:(half + 1) * 512]).then_inc(q_bc, 1)

            def value_page(r, p):
                pe.wait_ge(v_loaded[p % RING], r * (16 * PAGES // RING) + 16 * (p // RING + 1))
                for c in range(2):
                    last = mm(ps[0:HEADS, 4 + c, :], pr[:, p, :], vring[:, p % RING, c * 512:(c + 1) * 512],
                              p == 0, p == PAGES - 1)
                last.then_inc(v_used, 1)

            def pool_conv(c):
                if c == 2:
                    for b in range(2):
                        pe.wait_ge(acc_free[b], T_O // 2 + 1)
                    pe.wait_ge(p_states, 48)
                    for g in range(POOL_G):
                        tr(ps[:, 0, g * 120:(g + 1) * 120], strow[:, g * P:(g + 1) * P], 120)
                        last = tr(ps[:, 1, g * 16:(g + 1) * 16], cstrow[:, g * P:(g + 1) * P], 16)
                    last.then_inc(p_tr, 1)
                if 3 <= c < 7:
                    g = c - 3
                    pe.wait_ge(p_pooled, g + 1)
                    if g:
                        pe.wait_ge(p_y, 2 * g)
                    mm(ps[:, 2, :], poolw[:, g, :], pooled[:, 0:SEQ])
                    mm(ps[:, 3, 0:DEC], poolw[:, g, :], pooled[:, SEQ:T]).then_inc(p_mm, 1)
                if c == 7:
                    pe.wait_ge(p_stT, 2)
                    for g in range(POOL_G):
                        last = tr(ps[0:POOL_STATE, 0, g * P:(g + 1) * P], ub[:, g, 528 - POOL_STATE:528], P)
                    last.then_inc(r_full, 1)
                    for g in range(POOL_G):
                        last = tr(ps[0:DEC, 1, g * P:(g + 1) * P], projS[:, T_U + g, :], P)
                    last.then_inc(r_full, 1)
                    pe.wait_ge(p_y, 2 * POOL_G)
                    pe.wait_ge(v_done, CONV_T)
                    for j in range(CONV_T):
                        last = tr(ps[0:2, 2, j * P:(j + 1) * P], zl4[:, 2 * j:2 * j + 2], P)
                    last.then_inc(r_full, 1)
                    for j in range(CONV_T):
                        last = tr(ps[0:DEC, 3, j * P:(j + 1) * P], zs4[:, DEC * j:DEC * (j + 1)], P)
                    last.then_inc(r_full, 1)

            def round_(r, keys, more, values):
                p = 0
                for c in range(8):
                    if not keys:
                        pool_conv(c)
                    if c == 7:
                        if more:
                            broadcast_q(r + 1, 0)
                        if keys:
                            pe.wait_ge(c_mx, r + 1)
                            if values:
                                pe.wait_ge(c_dk, r)
                            tr(ps[0:HEADS, 7, 0:P], mx8[:, :], P).then_inc(c_mT, 1)
                    if keys:
                        u, half = divmod(c, 2)
                        chunk(r * 8 + 4 * R_IN, c, r * 2 + (T_IN // 2 + u // 2 + 1), u, half)
                    if values and c == 0:
                        pe.wait_ge(c_p, r)
                        pe.wait_ge(o_rows, r)
                    if values and c == 1:
                        pe.wait_ge(c_ps, r)
                        pe.wait_ge(o_kept, r)
                        mm(ps[:, 7, 136:144], ones[:, :], ps8[:, :]).then_inc(c_den, 1)
                    for _ in range(V_PER_CHUNK[c] if values else 0):
                        value_page(r - 1, p)
                        p += 1
                if more:
                    broadcast_q(r + 1, 1)
                if keys:
                    pe.wait_ge(c_dg, r + 1)
                if values:
                    pe.wait_ge(o_rows, r + 1)
                    pe.wait_ge(c_dk, r)
                    for h in range(HEADS):
                        last = mm(ps[:, 7, 144 + h:145 + h], osb[:, h * P:(h + 1) * P], ident[0:HEADS, h:h + 1])
                    last.then_inc(o_cols, 1)
                if keys:
                    mm(ps[:, 7, P:P + HEADS], ones[0:HEADS, :], diag[:, :]).then_inc(c_mb, 1)

            broadcast_q(0, 0)
            broadcast_q(0, 1)
            round_(0, True, True, False)
            with pe.Fori(1, DEC - 1) as r:
                round_(r, True, True, True)
            round_(DEC - 1, True, False, True)
            round_(DEC, False, False, True)

            pe.wait_ge(o_kept, DEC + 1)
            pe.wait_ge(s_sq, 1)
            mm(ps[:, 6, 0:64], ones[:, :], sm[:, :, :].rearrange("p h b -> p (h b)")).then_inc(s_sum, 1)

            def sum_squares(h, b):
                pe.wait_ge(h_sq, h + 1)
                for c in range(2):
                    last = mm(ps[:, c, :], ones[:, :], sqs[b][:, c, :])
                last.then_inc(h_sum, 1)

            def rows_of(h, b, n):
                if n:
                    pe.wait_ge(h_qk, h + 1)
                for j in range(4):
                    src = (qk[b][:, 1], qkv[b][:, 2])[1 - n]
                    last = tr(ps[:, 3 - n, j * P:(j + 1) * P], src[:, j * P:(j + 1) * P], P)
                last.then_inc(h_rowsF, 1)

            pe.wait_ge(r_copied, 4)
            sum_squares(0, 0)
            pe.wait_ge(s_pd, 1)
            mm(ps[:, 6, 64:128], ones[:, :], tmp5[0]).then_inc(s_sc, 1)
            for h in range(HEADS):
                last = tr(ps[0:DEC, 2 + h // 4, (h % 4) * P:(h % 4 + 1) * P], kSn[:, h, :], P)
            last.then_inc(r_full, 1)
            for h in range(HEADS):
                last = tr(ps[0:DEC, 4 + h // 4, (h % 4) * P:(h % 4 + 1) * P], projS[:, T_V + h, :], P)
            last.then_inc(r_full, 1)
            pe.wait_ge(r_copied, 6)
            rows_of(0, 0, 0)
            rows_of(0, 0, 1)
            pe.wait_ge(s_done, 1)

            def head_step(h, b, last_head):
                def scores(i):
                    n = (i + 1) * P
                    if i >= 2:
                        pe.wait_ge(h_t, h * 4 + (i - 1))
                    mm(ps[:, 4 + i % 2, 0:n], qk[b][:, 0, i * P:(i + 1) * P], qk[b][:, 1, 0:n]).then_inc(h_S, 1)

                scores(0)
                scores(1)
                if not last_head:
                    pe.wait_ge(h_done, h + 1)
                    sum_squares(h + 1, 1 - b)
                scores(2)
                transposed_probs(pe, tr, h, 0)
                scores(3)
                transposed_probs(pe, tr, h, 1)
                if not last_head:
                    pe.wait_ge(h_rowsC, h * 2 + 2)
                    rows_of(h + 1, 1 - b, 0)
                transposed_probs(pe, tr, h, 2)
                if not last_head:
                    rows_of(h + 1, 1 - b, 1)
                transposed_probs(pe, tr, h, 3)
                pe.wait_ge(h_pC, h * 4 + 4)
                pe.wait_ge(h_rowsC, h * 2 + 2)
                if not last_head:
                    pe.wait_ge(h_ln, h + 2)
                for k in range(4):
                    last = mm(ps[:, 0, k * P:SEQ], vrow[b][:, k * P:(k + 1) * P], pT[:, k, k * P:SEQ], k == 0, k == 3)
                last.then_inc(h_O, 1)

            attention(pe, head_step)
            pe.wait_ge(h_done, HEADS + 1)

            for group in (1, 2, 3):
                norm(group)
            with pe.Fori(0, 4) as i:
                for u in range(4):
                    for half in range(2):
                        chunk(i * 8 + 4 * R_O, 2 * u + half, i * 2 + (T_O // 2 + u // 2 + 1), u, half, 16)
            pe.wait_ge(g_states, 16)
            pe.wait_ge(n_rb, 4)
            for s in range(2 * DEC):
                last = tr(ps[:, 6 + s // 11, (s % 11) * FT:(s % 11 + 1) * FT], strows[:, s, :], FT)
            last.then_inc(g_tr, 1)
            norm(4)

            def up(i, c0, us):
                for u in us:
                    for half in range(2):
                        chunk(i * 24 + 4 * R_F, c0 + 2 * u + half, i * 12 + (T_FF // 2 + u // 2 + 1), u, half,
                              32 if isinstance(i, int) and i == 0 else None)

            def down(i, c0, t0):
                g = i * 24 + 4 * R_F
                for c in range(8):
                    pe.wait_ge(w_lo, g + (c0 + c + 1))
                    if c == 0:
                        pe.wait_ge(g_lo, i * 4 + 4)
                    for m in range(2):
                        pe.wait_ge(acc_free[m], i * 12 + (t0 + c + 1))
                        for k in range(FG):
                            at = k * 256 + m * P
                            block_h = wh[:, c % 4, at:at + P]
                            block_l = wl[:, c % 4, at:at + P]
                            for w, x in ((block_h, hh), (block_h, hl), (block_l, hh)):
                                for b in range(2):
                                    last = mm(ps[:, 2 * m + b, 0:HALF], w, x[:, k, b * HALF:(b + 1) * HALF],
                                              k == 0 and w is block_h and x is hh, k == FG - 1 and w is block_l)
                        last.then_inc(g_half if m == 0 else w_used, 1)

            up(0, 0, (0, 1))
            with pe.Fori(0, GROUPS - 1) as i:
                up(i, 0, range(2, 10))
                down(i, 20, T_FF // 2 + 5)
            up(GROUPS - 1, 0, range(2, 8))
            down(GROUPS - 1, 16, T_FF // 2 + 4)

            pe.wait_ge(g_kept, FT)
            for s in range(DEC + 2):
                last = tr(ps[0:FT, 4 + s // 4, (s % 4) * P:(s % 4 + 1) * P], ast[:, s, :], P)
            last.then_inc(z_ffn, 1)
            pe.wait_ge(g_y, 1)
            for i in range(20):
                j, q = divmod(i, 4)
                if i >= 4:
                    pe.wait_ge(z_rows, i - 3)
                n = P if j < 4 else DEC
                for k in range(4):
                    last = tr(ps[0:n, i % 4, k * P:(k + 1) * P], xT[:, 4 * q + k, j * P:j * P + n], P)
                last.then_inc(z_full, 1)


        @block.scalar
        def _(act):
            seq = Count(act_seq)

            def copy(out, in_):
                return act.activation(out, in_, ACT.Copy)

            for b in range(2):
                act.sem_inc(acc_free[b], 1)
            act.sem_inc(o_rows, 1)
            act.sem_inc(g_hi, 2)
            act.wait_ge(par_full, 1)
            copy(par[:, :], ps[:, 7, 0:242]).then_inc(par_ready, 1)
            act.wait_ge(x_full, 1)
            copy(xT[:, :, SEQ:T], ps[:, 6, 0:KT * DEC].rearrange("p (k b) -> p k b", k=KT)).then_inc(x_moved_act, 1)
            for i in range(0, 16, 2):
                j, g = divmod(i, 4)
                act.wait_ge(x_full, i + 2)
                copy(xT[:, 4 * g:4 * g + 4, j * P:(j + 1) * P],
                     ps[:, i % 4, :].rearrange("p (k t) -> p k t", k=4)).then_inc(x_moved_act, 1)

            def norm(group):
                lo, hi, _, width = norm_groups[group]
                n0 = norm_first[group]
                for t in range(lo, hi):
                    n = n0 + t - lo
                    if t - lo >= 2:
                        act.wait_ge(n_sum, n - 1)
                    elif group:
                        act.wait_ge(n_lo, n0)
                    if group == 4:
                        act.wait_ge(x2_ready, t + 2)
                    act.activation(stg[:, n % 2, :], xT[:, t, :], ACT.Square).then_inc(n_sq, 1)
                act.wait_ge(n_sum, n0 + hi - lo)
                step(act, seq, act.activation(two(rb), ps[:, 4:6, 0:HALF], ACT.Ln, bias=epsc[:, :], scale=1.0 / width))
                act.activation(rb, rb, ACT.Exp, scale=-0.5).then_inc(n_rb, 1)
                for t in range(lo, hi):
                    n = n0 + t - lo
                    act.wait_ge(n_tmp, n + 1)
                    copy(xh[:, t, :], stg[:, n % 2, :]).then_inc(n_hi, 1)

            act.wait_ge(x_moved_dve, 8)
            act.wait_ge(x_moved_act, 9)
            norm(0)

            def raw_chunk(c, down):
                raw, q = wraw[:, (c // 4) % 2, :], c % 4
                if down:
                    return raw.rearrange("p (k n) -> p k n", k=FG)[:, :, q * 256:(q + 1) * 256]
                m, half = divmod(q, 2)
                return raw.rearrange("p (k n) -> p k n", k=KT)[:, half * 8:half * 8 + 8, m * P:(m + 1) * P]

            def blocks(buf, c, down):
                return buf[:, c % 4, :].rearrange("p (k n) -> p k n", k=FG if down else 8)

            def head(g, c, down=False):
                if c % 4 == 0:
                    act.wait_ge(w_loaded[(c // 4) % 2], g * 2 + 16 * (c // 8 + 1))
                act.wait_ge(w_used, g + (c + 1))
                copy(blocks(wh, c, down), raw_chunk(c, down)).then_inc(w_hi, 1)

            for c in range(4):
                head(0, c)

            def move_tile(t, u, dst, used):
                s = u % 2
                act.wait_ge(w_used, used)
                if not (isinstance(t, int) and t + u < 2):
                    act.wait_ge(tile_spilled[s], t * 8 + 16 * (u // 2))
                    act.wait_ge(tile_kept, t + (u - 1))
                act.activation(two(stg[:, s, :]), ps[:, 2 * s:2 * s + 2, 0:HALF], ACT.Copy).then_inc(acc_free[s], 1)
                act.wait_ge(acc_free[s], t // 2 + (u // 2 + 2))
                copy(projS[:, bass.ds(dst, 1), :], stg[:, s:s + 1, SEQ:T]).then_inc(tile_kept, 1)
                act.dma_start(scr[bass.ds(dst, 1)].rearrange("a p t -> (a p) t"), stg[:, s, 0:SEQ]).then_inc(tile_spilled[s], 16)

            act.wait_ge(f_nz, 1)
            step(act, seq, act.activation(fn, fn, ACT.Exp))
            act.activation(fn, fn, ACT.Ln, bias=1.0).then_inc(f_soft, 1)
            for i in range(2):
                for u in range(4):
                    for c in (2 * u, 2 * u + 1):
                        head(8 * i, 4 + c)
                    move_tile(4 * i, u, T_Q + 4 * i + u, 4 + 8 * i + 2 * u + 2)
                if i == 0:
                    act.wait_ge(f_cols, 1)
                    copy(lfT[:, :, :], ps[:, 4, 0:32].rearrange("p (j h) -> p j h", j=4)).then_inc(f_kept, 1)
                    copy(cqT[:, :, :], ps[:, 4, 32:64].rearrange("p (j h) -> p j h", j=4)).then_inc(f_kept, 1)
                    copy(lfS[:, :], ps[0:DEC, 4, 64:72]).then_inc(f_kept, 1)
                    for n in range(4):
                        act.wait_ge(e_full, n + 1)
                        c, h = divmod(4 * n, HEADS)
                        copy(Eb[:, c * P:(c + 1) * P, h:h + 4].rearrange("p g h -> p h g"),
                             ps[:, 4 + n % 2, :].rearrange("p (h g) -> p h g", h=4)).then_inc(e_kept, 1)

            def rstd64(summed, done):
                act.wait_ge(summed, 1)
                v = sm[:, :, :].rearrange("p h b -> p (h b)")
                step(act, seq, act.activation(v, ps[:, 6, 0:64], ACT.Ln, bias=epsc[:, :], scale=1.0 / HD))
                act.activation(v, v, ACT.Exp, scale=-0.5).then_inc(done, 1)

            rstd64(q_sum, q_rs)
            act.wait_ge(q_tr, 1)
            copy(qrows.rearrange("p (c n) -> p c n", c=2), ps[0:DEC, 6:8, :]).then_inc(q_rows, 1)

            def take_q(s, half):
                act.wait_ge(q_bc, s * 2 + (half + 1))
                if half == 0:
                    act.wait_ge(k_used, s * PAGES + PRIME)
                copy(qcur[:, half * 512:(half + 1) * 512], ps[:, 6, :]).then_inc(q_cur, 1)

            def round_(r, keys, more, values):
                g = r * 8 + 4 * R_IN
                for u in range(4):
                    for c in (2 * u, 2 * u + 1):
                        if c == 7:
                            if more:
                                take_q(r + 1, 0)
                            if values:
                                act.wait_ge(v_used, r * PAGES + PRIME)
                                copy(osb.rearrange("p (c n) -> p c n", c=2), ps[0:HEADS, 4:6, :]).then_inc(o_rows, 1)
                        if keys:
                            head(g, 4 + c)
                    if keys:
                        move_tile(r * 4 + T_IN, u, r * 4 + (r // 4) * 8 + u, g + (4 + 2 * u + 2))
                if more:
                    take_q(r + 1, 1)
                if keys:
                    act.wait_ge(c_sub, r + 1)
                    act.activation(pr[:, :, :], shifts, ACT.Exp).then_inc(c_p, 1)

            take_q(0, 0)
            take_q(0, 1)
            round_(0, True, True, False)
            with act.Fori(1, DEC - 1) as r:
                round_(r, True, True, True)
            round_(DEC - 1, True, False, True)
            act.wait_ge(p_tr, 1)
            copy(stT, ps[:, 0, 0:480].rearrange("p (g b) -> p g b", g=POOL_G)).then_inc(p_stT, 1)
            copy(cstT, ps[:, 1, 0:64].rearrange("p (g b) -> p g b", g=CONV_T)).then_inc(p_stT, 1)
            for g in range(POOL_G):
                act.wait_ge(p_mm, g + 1)
                act.activation(xT[:, g, 0:SEQ], ps[:, 2, :], ACT.Copy, scale=par[:, PS + g:PS + g + 1]).then_inc(p_y, 1)
                act.activation(xT[:, g, SEQ:T], ps[:, 3, 0:DEC], ACT.Copy,
                               scale=par[:, PS + g:PS + g + 1]).then_inc(p_y, 1)
            for n, (out, in_) in enumerate(((rows1[0:POOL_STATE, 0:512], ps[0:POOL_STATE, 0, :]),
                                            (rows1[0:DEC, 512:1024], ps[0:DEC, 1, :]),
                                            (rows2[0:2, 0:512], ps[0:2, 2, :]),
                                            (rows2[0:DEC, 512:1024], ps[0:DEC, 3, :]))):
                act.wait_ge(r_full, 1 + n)
                copy(out, in_).then_inc(r_copied, 1)
            round_(DEC, False, False, True)

            def head_rstd(h, b):
                act.wait_ge(h_sum, h + 1)
                act.activation(sqs[b], ps[:, 0:2, :], ACT.Ln, bias=epsc[:, :], scale=1.0 / HD).then_inc(h_ln, 1)
                act.wait_ge(h_ln, h + 1)
                act.activation(sqs[b], sqs[b], ACT.Exp, scale=-0.5).then_inc(h_rs, 1)

            def head_rows(h, b, n):
                act.wait_ge(h_rowsF, h * 2 + (n + 1))
                if n == 0:
                    act.wait_ge(h_rowfree, h + 1)
                copy((vrow, krow)[n][b], ps[:, 3 - n, :]).then_inc(h_rowsC, 1)

            rstd64(s_sum, s_rs)
            head_rstd(0, 0)
            act.wait_ge(s_e, 1)
            act.activation(tmp5[2], tmp5[2], ACT.Exp).then_inc(s_x, 1)
            act.activation(tmp5[3], tmp5[3], ACT.Exp).then_inc(s_x, 1)
            act.wait_ge(r_full, 5)
            for b in range(2):
                act.wait_ge(tile_spilled[b], 16 * 20)
            copy(krs.rearrange("p (c n) -> p c n", c=2), ps[0:DEC, 2:4, :]).then_inc(r_copied, 1)
            act.wait_ge(r_full, 6)
            copy(vrs.rearrange("p (c n) -> p c n", c=2), ps[0:DEC, 4:6, :]).then_inc(r_copied, 1)
            head_rows(0, 0, 0)
            head_rows(0, 0, 1)

            act.sem_inc(h_done, 1)

            def head_step(h, b, last_head):
                def exps(i):
                    act.wait_ge(h_t, h * 4 + (i + 1))
                    act.activation(probs2[i], shifted[i], ACT.Exp, bias=nmax[:, i:i + 1],
                                   accum_out=rsum[:, i:i + 1]).then_inc(h_e, 1)

                exps(0)
                exps(1)
                if not last_head:
                    head_rstd(h + 1, 1 - b)
                copy_probs(act, copy, h, 0)
                exps(2)
                copy_probs(act, copy, h, 1)
                if not last_head:
                    head_rows(h + 1, 1 - b, 0)
                exps(3)
                copy_probs(act, copy, h, 2)
                if not last_head:
                    head_rows(h + 1, 1 - b, 1)
                copy_probs(act, copy, h, 3)
                act.wait_ge(h_O, h + 1)
                copy(xT[:, bass.ds(h + 8, 1), 0:SEQ], ps[:, 0:1, :]).then_inc(h_done, 1)

            attention(act, head_step)
            act.wait_ge(r_stored, 96)
            act.wait_ge(h_done, HEADS + 1)
            for n in range(2):
                act.wait_ge(h_stored[n], 16 * HEADS)

            for group in (1, 2, 3):
                norm(group)

            with act.Fori(0, 4) as i:
                for c in range(8):
                    head(i * 8 + 4 * R_O, 4 + c)
            act.wait_ge(g_tr, 1)
            copy(stfT[:, 0:11, :], ps[:, 6, 0:484].rearrange("p (s f) -> p s f", f=FT)).then_inc(g_stT, 1)
            copy(stfT[:, 11:16, :], ps[:, 7, 0:220].rearrange("p (s f) -> p s f", f=FT)).then_inc(g_stT, 1)
            norm(4)

            def ffn(i, us, first_down):
                g = i * 24 + 4 * R_F
                for u in us:
                    for c in (2 * u, 2 * u + 1):
                        head(g, 4 + c, down=first_down is not None and 4 + c >= first_down)
                    act.wait_ge(w_used, g + (4 + 2 * u + 2))
                    pair, gate, n = u // 4, (u // 2) % 2, u % 2
                    if not gate:
                        act.wait_ge(g_cv, i * 4 + (2 * pair + n + 1))
                        act.activation(abuf[:, n, 2:2 + T].rearrange("p (c t) -> p c t", c=2),
                                       ps[:, 2 * n:2 * n + 2, 0:HALF], ACT.Copy).then_inc(acc_free[n], 1)
                    else:
                        tile = 2 * pair + n
                        act.wait_ge(g_cv, i * 4 + (tile + 3))
                        act.activation(cv[:, n, :], cv[:, n, :], ACT.Silu, bias=fcur[:, 3, tile:tile + 1])\
                           .then_inc(g_silu, 1)
                        act.wait_ge(g_h, i * 4 + (tile + 1))
                        copy(hh[:, tile, :], cv[:, n, :]).then_inc(g_hi, 1)
                if first_down is not None:
                    for c in range(4):
                        head(g, first_down + 4 + c, down=True)
                    if first_down == 20:
                        for c in range(4):
                            head(g, 28 + c)

            ffn(0, (0, 1), None)
            with act.Fori(0, GROUPS - 1) as i:
                ffn(i, range(2, 10), 20)
            ffn(GROUPS - 1, range(2, 8), 16)
            for n, (lo, hi) in enumerate(((0, 4), (4, 8), (8, 10))):
                act.wait_ge(z_ffn, 1)
                copy(astrows[:, lo:hi, :], ps[0:FT, 4 + n, 0:(hi - lo) * P].rearrange("p (s n) -> p s n", n=P))\
                    .then_inc(z_act, 1)


        @block.vector
        def _(dve):
            seq = Count(dve_seq)

            def tt(out, in0, in1, op):
                return dve.tensor_tensor(out, in0, in1, op)

            def fma(out, in0, scalar, in1):
                return dve.scalar_tensor_tensor(out, in0, scalar, in1, ALU.mult, ALU.add)

            dve.sem_inc(k_used, PRIME)
            dve.sem_inc(x2_ready, 1)
            dve.sem_inc(o_kept, 1)
            dve.sem_inc(g_cv, 2)
            for i in range(1, 16, 2):
                j, g = divmod(i, 4)
                dve.wait_ge(x_full, i + 2)
                dve.tensor_copy(xT[:, 4 * g:4 * g + 4, j * P:(j + 1) * P],
                                ps[:, i % 4, :].rearrange("p (k t) -> p k t", k=4)).then_inc(x_moved_dve, 1)

            def norm(group):
                lo, hi, gcol, _ = norm_groups[group]
                n0 = norm_first[group]
                dve.wait_ge(n_rb, group + 1)

                def rest(t):
                    n = n0 + t - lo
                    dve.wait_ge(n_hi, n + 1)
                    tt(xl[:, t, :], stg[:, n % 2, :], xh[:, t, :].bitcast(F32), ALU.subtract).then_inc(n_lo, 1)

                for t in range(lo, hi):
                    n = n0 + t - lo
                    if t - lo >= 2:
                        dve.wait_ge(n_lo, n - 1)
                    dve.scalar_tensor_tensor(stg[:, n % 2, :], xT[:, t, :], par[:, gcol + t - lo:gcol + t - lo + 1], rb,
                                             ALU.mult, ALU.mult).then_inc(n_tmp, 1)
                    if t > lo:
                        rest(t - 1)
                rest(hi - 1)

            dve.wait_ge(par_ready, 1)
            dve.tensor_scalar(qgs[:, :], par[:, QG:QG + 1], SCALE, None, ALU.mult)
            dve.wait_ge(x_moved_act, 9)
            dve.wait_ge(x_moved_dve, 8)
            norm(0)

            def raw_chunk(c, down):
                raw, q = wraw[:, (c // 4) % 2, :], c % 4
                if down:
                    return raw.rearrange("p (k n) -> p k n", k=FG)[:, :, q * 256:(q + 1) * 256]
                m, half = divmod(q, 2)
                return raw.rearrange("p (k n) -> p k n", k=KT)[:, half * 8:half * 8 + 8, m * P:(m + 1) * P]

            def blocks(buf, c, down):
                return buf[:, c % 4, :].rearrange("p (k n) -> p k n", k=FG if down else 8)

            def rest(g, c, down=False):
                dve.wait_ge(w_hi, g + (c + 1))
                tt(blocks(wl, c, down), raw_chunk(c, down), blocks(wh, c, down).bitcast(F32),
                   ALU.subtract).then_inc(w_lo, 1)

            for c in range(4):
                rest(0, c)

            dve.wait_ge(small_loaded, 48)
            dve.wait_ge(f_full, 1)
            step(dve, seq, dve.tensor_scalar(two(fz), ps[0:HEADS, 4:6, 0:HALF], bf[:, :], None, ALU.add))
            dve.scalar_tensor_tensor(fn, fz, -1.0, fz, ALU.mult, ALU.min).then_inc(f_nz, 1)
            dve.wait_ge(f_soft, 1)
            step(dve, seq, dve.scalar_tensor_tensor(lgv, fz, 0.0, fn, ALU.min, ALU.subtract))
            dve.tensor_tensor_scan(out=junk[0:HEADS, 0:SEQ], data0=lgv[:, 0:SEQ], data1=lgv[:, 0:SEQ], initial=0.0,
                                   op0=ALU.add, op1=ALU.bypass).then_inc(f_cum, 1)
            for i in range(2):
                for c in range(8):
                    rest(8 * i, 4 + c)
                if i == 0:
                    dve.wait_ge(e_loaded, 32)
                    lf4 = work[:, 0:2048].rearrange("p (c t h) -> p c t h", c=2, h=HEADS)
                    P4 = work[:, 2048:4096].rearrange("p (c t h) -> p c t h", c=2, h=HEADS)
                    for c in range(2):
                        for h in range(HEADS):
                            last = dve.tensor_tensor_scan(out=P4[:, c, :, h], data0=lf4[:, c, :, h],
                                                          data1=lf4[:, c, :, h], initial=0.0,
                                                          op0=ALU.add, op1=ALU.bypass)
                    last.then_inc(e_scan, 1)
                    dve.wait_ge(e_tail, 1)
                    step(dve, seq, dve.tensor_copy(tot[:, :, :], ps[:, 5, 0:16].rearrange("p (c h) -> p c h", c=2)))
                    for c in range(2):
                        for h in range(HEADS):
                            last = dve.tensor_scalar(lfE[:, c, h, :], P4[:, c, :, h], -1.0, tot[:, c, h:h + 1],
                                                     ALU.mult, ALU.add)
                    last.then_inc(e_bias, 1)
            dve.wait_ge(tile_kept, 8)
            tt(sm[:, :, :], projS[:, T_Q:T_Q + HEADS, :], projS[:, T_Q:T_Q + HEADS, :], ALU.mult).then_inc(q_sq, 1)
            dve.wait_ge(q_rs, 1)
            dve.scalar_tensor_tensor(qS[:, :, :], projS[:, T_Q:T_Q + HEADS, :], par[:, QG:QG + 1], sm[:, :, :],
                                     ALU.mult, ALU.mult).then_inc(q_n, 1)
            dve.wait_ge(q_rows, 1)
            dve.wait_ge(f_stored, 48)
            dve.wait_ge(e_kept, 4)

            def key_page(r, p):
                dve.wait_ge(k_loaded[p % RING], r * (16 * PAGES // RING) + 16 * (p // RING + 1))
                dve.wait_ge(k_used, r * PAGES + (p + PRIME))
                for h in range(HEADS):
                    last = dve.tensor_tensor_reduce(
                        out=junk[:, h * HD:(h + 1) * HD], in0=kring[:, p % RING, h * HD:(h + 1) * HD],
                        in1=qcur[:, h * HD:(h + 1) * HD], scale=SCALE, scalar=0.0, op0=ALU.mult, op1=ALU.add,
                        accum_out=S[:, p, h:h + 1])
                last.then_inc(k_used, 1)

            def pool_conv():
                dve.wait_ge(w_used, 4 * R_O + 4)
                dve.memset(ub[:, :, 0:16], 0.0)
                dve.memset(shA[:, 0:16], 0.0)
                step(dve, seq, dve.memset(shB[:, 0:16], 0.0))
                dve.wait_ge(p_loaded, 16)
                dve.wait_ge(p_stT, 2)
                n_mm = 0
                for g in range(POOL_G):
                    win = 2 << g
                    cur = ub[:, g, :]
                    for n in range(g + 1):
                        nxt = shA if n % 2 == 0 else shB
                        sh = 1 << n
                        step(dve, seq, tt(nxt[:, 16:528], cur[:, 16:528], cur[:, 16 - sh:528 - sh], ALU.add))
                        cur = nxt
                    if g:
                        dve.wait_ge(p_mm, g)
                    step(dve, seq, tt(pooled[:, 0:win], cur[:, 16:16 + win], rc[:, 0:win], ALU.mult))
                    step(dve, seq, tt(pooled[:, 0:win], pooled[:, 0:win], ub[:, g, 16:16 + win], ALU.subtract))
                    step(dve, seq, dve.scalar_tensor_tensor(pooled[:, win:SEQ], cur[:, 16 + win:528], 1.0 / win,
                                                            ub[:, g, 16 + win:528], ALU.mult, ALU.subtract))
                    old = stT[:, g, :].rearrange("p (b t) -> p b t", b=DEC)[:, :, POOL_STATE + 1 - win:POOL_STATE]
                    step(dve, seq, dve.tensor_reduce(pooled[:, SEQ:T], old, AX.X, ALU.add))
                    step(dve, seq, tt(pooled[:, SEQ:T], pooled[:, SEQ:T], projS[:, T_U + g, :], ALU.add))
                    dve.scalar_tensor_tensor(pooled[:, SEQ:T], pooled[:, SEQ:T], 1.0 / win, projS[:, T_U + g, :],
                                             ALU.mult, ALU.subtract).then_inc(p_pooled, 1)

                def tap(j, t):
                    return par[:, CW + 4 * j + t:CW + 4 * j + t + 1]

                step(dve, seq, dve.memset(cz[:, 0:2], 0.0))
                for t in range(CONV_T):
                    dve.wait_ge(v_in[t], 16)
                    cs = cstT[:, t, :].rearrange("p (b j) -> p b j", j=2)
                    zs = zs4[:, DEC * t:DEC * (t + 1)]
                    tt(zs, projS[:, T_C + t, :], projS[:, T_X + t, :], ALU.mult)
                    step(dve, seq, tt(cz[:, 2:514], c3[:, t, 1, :], c3[:, t, 2, :], ALU.mult))
                    dve.tensor_copy(zl4[:, 2 * t:2 * t + 2], cz[:, 512:514])
                    dve.tensor_scalar(ct[:, SEQ:T], cs[:, :, 0], tap(0, t), None, ALU.mult)
                    step(dve, seq, dve.tensor_scalar(ct[:, 0:SEQ], cz[:, 0:512], tap(0, t), None, ALU.mult))
                    fma(ct[:, SEQ:T], cs[:, :, 1], tap(1, t), ct[:, SEQ:T])
                    step(dve, seq, fma(ct[:, 0:SEQ], cz[:, 1:513], tap(1, t), ct[:, 0:SEQ]))
                    fma(ct[:, SEQ:T], zs, tap(2, t), ct[:, SEQ:T])
                    step(dve, seq, fma(ct[:, 0:SEQ], cz[:, 2:514], tap(2, t), ct[:, 0:SEQ]))
                    tt(xT[:, 4 + t, SEQ:T], ct[:, SEQ:T], projS[:, T_B + t, :], ALU.mult)
                    tt(xT[:, 4 + t, 0:SEQ], ct[:, 0:SEQ], c3[:, t, 0, :], ALU.mult).then_inc(v_done, 1)
                    dve.wait_ge(v_done, t + 1)

            def mask_q(s):
                if not (isinstance(s, int) and s == 0):
                    dve.wait_ge(q_bc, s * 2)
                dve.tensor_scalar(qmask, qrows, ident[0:DEC, bass.ds(s, 1)], None, ALU.mult).then_inc(q_mask, 1)

            def round_(r, keys, more, values):
                g = r * 8 + 4 * R_IN
                if values:
                    dve.wait_ge(c_p, r)
                    dve.tensor_reduce(ps8[:, :], pr[:, :, :].rearrange("p g h -> p h g"), AX.X, ALU.add).then_inc(c_ps, 1)
                if keys:
                    dve.wait_ge(q_cur, r * 2 + 2)
                p = 0
                for c in range(8):
                    if c == 5 and more:
                        mask_q(r + 1)
                    if c == 2 and values:
                        if not keys:
                            pool_conv()
                        dve.wait_ge(c_den, r)
                        dve.tensor_copy(denall[:, bass.ds(r - 1, 1), :], ps[:, 7:8, 136:144]).then_inc(c_dk, 1)
                    if c == 7 and keys:
                        dve.wait_ge(k_used, r * PAGES + (PAGES + PRIME))
                        if values:
                            dve.wait_ge(c_p, r)
                        tt(shifts, S[:, :, :], Eb[:, bass.ds(r * PAGES, PAGES), :], ALU.add).then_inc(c_se, 1)
                        dve.wait_ge(c_se, r + 1)
                        dve.tensor_reduce(mx8[:, :], shifts.rearrange("p g h -> p h g"), AX.X, ALU.max).then_inc(c_mx, 1)
                        dve.wait_ge(c_mT, r + 1)
                        dve.tensor_reduce(mx1[:, :], ps[0:HEADS, 7, 0:P], AX.X, ALU.max).then_inc(c_m1, 1)
                        dve.wait_ge(c_m1, r + 1)
                        dve.tensor_scalar(diag[:, :], ident[0:HEADS, 0:HEADS], mx1[:, :], None, ALU.mult).then_inc(c_dg, 1)
                    for _ in range(min(3, K_PER_CHUNK[c]) if keys else 0):
                        key_page(r, p)
                        p += 1
                    if keys:
                        rest(g, 4 + c)
                    for _ in range(K_PER_CHUNK[c] - 3 if keys else 0):
                        key_page(r, p)
                        p += 1
                if keys:
                    dve.wait_ge(c_mb, r + 1)
                    dve.tensor_copy(mxb[:, :], ps[:, 7, P:P + HEADS]).then_inc(c_mk, 1)
                if values:
                    dve.wait_ge(o_cols, r)
                    dve.tensor_copy(ocomb[:, bass.ds(r - 1, 1), :], ps[:, 7:8, 144:152]).then_inc(o_kept, 1)
                if keys:
                    dve.wait_ge(c_mk, r + 1)
                    tt(shifts, shifts, mxb[:, :].unsqueeze(1).broadcast_to([P, PAGES, HEADS]),
                       ALU.subtract).then_inc(c_sub, 1)
                    dve.tensor_copy(maxall[:, bass.ds(r, 1), :], mxb[:, :].unsqueeze(1))

            mask_q(0)
            round_(0, True, True, False)
            with dve.Fori(1, DEC - 1) as r:
                round_(r, True, True, True)
            round_(DEC - 1, True, False, True)
            round_(DEC, False, False, True)

            def squares(h, b):
                dve.wait_ge(h_loaded[0], h * 16 + 16)
                dve.wait_ge(h_loaded[1], h * 16 + 16)
                tt(sqs[b], qkv[b][:, 0:2, :], qkv[b][:, 0:2, :], ALU.mult).then_inc(h_sq, 1)
                dve.tensor_copy(cqh[:, b, :], cqT[:, :, bass.ds(h, 1)].rearrange("p j a -> p (j a)")).then_inc(h_cq, 1)

            def qk_norm(h, b):
                dve.wait_ge(h_rs, h + 1)
                for n, g in enumerate((qgs[:, :], par[:, KG:KG + 1])):
                    last = dve.scalar_tensor_tensor(qk[b][:, n, :], qkv[b][:, n, :], g, sqs[b][:, n, :],
                                                    ALU.mult, ALU.mult)
                last.then_inc(h_qk, 1)

            def decays(h, b):
                dve.wait_ge(h_cq, h + 1)
                for i in range(4):
                    last = dve.tensor_scalar(shifted[i], cb[b][:, 0:(i + 1) * P], -1.0, cqh[:, b, i:i + 1],
                                             ALU.mult, ALU.add)
                last.then_inc(h_bias, 1)
                dve.wait_ge(h_bias, h * 2 + 1)
                for i in range(4):
                    d = shifted[i][:, i * P:(i + 1) * P]
                    last = tt(d, d, cmask[:, :], ALU.add)
                last.then_inc(h_bias, 1)
                dve.wait_ge(h_bias, h * 2 + 2)
                dve.wait_ge(h_rowsF, h * 2 + 2)
                dve.sem_inc(h_free, 1)

            squares(0, 0)
            kv = projS[:, T_K:T_K + HEADS, :]
            dve.wait_ge(tile_kept, 40)
            tt(sm[:, :, :], kv, kv, ALU.mult).then_inc(s_sq, 1)
            dve.wait_ge(s_rs, 1)
            dve.scalar_tensor_tensor(kSn[:, :, :], kv, par[:, KG:KG + 1], sm[:, :, :], ALU.mult, ALU.mult).then_inc(s_kn, 1)
            dve.wait_ge(s_kn, 1)
            t3 = [t.rearrange("p (h b) -> p h b", h=HEADS) for t in tmp5]
            hb = [t[:, :, :].rearrange("p b h -> p h b") for t in (maxall, denall, ocomb)]
            tt(t3[0], qS[:, :, :], kSn[:, :, :], ALU.mult).then_inc(s_pd, 1)
            qk_norm(0, 0)
            dve.wait_ge(s_sc, 1)
            own = ps[:, 6, 64:128].rearrange("p (h b) -> p h b", h=HEADS)
            dve.wait_ge(c_dk, DEC)
            step(dve, seq, dve.tensor_scalar(t3[4], own, SCALE, None, ALU.mult))
            step(dve, seq, tt(t3[1], t3[4], hb[0], ALU.max))
            tt(t3[2], hb[0], t3[1], ALU.subtract)
            tt(t3[3], t3[4], t3[1], ALU.subtract).then_inc(s_e, 1)
            dve.wait_ge(s_x, 2)
            step(dve, seq, tt(t3[0], hb[1], t3[2], ALU.mult))
            step(dve, seq, tt(t3[0], t3[0], t3[3], ALU.add))
            step(dve, seq, dve.reciprocal(t3[4], t3[0]))
            step(dve, seq, tt(t3[1], hb[2], t3[2], ALU.mult))
            step(dve, seq, tt(t3[3], t3[3], projS[:, T_V:T_V + HEADS, :], ALU.mult))
            step(dve, seq, tt(t3[1], t3[1], t3[3], ALU.add))
            tt(xT[:, 8:16, SEQ:T], t3[1], t3[4], ALU.mult).then_inc(s_done, 1)
            decays(0, 0)

            def head_step(h, b, last_head):
                def scores(i):
                    dve.wait_ge(h_S, h * 4 + (i + 1))
                    tt(shifted[i], ps[:, 4 + i % 2, 0:(i + 1) * P], shifted[i], ALU.add).then_inc(h_sc, 1)
                    dve.wait_ge(h_sc, h * 4 + (i + 1))
                    dve.tensor_reduce(rmax[:, i:i + 1], shifted[i], AX.X, ALU.max).then_inc(h_mx, 1)
                    dve.wait_ge(h_mx, h * 4 + (i + 1))
                    dve.tensor_scalar(nmax[:, i:i + 1], rmax[:, i:i + 1], -1.0, None, ALU.mult).then_inc(h_t, 1)

                scores(0)
                scores(1)
                if not last_head:
                    squares(h + 1, 1 - b)
                normalize(dve, h, 0)
                scores(2)
                normalize(dve, h, 1)
                if not last_head:
                    qk_norm(h + 1, 1 - b)
                scores(3)
                normalize(dve, h, 2)
                normalize(dve, h, 3)
                if not last_head:
                    decays(h + 1, 1 - b)

            attention(dve, head_step)

            for group in (1, 2, 3):
                norm(group)

            with dve.Fori(0, 4) as i:
                g = i * 8 + 4 * R_O
                for u in range(4):
                    for c in (2 * u, 2 * u + 1):
                        rest(g, 4 + c)
                    dve.wait_ge(w_used, g + (4 + 2 * u + 2))
                    if u == 0:
                        dve.wait_ge(res_loaded, i * 16 + 16)
                    b = 2 * (u % 2)
                    tt(two(xres[:, u, :]), ps[:, b:b + 2, 0:HALF], two(xres[:, u, :]), ALU.add).then_inc(acc_free[u % 2], 1)
                    dve.wait_ge(acc_free[u % 2], i * 2 + (T_O // 2 + u // 2 + 2))
                    dve.tensor_copy(xT[:, bass.ds(i * 4 + u, 1), :], xres[:, u:u + 1, :]).then_inc(x2_ready, 1)
            dve.wait_ge(x2_ready, KT + 1)
            norm(4)

            fw = par[:, FW:FW + 4 * FT].rearrange("p (j f) -> p j f", j=4)
            dve.memset(abuf[:, :, 0:2], 0.0).then_inc(g_cur, 1)
            dve.wait_ge(g_stT, 2)

            def conv(i, tile, n, u):
                dve.wait_ge(acc_free[n], i * 12 + (T_FF // 2 + u // 2 + 2))
                A = abuf[:, n, :]
                at = tile % FG
                w = [fcur[:, j, at:at + 1] for j in range(3)]
                old = stcur.rearrange("p (b j) f -> p b j f", j=2)[:, :, :, at]
                dve.tensor_copy(ast[:, 0:DEC, bass.ds(i * 4 + tile, 1)], A[:, 514:522].unsqueeze(2))
                dve.tensor_copy(ast[:, DEC:DEC + 2, bass.ds(i * 4 + tile, 1)], A[:, 512:514].unsqueeze(2)).then_inc(g_kept, 1)
                dve.wait_ge(g_hi, i * 4 + (tile + 1))
                dve.wait_ge(g_lo_own, i * 4 + (tile + 1))
                C = cv[:, n, :]
                dve.tensor_scalar(C[:, SEQ:T], old[:, :, 0], w[0], None, ALU.mult)
                dve.tensor_scalar(C[:, 0:SEQ], A[:, 0:512], w[0], None, ALU.mult).then_inc(g_t0, 1)
                dve.wait_ge(g_t0, i * 4 + (tile + 1))
                fma(C[:, SEQ:T], old[:, :, 1], w[1], C[:, SEQ:T])
                fma(C[:, 0:SEQ], A[:, 1:513], w[1], C[:, 0:SEQ]).then_inc(g_t1, 1)
                dve.wait_ge(g_t1, i * 4 + (tile + 1))
                fma(C[:, SEQ:T], A[:, 514:522], w[2], C[:, SEQ:T])
                fma(C[:, 0:SEQ], A[:, 2:514], w[2], C[:, 0:SEQ]).then_inc(g_cv, 1)

            def group_constants(i):
                dve.tensor_copy(fcur, fw[:, :, bass.ds(i * FG, FG)])
                dve.tensor_copy(stcur, stfT[:, :, bass.ds(i * FG, FG)]).then_inc(g_cur, 1)
                dve.wait_ge(g_cur, i + 2)

            def ffn(i, us, first_down):
                g = i * 24 + 4 * R_F
                for u in us:
                    for c in (2 * u, 2 * u + 1):
                        rest(g, 4 + c, down=first_down is not None and 4 + c >= first_down)
                    pair, gate, n = u // 4, (u // 2) % 2, u % 2
                    tile = 2 * pair + n
                    if u == 8:
                        group_constants(i + 1)
                    if not gate:
                        conv(i, tile, n, u)
                    else:
                        dve.wait_ge(w_used, g + (4 + 2 * u + 2))
                        dve.wait_ge(g_silu, i * 4 + (tile + 1))
                        dve.tensor_tensor(two(cv[:, n, :]), ps[:, 2 * n:2 * n + 2, 0:HALF], two(cv[:, n, :]),
                                          ALU.mult).then_inc(acc_free[n], 1)
                        dve.wait_ge(acc_free[n], i * 12 + (T_FF // 2 + u // 2 + 2))
                        dve.sem_inc(g_h, 1)
                        dve.wait_ge(g_hi, i * 4 + (tile + 3))
                        tt(hl[:, tile, :], cv[:, n, :], hh[:, tile, :].bitcast(F32), ALU.subtract).then_inc(g_lo, 1)
                        dve.wait_ge(g_lo, i * 4 + (tile + 1))
                        dve.sem_inc(g_lo_own, 1)
                for c in range(8 if first_down is not None else 0):
                    for m in range(2):
                        dve.wait_ge(*((g_half, i * 8 + (c + 1)) if m == 0 else (w_used, g + (4 + first_down + c + 1))))
                        y = two(xT[:, 2 * c + m, :])
                        tt(y, ps[:, 2 * m:2 * m + 2, 0:HALF], y, ALU.add).then_inc(acc_free[m], 1)
                    if c < 4:
                        rest(g, first_down + 4 + c, down=True)
                    elif first_down == 20:
                        rest(g, 24 + c)

            dve.sem_inc(g_lo_own, 2)
            group_constants(0)
            ffn(0, (0, 1), None)
            with dve.Fori(0, GROUPS - 1) as i:
                ffn(i, range(2, 10), 20)
            ffn(GROUPS - 1, range(2, 8), 16)
            for m in range(2):
                dve.wait_ge(acc_free[m], (GROUPS - 1) * 12 + (T_FF // 2 + 13))
            dve.sem_inc(g_y, 1)
            for i in range(20):
                j, q = divmod(i, 4)
                dve.wait_ge(z_full, i + 1)
                if q == 0 and j >= 2:
                    dve.wait_ge(z_stored[j % 2], 16 * (j // 2))
                n = P if j < 4 else DEC
                dve.tensor_copy(orow[0:n, j % 2, q * 512:(q + 1) * 512], ps[0:n, i % 4, :]).then_inc(z_rows, 1)



_OUTS = [("y_prompt", (1, SEQ, D_MODEL)), ("y_sample", (DEC, 1, D_MODEL)),
         ("k_prompt", (1, 1, SEQ, HEADS, HD)), ("v_prompt", (1, 1, SEQ, HEADS, HD)),
         ("logf_prompt", (1, 1, SEQ, HEADS)), ("pool_prompt", (1, 1, POOL_STATE, 512)),
         ("conv_prompt", (1, 1, 2, 512)), ("ffn_prompt", (1, 1, 2, D_FF)),
         ("k_sample", (1, DEC, 1, HEADS, HD)), ("v_sample", (1, DEC, 1, HEADS, HD)),
         ("logf_sample", (1, DEC, 1, HEADS)), ("pool_sample", (1, DEC, POOL_STATE, 512)),
         ("conv_sample", (1, DEC, 2, 512)), ("ffn_sample", (1, DEC, 2, D_FF))]


def kernel(**inputs):
    import concourse.bacc as bacc
    from concourse.bass_utils import run_bass_kernel_spmd

    nc = bacc.Bacc("TRN2", target_bir_lowering=False, num_devices=1)
    arrays, a, o = {}, {}, {}
    for name, value in inputs.items():
        v = np.ascontiguousarray(value)
        arrays[f"in_{name}"] = v
        a[name] = nc.dram_tensor(f"in_{name}", v.shape, mybir.dt.from_np(v.dtype), kind="ExternalInput").ap()
    for name, shape in _OUTS:
        o[name] = nc.dram_tensor(f"out_{name}", shape, F32, kind="ExternalOutput").ap()
    hybrid_layer_kernel(nc, a, o)
    r = run_bass_kernel_spmd(nc, [arrays], core_ids=[0])
    return tuple(r.results[0][f"out_{name}"] for name, _ in _OUTS)
```

```python
import concourse.bass as bass
import numpy as np
from concourse import mybir
from contextlib import ExitStack

F32 = mybir.dt.float32
F32R = mybir.dt.float32r
I32 = mybir.dt.int32
ALU = mybir.AluOpType
ACT = mybir.ActivationFunctionType
AX = mybir.AxisListType
P = 128

D_MODEL = 2048
SEQ = 512
DEC = 8
T = SEQ + DEC
HALF = T // 2
HEADS = 8
HD = 128
PAST = 4096
PAGES = PAST // P
POOL_G = 4
POOL_STATE = 15
CONV_T = 4
D_FF = 5632
KT = D_MODEL // P
FT = D_FF // P
FG = 4
GROUPS = FT // FG
EPS = 1e-6
SCALE = HD ** -0.5
MASKED = -1e30

T_U, T_B, T_C, T_X, T_Q, T_K, T_V, T_F = 0, 4, 8, 12, 16, 24, 32, 40
G1, G2, GO, PS, CW, QG, KG, FW, FB = 0, 16, 32, 48, 52, 64, 65, 66, 198
PARAM_ROWS = 66
RAW = 4096
CHUNK = 1024
RING = 4
K_PER_CHUNK = [5, 5, 5, 5, 4, 4, 4, 0]
V_PER_CHUNK = [4, 4, 5, 5, 5, 5, 4, 0]


class Count:

    def __init__(self, sem):
        self.sem, self.base, self.n = sem, 0, 0

    def inc(self, ins):
        ins.then_inc(self.sem, 1)
        self.n += 1
        return ins

    def value(self):
        return self.base + self.n

    def loop(self, i, start, per):
        self.base, self.n = i * per + start, 0

    def after(self, value):
        self.base, self.n = value, 0


def hybrid_layer_kernel(nc, a, o):
    ctx = ExitStack()
    with ctx:
        def sb(name, shape, dt=F32):
            return ctx.enter_context(nc.sbuf_tensor("t_" + name, shape, dt))

        def sem(name):
            return ctx.enter_context(nc.semaphore(name))

        with nc.sbuf_tensor("t_aux0", [P, KT * T], F32) as aux0:
            pass
        xh = sb("xh", [P, KT, T], F32R)
        with nc.sbuf_tensor("t_aux1", [P, KT * T], F32) as aux1:
            pass
        xl = sb("xl", [P, KT, T], F32R)
        r1 = sb("r1", [P, KT * T])
        xT = r1[:, :].rearrange("p (k t) -> p k t", k=KT)
        kring = r1[:, 0:RING * 1024].rearrange("p (s n) -> p s n", s=RING)
        vring = r1[:, KT * T - RING * 1024:KT * T].rearrange("p (s n) -> p s n", s=RING)
        wraw = sb("wraw", [P, 2, RAW])
        wh = sb("wh", [P, 4, CHUNK], F32R)
        wl = sb("wl", [P, 4, CHUNK], F32R)
        stg = sb("stg", [P, 2, T])
        ident = sb("ident", [P, P])
        ones = sb("ones", [P, P])
        cmask = sb("cmask", [P, P])
        par = sb("par", [P, 242])
        rc = sb("rc", [P, 16])
        epsc = sb("epsc", [P, 1])
        projS = sb("projS", [P, 40, DEC])
        bf = sb("bf", [HEADS, 1])
        ptr = sb("ptr", [1, DEC * PAGES], I32)
        pti = sb("pti", [P, 2], I32)
        fraw = sb("fraw", [P, KT, HEADS])
        S = sb("S", [P, PAGES, HEADS])
        pr = sb("pr", [P, PAGES, HEADS])
        tri = pr[:, 0:P // HEADS, :].rearrange("p g h -> p (g h)")
        sel = S[0:DEC, :, :].rearrange("p g h -> p (g h)")
        qS = sb("qS", [P, HEADS, DEC])
        sm = sb("sm", [P, HEADS, DEC])
        kSn = sb("kSn", [P, HEADS, DEC])
        maxall = sb("maxall", [P, DEC, HEADS])
        denall = sb("denall", [P, DEC, HEADS])
        ocomb = sb("ocomb", [P, DEC, HEADS])
        mx8 = sb("mx8", [P, HEADS])
        mx1 = sb("mx1", [HEADS, 1])
        mxb = sb("mxb", [P, HEADS])
        diag = sb("diag", [HEADS, HEADS])
        ps8 = sb("ps8", [P, HEADS])
        lfT = sb("lfT", [P, 4, HEADS])
        cqT = sb("cqT", [P, 4, HEADS])
        lfS = sb("lfS", [DEC, HEADS])
        tot = sb("tot", [P, 2, HEADS])
        cqh = sb("cqh", [P, 2, 4])
        rmax = sb("rmax", [P, 4])
        nmax = sb("nmax", [P, 4])
        rsum = sb("rsum", [P, 4])
        qgs = sb("qgs", [P, 1])
        with nc.sbuf_tensor("t_work", [P, 8192], F32) as work:
            pass
        hh = sb("hh", [P, FG, T], F32R)
        hl = sb("hl", [P, FG, T], F32R)
        xr = work[:, :].rearrange("p (s n) -> p s n", s=4)
        sumsq = [work[:, x:x + T] for x in (5648, 5648, 6168, 6688, 5648)]
        rbs = [work[:, x:x + T] for x in (7672, 4608, 5128, 7672, 7672)]
        norm_bank = [4, 0, 0, 6, 4]
        lf = work[:, 0:2048].rearrange("p (c n) -> p c n", c=2)
        Eb = work[:, 2048:4096].rearrange("p (g h) -> p g h", h=HEADS)
        qmask = work[0:DEC, 0:1024]
        junk = work[:, 4096:5120]
        qrows = work[0:DEC, 5120:6144]
        qcur = work[:, 6144:7168]
        osb = work[0:HEADS, 7168:8192]
        shifts = work[:, 1024:1280].rearrange("p (g h) -> p g h", h=HEADS)
        ps = ctx.enter_context(nc.psum_tensor("ps", [P, 8, 512], F32))

        def two(ap):
            return ap.rearrange("p (c t) -> p c t", c=2)

        scr = nc.dram_tensor("scr_proj", (40, P, SEQ), F32, kind="Internal").ap()
        scrx = nc.dram_tensor("scr_x", (KT, P, T), F32, kind="Internal").ap()
        scrc = nc.dram_tensor("scr_c", (HEADS, SEQ), F32, kind="Internal").ap()

        def sems(names):
            return [sem(x) for x in names.split()]

        const_ready, prow_loaded, small_loaded, par_full, par_ready = sems(
            "const_ready param_rows_loaded small_loaded params_transposed params_ready")
        xs_loaded, x_full, x_moved_act, x_moved_dve, x_spilled = sems(
            "x_sample_loaded x_transposed x_moved_by_act x_moved_by_dve x_spilled")
        x_loaded = [sem(f"x_block{j}_loaded") for j in range(4)]
        n_sq, n_sum, n_full, n_log, n_rb, n_tmp, n_hi, n_lo = sems(
            "norm_square_ready norm_square_summed norm_sum_full norm_log_ready norm_rstd_ready norm_scaled_ready "
            "norm_head_ready norm_rest_ready")
        w_loaded = [sem(f"weights_loaded{j}") for j in range(2)]
        w_hi, w_lo, w_used = sems("weight_head_ready weight_rest_ready weight_chunk_used")
        acc_free = [sem(f"accumulators{j}_free") for j in range(2)]
        tile_kept, act_seq, dve_seq = sems("sample_columns_kept act_sequence dve_sequence")
        tile_spilled = [sem(f"tile_spilled{j}") for j in range(2)]
        f_loaded, f_full, f_nz, f_soft, f_cum, f_cols, f_kept, f_stored = sems(
            "f_weights_loaded f_full f_negabs_ready f_softplus_ready "
            "logf_summed logf_columns_full logf_columns_kept logf_stored")
        e_loaded, e_scan, e_tail, e_bias, e_full, e_kept = sems(
            "page_logf_loaded page_logf_summed tails_full biases_ready biases_transposed biases_kept")
        q_sq, q_sum, q_rs, q_n, q_tr, q_rows = sems(
            "q_square_ready q_square_summed q_rstd_ready q_normed q_rows_full q_rows_ready")
        k_loaded = [sem(f"k_page_loaded{j}") for j in range(RING)]
        v_loaded = [sem(f"v_page_loaded{j}") for j in range(RING)]
        k_used, v_used = sems("k_page_used v_page_used")
        q_mask, q_bc, q_cur = sems("q_row_masked q_broadcast_full q_current_ready")
        c_se, c_mx, c_mT, c_m1, c_dg, c_mb, c_sub, c_mk, c_p, c_ps, c_den, c_dk = sems(
            "scores_biased page_max_ready page_max_transposed sequence_max_ready sequence_max_diagonal max_broadcast_full "
            "scores_shifted max_kept probs_ready probs_summed den_full den_kept")
        o_rows, o_cols, o_kept = sems("o_rows_ready o_columns_full o_columns_kept")
        s_e, s_x, s_sq, s_sum, s_rs, s_kn, s_pd, s_sc, s_done = sems(
            "own_exponents_ready own_exp_ready k_square_ready k_square_summed k_rstd_ready k_normed qk_product_ready qk_sum_full sample_mixed")
        r_full, r_copied, r_stored = sems("rows_full rows_copied rows_stored")
        p_loaded, p_states, p_tr, p_stT, p_pooled, p_mm, p_y = sems(
            "pool_inputs_loaded mixer_states_loaded states_transposed states_ready pooled_ready pool_mixed pool_y_ready")
        v_in = [sem(f"conv_inputs{j}_loaded") for j in range(CONV_T)]
        v_done = sem("conv_done")
        h_loaded = sems("head_loaded head_decays_loaded")
        h_stored = sems("head_keys_stored head_values_stored")
        h_rowfree, h_ln, h_free, h_sq, h_sum, h_rs, h_qk, h_rowsF, h_rowsC = sems(
            "head_rows_free head_log_ready head_inputs_free head_squares_ready head_squares_summed head_rstd_ready head_qk_normed head_rows_full "
            "head_rows_copied")
        h_cq, h_bias, h_sc, h_mx, h_ri, h_S, h_t, h_e, h_pn, h_pT, h_pC, h_O, h_done = sems(
            "head_decays_ready head_bias_ready head_scores_ready head_max_ready head_sum_inverted head_scores_full head_scores_shifted head_exp_ready head_probs_ready head_probs_transposed "
            "head_probs_copied head_out_full head_out_ready")
        res_loaded, x2_ready = sems("residual_loaded x2_ready")
        g_states, g_tr, g_stT, g_cur, g_kept, g_cv, g_silu, g_h, g_hi, g_lo, g_half = sems(
            "ffn_states_loaded ffn_states_full ffn_states_ready ffn_columns_ready a_kept conv_ready "
            "silu_ready hidden_ready hidden_head hidden_rest down_tile_full")
        g_t0, g_t1, g_lo_own = sems("tap0_done tap1_done hidden_slot_free")
        z_full, z_ffn, z_act, z_rows, z_rows_act = sems(
            "out_full ffn_rows_full ffn_rows_copied out_rows_ready out_rows_ready_act")
        z_stored = sem("out_stored")
        states_copied = sem("states_copied")

        w_in_v = a["w_in"].rearrange("l (k p) n -> p (l k) n", p=P)
        w_o_v = a["w_o"].rearrange("l (k p) n -> p (l k) n", p=P)
        w_up_v = a["w_up"].rearrange("l (k p) n -> p (l k) n", p=P)
        w_down_v = a["w_down"].rearrange("l (k p) n -> p (l k) n", p=P)
        k_pages = a["cache_k"].rearrange("l g t h d -> (l g) t (h d)")
        v_pages = a["cache_v"].rearrange("l g t h d -> (l g) t (h d)")
        lf_pages = a["cache_logf"].rearrange("l g t h -> (l g) (t h)")
        N_POOL = k_pages.shape[0]

        R_Q, R_IN, R_O, R_F = 0, 4, 20, 28
        T_IN, T_O, T_FF = 8, 40, 56
        N_CONST = 28
        PRIME = RING

        def step(eng, count, ins):
            count.inc(ins)
            eng.wait_ge(count.sem, count.value())

        lgv = work[0:HEADS, 6144:6144 + T]
        fz = work[0:HEADS, 7168:7168 + T]
        fn = junk[0:HEADS, 0:T]
        Pc = work[:, 2048:4096].rearrange("p (c n) -> p c n", c=2)
        lfE = work[:, 0:2048].rearrange("p (c h t) -> p c h t", c=2, h=HEADS)
        ub = aux0[:, 0:2112].rearrange("p (g t) -> p g t", g=POOL_G)
        shA, shB = aux0[:, 2112:2640], aux0[:, 2640:3168]
        pooled = aux0[:, 3168:3688]
        strow = aux0[0:120, 3688:4200]
        cstrow = aux0[0:16, 4200:4712]
        poolw = aux0[:, 4712:5224].rearrange("p (g d) -> p g d", g=POOL_G)
        stT = aux0[:, 5224:5704].rearrange("p (g b) -> p g b", g=POOL_G)
        cstT = aux0[:, 5704:5768].rearrange("p (g b) -> p g b", g=CONV_T)
        rows1 = aux0[0:16, 5768:6792]
        rows2 = aux0[0:16, 6792:7816]
        c3 = aux1[:, 0:CONV_T * 1536].rearrange("p (g c t) -> p g c t", g=CONV_T, c=3)
        ct, cz = aux1[:, 6144:6664], aux1[:, 6664:7178]
        zs4 = aux1[:, 7178:7210]
        zl4 = aux1[:, 7210:7218]
        tmp5 = [work[:, 7816 + 64 * i:7880 + 64 * i] for i in range(5)]
        krs = stg[0:DEC, :, :].rearrange("p a b -> p (a b)")[:, 0:1024]
        vrs = work[0:DEC, 2560:3584]
        qkv = [x[:, 0:1536].rearrange("p (c t) -> p c t", c=3) for x in (aux0, aux1)]
        cb = [x[:, 1536:2048] for x in (aux0, aux1)]
        qk = [x[:, 2048:3072].rearrange("p (c t) -> p c t", c=2) for x in (aux0, aux1)]
        sqs = [x[:, 3072:4096].rearrange("p (c t) -> p c t", c=2) for x in (aux0, aux1)]
        krow = [x[:, 4096:4608] for x in (aux0, aux1)]
        vrow = [x[:, 4608:5120] for x in (aux0, aux1)]
        at = [0, P, 3 * P, 6 * P, 10 * P]
        shifted = [work[:, at[i]:at[i + 1]] for i in range(4)]
        probs2 = [work[:, 1280 + at[i]:1280 + at[i + 1]] for i in range(4)]
        pT = work[:, 2560:4608].rearrange("p (k t) -> p k t", k=4)
        xres = work[:, 0:4 * T].rearrange("p (m t) -> p m t", m=4)
        abuf = work[:, 4160:5204].rearrange("p (s t) -> p s t", s=2)
        cv = work[:, 5204:6244].rearrange("p (s t) -> p s t", s=2)
        fcur = work[:, 6244:6260].rearrange("p (j i) -> p j i", j=4)
        stfT = work[:, 6260:6964].rearrange("p (s f) -> p s f", s=2 * DEC)
        ast = work[:, 6964:7404].rearrange("p (s f) -> p s f", s=DEC + 2)
        stcur = work[:, 7404:7468].rearrange("p (s i) -> p s i", s=2 * DEC)
        strows = work[0:FT, 2080:2080 + 2 * DEC * P].rearrange("p (s n) -> p s n", s=2 * DEC)
        astrows = aux1[0:FT, 2048:2048 + (DEC + 2) * P].rearrange("p (s n) -> p s n", s=DEC + 2)
        orow = aux0[:, 0:8192].rearrange("p (q j n) -> p q j n", q=4, j=4)
        srow = aux1[0:DEC, 0:2048]
        OUT_BLOCKS = SEQ // P + 1

        def out_pieces(q, odd):
            return [(OUT_BLOCKS * q + j, j) for j in range(OUT_BLOCKS) if (OUT_BLOCKS * q + j) % 2 == odd]

        def copy_piece(eng, copy, q, n, j, done):
            eng.wait_ge(z_full, n + 1)
            bank = ps[:, 4 + n % 4, :]
            if j < 4:
                copy(orow[:, q, j, :], bank).then_inc(done, 1)
            else:
                copy(srow[:, q * 512:(q + 1) * 512], bank[0:DEC]).then_inc(done, 1)

        def transposed_probs(pe, tr, h, i):
            pe.wait_ge(h_pn, h * 4 + (i + 1))
            if i >= 2:
                pe.wait_ge(h_pC, h * 4 + (i - 1))
            for k in range(i + 1):
                last = tr(ps[:, 6 + i % 2, k * P:(k + 1) * P], probs2[i][:, k * P:(k + 1) * P], P)
            last.then_inc(h_pT, 1)

        def copy_probs(act, copy, h, i):
            act.wait_ge(h_pT, h * 4 + (i + 1))
            copy(pT[:, 0:i + 1, i * P:(i + 1) * P],
                 ps[:, 6 + i % 2, 0:(i + 1) * P].rearrange("p (k t) -> p k t", t=P)).then_inc(h_pC, 1)

        def normalize(dve, h, i):
            dve.wait_ge(h_e, h * 4 + (i + 1))
            dve.reciprocal(rsum[:, i:i + 1], rsum[:, i:i + 1]).then_inc(h_ri, 1)
            dve.wait_ge(h_ri, h * 4 + (i + 1))
            dve.tensor_scalar(probs2[i], probs2[i], rsum[:, i:i + 1], None, ALU.mult).then_inc(h_pn, 1)

        def attention(eng, step_):
            step_(0, 0, 2)
            step_(1, 1, 2)
            with eng.Fori(1, HEADS // 2 - 1) as j:
                step_(j * 2, 0, 2)
                step_(j * 2 + 1, 1, 2)
            step_(HEADS - 2, 0, 1)
            step_(HEADS - 1, 1, 0)

        block = ctx.enter_context(nc.Block())

        @block.gpsimd
        def _(pool):
            cst = Count(const_ready)
            cst.inc(pool.memset(ident[:, :], 0.0))
            cst.inc(pool.memset(ones[:, :], 1.0))
            cst.inc(pool.memset(cmask[:, :], 0.0))
            cst.inc(pool.memset(tri[:, :], 1.0))
            cst.inc(pool.memset(sel[:, :], 1.0))
            for t in range(16):
                cst.inc(pool.memset(rc[:, t:t + 1], 1.0 / (t + 1)))
            cst.inc(pool.memset(epsc[:, :], EPS))
            pool.wait_ge(const_ready, cst.value())
            cst.inc(pool.affine_select(out=ident[:, :], in_=ident[:, :], compare_op=ALU.not_equal, fill=1.0,
                                       base=0, pattern=[[-1, P]], channel_multiplier=1))
            cst.inc(pool.affine_select(out=cmask[:, :], in_=cmask[:, :], compare_op=ALU.is_ge, fill=MASKED,
                                       base=0, pattern=[[-1, P]], channel_multiplier=1))
            cst.inc(pool.affine_select(out=tri[:, :], in_=tri[:, :], compare_op=ALU.is_ge, fill=0.0,
                                       base=0, pattern=[[-1, P]], channel_multiplier=1))
            pool.wait_ge(const_ready, cst.value())
            tv = tri.rearrange("p (a c) -> p a c", c=PAGES)
            cst.inc(pool.affine_select(out=tv, in_=tv, compare_op=ALU.is_ge, fill=0.0, base=PAGES - 1,
                                       pattern=[[PAGES, P // PAGES], [0, PAGES]], channel_multiplier=-1))
            sv = sel.rearrange("p (a c) -> p a c", c=PAGES)
            cst.inc(pool.affine_select(out=sv, in_=sv, compare_op=ALU.is_equal, fill=0.0, base=0,
                                       pattern=[[-1, DEC], [0, PAGES]], channel_multiplier=1))
            assert cst.value() <= N_CONST, cst.value()
            cst.inc(pool.memset(mx8[:, :], 0.0))
            pool.wait_ge(x_moved_act, 9)
            pool.wait_ge(x_moved_dve, 8)
            pool.dma_start(scrx.rearrange("k p t -> p k t"), xT).then_inc(x_spilled, 16)
            pool.wait_ge(small_loaded, 48)
            pool.wait_ge(n_lo, KT)
            for c in range(2):
                pool.indirect_dma_start(lf[:, c, :], None, lf_pages,
                                        bass.IndirectOffsetOnAxis(ap=pti[:, c:c + 1], axis=0)).then_inc(e_loaded, 16)
            pool.dma_start(o["pool_sample"][0, :, 0:POOL_STATE - 1, :],
                           a["state_pool"][0, :, 1:POOL_STATE, :]).then_inc(states_copied, 16)
            pool.dma_start(o["conv_sample"][0, :, 0:1, :], a["state_conv"][0, :, 1:2, :]).then_inc(states_copied, 16)
            pool.dma_start(o["ffn_sample"][0, :, 0:1, :], a["state_ffn"][0, :, 1:2, :]).then_inc(states_copied, 16)
            pool.wait_ge(f_cum, 1)
            pool.dma_start(scrc, junk[0:HEADS, 0:SEQ]).then_inc(f_stored, 16)
            pool.wait_ge(f_kept, 3)
            pool.dma_start(o["logf_prompt"][0, 0].rearrange("(j p) h -> p j h", p=P), lfT[:, :, :]).then_inc(f_stored, 16)
            pool.dma_start(o["logf_sample"][0, :, 0, :], lfS[:, :]).then_inc(f_stored, 16)

            for n, (dst, src) in enumerate(((o["pool_prompt"][0, 0], rows1[0:POOL_STATE, 0:512]),
                                            (o["pool_sample"][0, :, POOL_STATE - 1, :], rows1[0:DEC, 512:1024]),
                                            (o["conv_prompt"][0, 0], rows2[0:2, 0:512]),
                                            (o["conv_sample"][0, :, 1, :], rows2[0:DEC, 512:1024]),
                                            (o["k_sample"][0, :, 0].rearrange("b h d -> b (h d)"), krs),
                                            (o["v_sample"][0, :, 0].rearrange("b h d -> b (h d)"), vrs))):
                pool.wait_ge(r_copied, n + 1)
                pool.dma_start(dst, src).then_inc(r_stored, 16)

            pool.wait_ge(z_act, 3)
            for b in range(DEC):
                pool.dma_start(o["ffn_sample"][0, b, 1, :].rearrange("(t n) -> t n", n=P),
                               astrows[:, b, :]).then_inc(states_copied, 16)
            for j in range(2):
                pool.dma_start(o["ffn_prompt"][0, 0, j, :].rearrange("(t n) -> t n", n=P),
                               astrows[:, DEC + j, :]).then_inc(states_copied, 16)
            pool.wait_ge(states_copied, 16 * 13)
            pool.wait_ge(f_stored, 48)
            pool.wait_ge(r_stored, 96)

        @block.sync
        def _(sp):
            sp.dma_start(xr[0:DEC, 3, :], a["x_sample"].rearrange("b t d -> (b t) d")).then_inc(xs_loaded, 16)
            xp = a["x_prompt"].rearrange("b (j p) d -> (b j) p d", p=P)
            for j in range(3):
                sp.dma_start(xr[:, j, :], xp[j]).then_inc(x_loaded[j], 16)
            pv = stg[:, :, :].rearrange("p a b -> p (a b)")

            def rows(lo, n, ap):
                at, row = (0, lo) if lo < P else (lo // P, lo % P)
                sp.dma_start(pv[row:row + n, at * P:(at + 1) * P], ap).then_inc(prow_loaded, 16)

            rows(G1, 16, a["norm1_g"][0].rearrange("(k p) -> k p", p=P))
            rows(G2, 16, a["norm2_g"][0].rearrange("(k p) -> k p", p=P))
            rows(GO, 16, a["out_norm_g"][0].rearrange("(k p) -> k p", p=P))
            rows(PS, 4, a["pool_scale"][0].rearrange("(k p) -> k p", p=P))
            for j in range(3):
                rows(CW + 4 * j, 4, a["conv_w"][0, j].rearrange("(k p) -> k p", p=P))
            rows(QG, 1, a["q_norm_g"])
            rows(KG, 1, a["k_norm_g"])
            for j in range(2):
                rows(P + j * FT, FT, a["ffn_conv_w"][0, j].rearrange("(k p) -> k p", p=P))
            rows(2 * P, FT, a["ffn_conv_w"][0, 2].rearrange("(k p) -> k p", p=P))
            rows(2 * P + FT, FT, a["ffn_conv_b"][0].rearrange("(k p) -> k p", p=P))
            sp.dma_start(bf[:, :], a["b_f"].rearrange("l h -> h l"),
                         allow_slow_non_contiguous=True).then_inc(small_loaded, 16)
            sp.dma_start(ptr[:, :], a["page_table"].rearrange("(o b) g -> o (b g)", o=1)).then_inc(small_loaded, 16)
            sp.dma_start(pti[:, :], a["page_table"].rearrange("(c b) g -> (b g) c", c=2),
                         allow_slow_non_contiguous=True).then_inc(small_loaded, 16)
            sp.wait_ge(x_full, 1)
            sp.dma_start(xr[:, 3, :], xp[3]).then_inc(x_loaded[3], 16)
            sp.dma_start(fraw[:, :, :], w_in_v[:, :, T_F * P:T_F * P + HEADS]).then_inc(f_loaded, 16)

            def load_raw(n, slot, source, col, k=KT, width=2 * P):
                sp.wait_ge(w_lo, n * 4 - 4)
                sp.dma_start(wraw[:, slot, :].rearrange("p (k n) -> p k n", k=k),
                             source[:, :, bass.ds(col, width)]).then_inc(w_loaded[slot], 16)

            for n in range(2):
                sp.dma_start(wraw[:, n, :].rearrange("p (k n) -> p k n", k=KT),
                             w_in_v[:, :, (T_Q + 2 * n) * P:(T_Q + 2 * n + 2) * P]).then_inc(w_loaded[n], 16)
            for n in range(2, 4):
                load_raw(n, n % 2, w_in_v, (T_Q + 2 * n) * P)
            for n in range(4, 6):
                load_raw(n, n % 2, w_in_v, 2 * (n - R_IN) * P)

            def page(ring, pages, loads, used, r, p):
                g = sp.value_load(ptr[0:1, bass.ds(r * PAGES + p, 1)], min_val=0, max_val=N_POOL - 1)
                sp.wait_ge(used, r * PAGES + (p + 1))
                sp.dma_start(ring[:, p % RING, :],
                             pages[bass.ds(g, 1), :, :].rearrange("a p n -> (a p) n")).then_inc(loads[p % RING], 16)

            sp.wait_ge(small_loaded, 48)
            sp.wait_ge(n_lo, KT)
            sp.wait_ge(x_spilled, 16)

            def round_loads(r, weights, keys, values):
                kp, vp = 0, 0
                for c in range(8):
                    if weights and c % 4 == 1:
                        weights(c // 4)
                    for n in range(max(K_PER_CHUNK[c], V_PER_CHUNK[c])):
                        if keys and n < K_PER_CHUNK[c]:
                            page(kring, k_pages, k_loaded, k_used, r, kp)
                            kp += 1
                        if values and n < V_PER_CHUNK[c]:
                            page(vring, v_pages, v_loaded, v_used, r - 1, vp)
                            vp += 1

            def next_in(r):
                def load(m):
                    s = r + 1
                    load_raw(r * 2 + (R_IN + 2 + m), m, w_in_v, s * (4 * P) + (s // 4) * (8 * P) + 2 * m * P)
                return load

            def first_o(m):
                load_raw(R_O + m, m, w_o_v, 2 * m * P)

            round_loads(0, next_in(0), True, False)
            with sp.Fori(1, DEC - 1) as r:
                round_loads(r, next_in(r), True, True)
            round_loads(DEC - 1, first_o, True, True)
            for p in range(RING):
                page(vring, v_pages, v_loaded, v_used, DEC - 1, p)
            sp.wait_ge(w_used, 4 * R_O + 4)
            for b in range(2):
                sp.wait_ge(tile_spilled[b], 16 * 20)
            sp.dma_start(strow[:, :], a["state_pool"].rearrange("l b t c -> (l b t) c")).then_inc(p_states, 16)
            sp.dma_start(cstrow[:, :], a["state_conv"].rearrange("l b t c -> (l b t) c")).then_inc(p_states, 16)
            sp.dma_start(poolw, a["pool_w"].rearrange("l g c d -> c (l g) d")).then_inc(p_states, 16)
            sp.dma_start(ub[:, :, 16:528], scr[T_U:T_U + 4].rearrange("g p t -> p g t")).then_inc(p_loaded, 16)
            mixed = scr[T_B:T_B + 12].rearrange("(c g) p t -> g p c t", c=3)
            for p in range(RING, PAGES):
                page(vring, v_pages, v_loaded, v_used, DEC - 1, p)
                if p % RING == 3 and p // RING <= CONV_T:
                    j = p // RING - 1
                    sp.dma_start(c3[:, j], mixed[j]).then_inc(v_in[j], 16)

            src = scr[T_Q:T_Q + 24].rearrange("(c h) p t -> h p c t", c=3)

            def load_head(h, b):
                sp.dma_start(qkv[b], src[bass.ds(h, 1)].rearrange("a p c t -> (a p) c t")).then_inc(h_loaded[0], 16)
                sp.dma_start(cb[b], scrc[bass.ds(h, 1), :].broadcast_to([P, SEQ])).then_inc(h_loaded[1], 16)

            def store_head(h, b):
                for n, (name, row) in enumerate((("v_prompt", vrow[b]), ("k_prompt", krow[b]))):
                    sp.wait_ge(h_rowsC, h * 2 + (n + 1))
                    dst = o[name].rearrange("l b (j p) h d -> p (l b j) h d", p=P)
                    sp.dma_start(dst[:, :, bass.ds(h, 1), :].rearrange("p j a d -> p (j a) d"),
                                 row.rearrange("p (j d) -> p j d", j=4)).then_inc(h_stored[n], 16)

            sp.wait_ge(p_y, 2 * POOL_G)
            sp.wait_ge(r_full, 2)
            load_head(0, 0)
            sp.wait_ge(v_done, CONV_T)
            for n in range(2):
                sp.wait_ge(h_loaded[n], 16)
            load_head(1, 1)
            sp.sem_inc(h_rowfree, 2)
            store_head(0, 0)

            def head_step(h, b, more):
                if more == 2:
                    sp.wait_ge(h_free, h + 1)
                    load_head(h + 2, b)
                for n in range(2):
                    sp.wait_ge(h_stored[n], h * 16 + 16)
                sp.sem_inc(h_rowfree, 1)
                if more:
                    store_head(h + 1, 1 - b)

            attention(sp, head_step)
            sp.wait_ge(h_done, HEADS + 1)
            sp.wait_ge(r_stored, 96)
            sp.dma_start(strows, a["state_ffn"].rearrange("l b j (t n) -> t (l b j) n", n=P)).then_inc(g_states, 16)

            def o_body(i, weights):
                sp.wait_ge(x2_ready, i * 4 + 1)
                sp.dma_start(xres, scrx.rearrange("(i m) p t -> i p m t", m=4)[bass.ds(i, 1)]
                             .rearrange("a p m t -> (a p) m t")).then_inc(res_loaded, 16)
                for m in range(2):
                    weights(i, m)

            with sp.Fori(0, 3) as i:
                o_body(i, lambda i, m: load_raw(i * 2 + (R_O + 2 + m), m, w_o_v, i * (4 * P) + (2 + m) * 2 * P))
            o_body(3, lambda i, m: load_raw(R_F + m, m, w_up_v, m * D_FF))
            def down(i, n, slot, m):
                sp.wait_ge(w_lo, n * 4 - 4)
                rows_ = w_down_v[:, bass.ds(i * FG, FG), 1024 * m:1024 * (m + 1)]
                sp.dma_start(wraw[:, slot, :].rearrange("p (k n) -> p k n", k=FG), rows_).then_inc(w_loaded[slot], 16)

            def ffn_body(i, more):
                n = i * 6 + R_F
                load_raw(n + 2, 0, w_up_v, i * (FG * P) + 2 * P)
                load_raw(n + 3, 1, w_up_v, i * (FG * P) + (D_FF + 2 * P))
                if more:
                    load_raw(n + 4, 0, w_up_v, i * (FG * P) + FG * P)
                    down(i, n + 5, 1, 0)
                    down(i, n + 6, 0, 1)
                    load_raw(n + 7, 1, w_up_v, i * (FG * P) + (FG * P + D_FF))
                else:
                    down(i, n + 4, 0, 0)
                    down(i, n + 5, 1, 1)

            with sp.Fori(0, GROUPS - 1) as i:
                ffn_body(i, True)
            ffn_body(GROUPS - 1, False)
            yp = o["y_prompt"].rearrange("b (j p) d -> p (b j) d", p=P)
            for q in range(4):
                n = OUT_BLOCKS * (q + 1)
                sp.wait_ge(z_rows, (n + 1) // 2)
                sp.wait_ge(z_rows_act, n // 2)
                sp.dma_start(yp[:, :, q * 512:(q + 1) * 512], orow[:, q]).then_inc(z_stored, 16)
            sp.dma_start(o["y_sample"].rearrange("b t d -> (b t) d"), srow).then_inc(z_stored, 16)
            sp.wait_ge(z_stored, 80)

        norm_groups = [(0, KT, G1, D_MODEL), (0, 4, GO, 512), (4, 8, GO + 4, 512), (8, 16, GO + 8, 1024),
                       (0, KT, G2, D_MODEL)]
        norm_first = [0, 16, 20, 24, 32]

        @block.tensor
        def _(pe):
            def mm(out, lhsT, rhs, start=True, stop=True):
                return pe.matmul(out, lhsT, rhs, start=start, stop=stop)

            def tr(out, in_, n):
                return pe.transpose(out, in_, ident[0:n, 0:n])

            pe.sem_inc(w_used, 4)
            pe.sem_inc(v_used, PRIME)
            pe.wait_ge(const_ready, N_CONST)
            pe.wait_ge(xs_loaded, 16)
            for k in range(KT):
                last = tr(ps[:, 6, k * DEC:(k + 1) * DEC], xr[0:DEC, 3, k * P:(k + 1) * P], DEC)
            last.then_inc(x_full, 1)
            for i in range(16):
                j, g = divmod(i, 4)
                if g == 0:
                    pe.wait_ge(x_loaded[j], 16)
                if i >= 4:
                    pe.wait_ge(*((x_moved_act, 1 + (i - 4) // 2 + 1) if i % 2 == 0 else (x_moved_dve, (i - 4) // 2 + 1)))
                for k in range(4):
                    last = tr(ps[:, i % 4, k * P:(k + 1) * P], xr[:, j, (4 * g + k) * P:(4 * g + k + 1) * P], P)
                last.then_inc(x_full, 1)

            pe.wait_ge(prow_loaded, 13 * 16)
            pv = stg[:, :, :].rearrange("p a b -> p (a b)")
            tr(ps[:, 7, 0:66], pv[0:66, 0:P], 66)
            tr(ps[:, 7, 66:154], pv[0:88, P:2 * P], 88)
            tr(ps[:, 7, 154:242], pv[0:88, 2 * P:3 * P], 88).then_inc(par_full, 1)

            def norm(group):
                lo, hi, _, _ = norm_groups[group]
                pe.wait_ge(n_sum, norm_first[group] + hi - lo)
                for c in range(2):
                    last = mm(ps[:, norm_bank[group] + c, 0:HALF], ones[:, :], sumsq[group][:, c * HALF:(c + 1) * HALF])
                last.then_inc(n_full, 1)

            norm(0)

            def f_part(k):
                if k == 0:
                    pe.wait_ge(f_loaded, 16)
                pe.wait_ge(n_tmp, k + 1)
                for c in range(2):
                    last = mm(ps[0:HEADS, 4 + c, 0:HALF], fraw[:, k, :], stg[:, k % 2, c * HALF:(c + 1) * HALF],
                              k == 0, k == KT - 1)
                last.then_inc(f_full, 1)

            def products(s, u, kt):
                k = kt % 8
                block_h = wh[:, s, k * P:(k + 1) * P]
                block_l = wl[:, s, k * P:(k + 1) * P]
                for w, x in ((block_h, xh), (block_h, xl), (block_l, xh)):
                    for b in range(2):
                        last = mm(ps[:, 2 * u + b, 0:HALF], w, x[:, kt, b * HALF:(b + 1) * HALF],
                                  kt == 0 and w is block_h and x is xh, kt == KT - 1 and w is block_l)
                return last

            def first_tiles(g, t, normed, us, before=None):
                for u in us:
                    pe.wait_ge(acc_free[u], t)
                for kt in range(KT):
                    half = kt // 8
                    if before is not None:
                        before(kt)
                    pe.wait_ge(n_lo, normed + kt + 1)
                    if kt % 8 == 0:
                        pe.wait_ge(w_lo, g + 2 * us[-1] + half + 1)
                    for u in us:
                        last = products(2 * u + half, u, kt)
                        if u == 0 and kt == 7:
                            last.then_inc(w_used, 1)
                last.then_inc(w_used, 2 * len(us) - 1)

            def chunk(g, c, t, u, half):
                if half == 0:
                    pe.wait_ge(acc_free[u % 2], t)
                pe.wait_ge(w_lo, g + (c + 1))
                for k in range(8):
                    last = products(c % 4, u % 2, 8 * half + k)
                last.then_inc(w_used, 1)

            def tile(g, t0, u):
                for half in range(2):
                    chunk(g, 2 * u + half, t0 // 2 + (u // 2 + 1), u, half)

            def biases_full(ns):
                pe.wait_ge(e_bias, 1)
                for i in ns:
                    if i >= 2:
                        pe.wait_ge(e_kept, i - 1)
                    for n in range(4):
                        c, h = divmod(4 * i + n, HEADS)
                        last = tr(ps[:, 4 + i % 2, n * P:(n + 1) * P], lfE[:, c, h, :], P)
                    last.then_inc(e_full, 1)

            first_tiles(0, 1, 0, (0,), f_part)
            tile(0, 0, 1)
            pe.wait_ge(f_cum, 1)
            for j in range(4):
                tr(ps[:, 4, j * HEADS:(j + 1) * HEADS], lgv[:, j * P:(j + 1) * P], HEADS)
                tr(ps[:, 4, 32 + j * HEADS:32 + (j + 1) * HEADS], junk[0:HEADS, j * P:(j + 1) * P], HEADS)
            tr(ps[0:DEC, 4, 64:72], lgv[:, SEQ:T], HEADS).then_inc(f_cols, 1)
            tile(0, 0, 2)
            pe.wait_ge(f_kept, 3)
            pe.wait_ge(e_scan, 1)
            for c in range(2):
                mm(ps[:, 5, c * HEADS:(c + 1) * HEADS], tri[:, :], Pc[:, c, 1024 - HEADS:1024], True, False)
                last = mm(ps[:, 5, c * HEADS:(c + 1) * HEADS], sel[:, c * P:(c + 1) * P], lfS[:, :], False, True)
            last.then_inc(e_tail, 1)
            tile(0, 0, 3)
            biases_full((0, 1))
            tile(8, 4, 0)
            biases_full((2, 3))
            for u in range(1, 4):
                tile(8, 4, u)
            pe.wait_ge(q_sq, 1)
            mm(ps[:, 6, 0:64], ones[:, :], sm[:, :, :].rearrange("p h b -> p (h b)")).then_inc(q_sum, 1)
            pe.wait_ge(q_n, 1)
            for h in range(HEADS):
                last = tr(ps[0:DEC, 6 + h // 4, (h % 4) * P:(h % 4 + 1) * P], qS[:, h, :], P)
            last.then_inc(q_tr, 1)

            def broadcast_q(s, half):
                if half == 0:
                    pe.wait_ge(q_mask, s + 1)
                if half or not (isinstance(s, int) and s == 0):
                    pe.wait_ge(q_cur, 2 * s + half)
                mm(ps[:, 6, :], ones[0:DEC, :], qmask[:, half * 512:(half + 1) * 512]).then_inc(q_bc, 1)

            def value_page(r, p):
                pe.wait_ge(v_loaded[p % RING], r * (16 * PAGES // RING) + 16 * (p // RING + 1))
                for c in range(2):
                    last = mm(ps[0:HEADS, 4 + c, :], pr[:, p, :], vring[:, p % RING, c * 512:(c + 1) * 512],
                              p == 0, p == PAGES - 1)
                last.then_inc(v_used, 1)

            def pool_conv(c):
                if c == 2:
                    for b in range(2):
                        pe.wait_ge(acc_free[b], T_O // 2 + 1)
                    pe.wait_ge(p_states, 48)
                    for g in range(POOL_G):
                        tr(ps[:, 0, g * 120:(g + 1) * 120], strow[:, g * P:(g + 1) * P], 120)
                        last = tr(ps[:, 1, g * 16:(g + 1) * 16], cstrow[:, g * P:(g + 1) * P], 16)
                    last.then_inc(p_tr, 1)
                if 3 <= c < 7:
                    g = c - 3
                    pe.wait_ge(p_pooled, g + 1)
                    if g:
                        pe.wait_ge(p_y, 2 * g)
                    mm(ps[:, 2, :], poolw[:, g, :], pooled[:, 0:SEQ])
                    mm(ps[:, 3, 0:DEC], poolw[:, g, :], pooled[:, SEQ:T]).then_inc(p_mm, 1)
                if c == 7:
                    pe.wait_ge(p_stT, 2)
                    for g in range(POOL_G):
                        last = tr(ps[0:POOL_STATE, 0, g * P:(g + 1) * P], ub[:, g, 528 - POOL_STATE:528], P)
                    last.then_inc(r_full, 1)
                    for g in range(POOL_G):
                        last = tr(ps[0:DEC, 1, g * P:(g + 1) * P], projS[:, T_U + g, :], P)
                    last.then_inc(r_full, 1)
                    pe.wait_ge(p_y, 2 * POOL_G)
                    pe.wait_ge(v_done, CONV_T)
                    for j in range(CONV_T):
                        last = tr(ps[0:2, 2, j * P:(j + 1) * P], zl4[:, 2 * j:2 * j + 2], P)
                    last.then_inc(r_full, 1)
                    for j in range(CONV_T):
                        last = tr(ps[0:DEC, 3, j * P:(j + 1) * P], zs4[:, DEC * j:DEC * (j + 1)], P)
                    last.then_inc(r_full, 1)

            def round_(r, keys, more, values):
                p = 0
                for c in range(8):
                    if not keys:
                        pool_conv(c)
                    if c == 7:
                        if more:
                            broadcast_q(r + 1, 0)
                        if keys:
                            pe.wait_ge(c_mx, r + 1)
                            if values:
                                pe.wait_ge(c_dk, r)
                            tr(ps[0:HEADS, 7, 0:P], mx8[:, :], P).then_inc(c_mT, 1)
                    if keys:
                        u, half = divmod(c, 2)
                        chunk(r * 8 + 4 * R_IN, c, r * 2 + (T_IN // 2 + u // 2 + 1), u, half)
                    if values and c == 0:
                        pe.wait_ge(c_p, r)
                        pe.wait_ge(o_rows, r)
                    if values and c == 1:
                        pe.wait_ge(c_ps, r)
                        pe.wait_ge(o_kept, r)
                        mm(ps[:, 7, 136:144], ones[:, :], ps8[:, :]).then_inc(c_den, 1)
                    for _ in range(V_PER_CHUNK[c] if values else 0):
                        value_page(r - 1, p)
                        p += 1
                if more:
                    broadcast_q(r + 1, 1)
                if keys:
                    pe.wait_ge(c_dg, r + 1)
                if values:
                    pe.wait_ge(o_rows, r + 1)
                    pe.wait_ge(c_dk, r)
                    for h in range(HEADS):
                        last = mm(ps[:, 7, 144 + h:145 + h], osb[:, h * P:(h + 1) * P], ident[0:HEADS, h:h + 1])
                    last.then_inc(o_cols, 1)
                if keys:
                    mm(ps[:, 7, P:P + HEADS], ones[0:HEADS, :], diag[:, :]).then_inc(c_mb, 1)

            broadcast_q(0, 0)
            broadcast_q(0, 1)
            round_(0, True, True, False)
            with pe.Fori(1, DEC - 1) as r:
                round_(r, True, True, True)
            round_(DEC - 1, True, False, True)
            round_(DEC, False, False, True)

            pe.wait_ge(o_kept, DEC + 1)
            pe.wait_ge(s_sq, 1)
            mm(ps[:, 6, 0:64], ones[:, :], sm[:, :, :].rearrange("p h b -> p (h b)")).then_inc(s_sum, 1)

            def sum_squares(h, b):
                pe.wait_ge(h_sq, h + 1)
                for c in range(2):
                    last = mm(ps[:, c, :], ones[:, :], sqs[b][:, c, :])
                last.then_inc(h_sum, 1)

            def rows_of(h, b, n):
                if n:
                    pe.wait_ge(h_qk, h + 1)
                for j in range(4):
                    src = (qk[b][:, 1], qkv[b][:, 2])[1 - n]
                    last = tr(ps[:, 3 - n, j * P:(j + 1) * P], src[:, j * P:(j + 1) * P], P)
                last.then_inc(h_rowsF, 1)

            pe.wait_ge(r_copied, 4)
            sum_squares(0, 0)
            pe.wait_ge(h_ln, 1)
            sum_squares(1, 1)
            pe.wait_ge(s_pd, 1)
            mm(ps[:, 6, 64:128], ones[:, :], tmp5[0]).then_inc(s_sc, 1)
            for h in range(HEADS):
                last = tr(ps[0:DEC, 2 + h // 4, (h % 4) * P:(h % 4 + 1) * P], kSn[:, h, :], P)
            last.then_inc(r_full, 1)
            for h in range(HEADS):
                last = tr(ps[0:DEC, 4 + h // 4, (h % 4) * P:(h % 4 + 1) * P], projS[:, T_V + h, :], P)
            last.then_inc(r_full, 1)
            pe.wait_ge(r_copied, 6)
            rows_of(0, 0, 0)
            rows_of(0, 0, 1)
            pe.wait_ge(s_done, 1)

            def scores(h, b, i):
                n = (i + 1) * P
                if i >= 2:
                    pe.wait_ge(h_t, h * 4 + (i - 1))
                mm(ps[:, 4 + i % 2, 0:n], qk[b][:, 0, i * P:(i + 1) * P], qk[b][:, 1, 0:n]).then_inc(h_S, 1)

            def head_step(h, b, more):
                scores(h, b, 2)
                transposed_probs(pe, tr, h, 0)
                scores(h, b, 3)
                transposed_probs(pe, tr, h, 1)
                if more:
                    pe.wait_ge(h_rowsC, h * 2 + 2)
                    pe.wait_ge(h_done, h + 1)
                    rows_of(h + 1, 1 - b, 0)
                transposed_probs(pe, tr, h, 2)
                if more:
                    rows_of(h + 1, 1 - b, 1)
                transposed_probs(pe, tr, h, 3)
                if more:
                    scores(h + 1, 1 - b, 0)
                    scores(h + 1, 1 - b, 1)
                if more == 2:
                    pe.wait_ge(h_ln, h + 2)
                    sum_squares(h + 2, b)
                else:
                    pe.wait_ge(*((h_ln, HEADS) if more else (n_log, 2)))
                    norm(2 - more)
                pe.wait_ge(h_pC, h * 4 + 4)
                pe.wait_ge(h_rowsC, h * 2 + (3 if more else 2))
                if not more:
                    pe.wait_ge(h_done, h + 1)
                for k in range(4):
                    last = mm(ps[:, 3, k * P:SEQ], vrow[b][:, k * P:(k + 1) * P], pT[:, k, k * P:SEQ], k == 0, k == 3)
                last.then_inc(h_O, 1)

            scores(0, 0, 0)
            scores(0, 0, 1)
            attention(pe, head_step)
            pe.wait_ge(h_done, HEADS + 1)

            norm(3)
            pe.wait_ge(n_rb, 4)
            first_tiles(4 * R_O, T_O // 2 + 1, 16, (0, 1))

            def out_tiles(i, us):
                for u in us:
                    for half in range(2):
                        chunk(i * 8 + 4 * R_O, 2 * u + half, i * 2 + (T_O // 2 + u // 2 + 1), u, half)

            out_tiles(0, (2, 3))
            with pe.Fori(1, 4) as i:
                out_tiles(i, range(4))
            pe.wait_ge(g_states, 16)
            for s in range(2 * DEC):
                last = tr(ps[:, 6 + s // 11, (s % 11) * FT:(s % 11 + 1) * FT], strows[:, s, :], FT)
            last.then_inc(g_tr, 1)
            norm(4)

            def up(i, c0, us):
                for u in us:
                    for half in range(2):
                        chunk(i * 24 + 4 * R_F, c0 + 2 * u + half, i * 12 + (T_FF // 2 + u // 2 + 1), u, half)

            def down(i, c0, t0, after=None):
                g = i * 24 + 4 * R_F
                for c in range(8):
                    pe.wait_ge(w_lo, g + (c0 + c + 1))
                    if c == 0:
                        pe.wait_ge(g_lo, i * 4 + 4)
                    for m in range(2):
                        pe.wait_ge(acc_free[m], i * 12 + (t0 + c + 1))
                        for k in range(FG):
                            at = k * 256 + m * P
                            block_h = wh[:, c % 4, at:at + P]
                            block_l = wl[:, c % 4, at:at + P]
                            for w, x in ((block_h, hh), (block_h, hl), (block_l, hh)):
                                for b in range(2):
                                    last = mm(ps[:, 2 * m + b, 0:HALF], w, x[:, k, b * HALF:(b + 1) * HALF],
                                              k == 0 and w is block_h and x is hh, k == FG - 1 and w is block_l)
                        last.then_inc(g_half if m == 0 else w_used, 1)
                    if after is not None:
                        after(c)

            def out_quarter(q):
                for j in range(OUT_BLOCKS):
                    n = OUT_BLOCKS * q + j
                    if n < 4:
                        pe.wait_ge(z_act, 3)
                    else:
                        pe.wait_ge(z_rows if n % 2 == 0 else z_rows_act, (n - 4) // 2 + 1)
                    size = P if j < 4 else DEC
                    for k in range(4):
                        last = tr(ps[0:size, 4 + n % 4, k * P:(k + 1) * P], xT[:, 4 * q + k, j * P:j * P + size], P)
                    last.then_inc(z_full, 1)

            first_tiles(4 * R_F, T_FF // 2 + 1, 32, (0, 1))
            with pe.Fori(0, GROUPS - 1) as i:
                up(i, 0, range(2, 10))
                down(i, 20, T_FF // 2 + 5)
            up(GROUPS - 1, 0, range(2, 8))
            pe.wait_ge(g_kept, FT)
            for s in range(DEC + 2):
                last = tr(ps[0:FT, 4 + s // 4, (s % 4) * P:(s % 4 + 1) * P], ast[:, s, :], P)
            last.then_inc(z_ffn, 1)
            down(GROUPS - 1, 16, T_FF // 2 + 4, lambda c: out_quarter(c // 2 - 1) if c in (2, 4, 6) else None)
            for m in range(2):
                pe.wait_ge(acc_free[m], (GROUPS - 1) * 12 + (T_FF // 2 + 13))
            out_quarter(3)

        @block.scalar
        def _(act):
            seq = Count(act_seq)

            def copy(out, in_):
                return act.activation(out, in_, ACT.Copy)

            for b in range(2):
                act.sem_inc(acc_free[b], 1)
            act.sem_inc(o_rows, 1)
            act.sem_inc(g_hi, 2)
            act.wait_ge(x_full, 1)
            copy(xT[:, :, SEQ:T], ps[:, 6, 0:KT * DEC].rearrange("p (k b) -> p k b", k=KT)).then_inc(x_moved_act, 1)
            for i in range(0, 16, 2):
                j, g = divmod(i, 4)
                act.wait_ge(x_full, i + 2)
                copy(xT[:, 4 * g:4 * g + 4, j * P:(j + 1) * P],
                     ps[:, i % 4, :].rearrange("p (k t) -> p k t", k=4)).then_inc(x_moved_act, 1)

            def square(t, dst):
                act.activation(dst, xT[:, bass.ds(t, 1), :], ACT.Square).then_inc(n_sq, 1)

            def squares(group):
                lo, hi, _, _ = norm_groups[group]
                for t in range(lo, hi):
                    n = norm_first[group] + t - lo
                    if t == lo:
                        square(t, sumsq[group].unsqueeze(1))
                        continue
                    if n >= 3:
                        act.wait_ge(n_sum, n - 1)
                    square(t, stg[:, n % 2:n % 2 + 1, :])
                    if group == 0 and t >= 9 and t % 2:
                        head(0, (t - 9) // 2)

            def rstds(groups):
                for group in groups:
                    act.wait_ge(n_full, group + 1)
                    b = norm_bank[group]
                    act.activation(two(rbs[group]), ps[:, b:b + 2, 0:HALF], ACT.Ln, bias=epsc[:, :],
                                   scale=1.0 / norm_groups[group][3]).then_inc(n_log, 1)
                for group in groups:
                    act.wait_ge(n_log, group + 1)
                    act.activation(rbs[group], rbs[group], ACT.Exp, scale=-0.5).then_inc(n_rb, 1)

            def heads(group):
                lo, hi, _, _ = norm_groups[group]
                for t in range(lo, hi):
                    n = norm_first[group] + t - lo
                    act.wait_ge(n_tmp, n + 1)
                    copy(xh[:, t, :], stg[:, n % 2, :]).then_inc(n_hi, 1)

            def raw_chunk(c, down):
                raw, q = wraw[:, (c // 4) % 2, :], c % 4
                if down:
                    return raw.rearrange("p (k n) -> p k n", k=FG)[:, :, q * 256:(q + 1) * 256]
                m, half = divmod(q, 2)
                return raw.rearrange("p (k n) -> p k n", k=KT)[:, half * 8:half * 8 + 8, m * P:(m + 1) * P]

            def blocks(buf, c, down):
                return buf[:, c % 4, :].rearrange("p (k n) -> p k n", k=FG if down else 8)

            def head(g, c, down=False):
                if c % 4 == 0:
                    act.wait_ge(w_loaded[(c // 4) % 2], g * 2 + 16 * (c // 8 + 1))
                act.wait_ge(w_used, g + (c + 1))
                copy(blocks(wh, c, down), raw_chunk(c, down)).then_inc(w_hi, 1)

            act.wait_ge(par_full, 1)
            copy(par[:, :], ps[:, 7, 0:242]).then_inc(par_ready, 1)
            act.wait_ge(x_moved_dve, 8)
            act.wait_ge(x_moved_act, 9)
            squares(0)
            rstds((0,))
            heads(0)

            def move_tile(t, u, dst, used):
                s = u % 2
                act.wait_ge(w_used, used)
                if not (isinstance(t, int) and t + u < 2):
                    act.wait_ge(tile_spilled[s], t * 8 + 16 * (u // 2))
                    act.wait_ge(tile_kept, t + (u - 1))
                act.activation(two(stg[:, s, :]), ps[:, 2 * s:2 * s + 2, 0:HALF], ACT.Copy).then_inc(acc_free[s], 1)
                act.wait_ge(acc_free[s], t // 2 + (u // 2 + 2))
                copy(projS[:, bass.ds(dst, 1), :], stg[:, s:s + 1, SEQ:T]).then_inc(tile_kept, 1)
                act.dma_start(scr[bass.ds(dst, 1)].rearrange("a p t -> (a p) t"), stg[:, s, 0:SEQ]).then_inc(tile_spilled[s], 16)

            act.wait_ge(f_nz, 1)
            step(act, seq, act.activation(fn, fn, ACT.Exp))
            act.activation(fn, fn, ACT.Ln, bias=1.0).then_inc(f_soft, 1)
            for i in range(2):
                for u in range(4):
                    for c in (2 * u, 2 * u + 1):
                        head(8 * i, 4 + c)
                    move_tile(4 * i, u, T_Q + 4 * i + u, 4 + 8 * i + 2 * u + 2)
                    if (i, u) == (0, 1):
                        act.wait_ge(f_cols, 1)
                        copy(lfT[:, :, :], ps[:, 4, 0:32].rearrange("p (j h) -> p j h", j=4)).then_inc(f_kept, 1)
                        copy(cqT[:, :, :], ps[:, 4, 32:64].rearrange("p (j h) -> p j h", j=4)).then_inc(f_kept, 1)
                        copy(lfS[:, :], ps[0:DEC, 4, 64:72]).then_inc(f_kept, 1)
                    for n in {(0, 3): (0, 1), (1, 0): (2, 3)}.get((i, u), ()):
                        act.wait_ge(e_full, n + 1)
                        c, h = divmod(4 * n, HEADS)
                        copy(Eb[:, c * P:(c + 1) * P, h:h + 4].rearrange("p g h -> p h g"),
                             ps[:, 4 + n % 2, :].rearrange("p (h g) -> p h g", h=4)).then_inc(e_kept, 1)

            def rstd64(summed, done):
                act.wait_ge(summed, 1)
                v = sm[:, :, :].rearrange("p h b -> p (h b)")
                step(act, seq, act.activation(v, ps[:, 6, 0:64], ACT.Ln, bias=epsc[:, :], scale=1.0 / HD))
                act.activation(v, v, ACT.Exp, scale=-0.5).then_inc(done, 1)

            rstd64(q_sum, q_rs)
            act.wait_ge(q_tr, 1)
            copy(qrows.rearrange("p (c n) -> p c n", c=2), ps[0:DEC, 6:8, :]).then_inc(q_rows, 1)

            def take_q(s, half):
                act.wait_ge(q_bc, s * 2 + (half + 1))
                if half == 0:
                    act.wait_ge(k_used, s * PAGES + PRIME)
                copy(qcur[:, half * 512:(half + 1) * 512], ps[:, 6, :]).then_inc(q_cur, 1)

            def round_(r, keys, more, values):
                g = r * 8 + 4 * R_IN
                for u in range(4):
                    for c in (2 * u, 2 * u + 1):
                        if c == 7:
                            if more:
                                take_q(r + 1, 0)
                            if values:
                                act.wait_ge(v_used, r * PAGES + PRIME)
                                copy(osb.rearrange("p (c n) -> p c n", c=2), ps[0:HEADS, 4:6, :]).then_inc(o_rows, 1)
                        if keys:
                            head(g, 4 + c)
                    if keys:
                        move_tile(r * 4 + T_IN, u, r * 4 + (r // 4) * 8 + u, g + (4 + 2 * u + 2))
                if more:
                    take_q(r + 1, 1)
                if keys:
                    act.wait_ge(c_sub, r + 1)
                    act.activation(pr[:, :, :], shifts, ACT.Exp).then_inc(c_p, 1)

            take_q(0, 0)
            take_q(0, 1)
            round_(0, True, True, False)
            with act.Fori(1, DEC - 1) as r:
                round_(r, True, True, True)
            round_(DEC - 1, True, False, True)
            act.wait_ge(p_tr, 1)
            copy(stT, ps[:, 0, 0:480].rearrange("p (g b) -> p g b", g=POOL_G)).then_inc(p_stT, 1)
            copy(cstT, ps[:, 1, 0:64].rearrange("p (g b) -> p g b", g=CONV_T)).then_inc(p_stT, 1)
            for g in range(POOL_G):
                act.wait_ge(p_mm, g + 1)
                act.activation(xT[:, g, 0:SEQ], ps[:, 2, :], ACT.Copy, scale=par[:, PS + g:PS + g + 1]).then_inc(p_y, 1)
                act.activation(xT[:, g, SEQ:T], ps[:, 3, 0:DEC], ACT.Copy,
                               scale=par[:, PS + g:PS + g + 1]).then_inc(p_y, 1)
            for n, (out, in_) in enumerate(((rows1[0:POOL_STATE, 0:512], ps[0:POOL_STATE, 0, :]),
                                            (rows1[0:DEC, 512:1024], ps[0:DEC, 1, :]),
                                            (rows2[0:2, 0:512], ps[0:2, 2, :]),
                                            (rows2[0:DEC, 512:1024], ps[0:DEC, 3, :]))):
                act.wait_ge(r_full, 1 + n)
                copy(out, in_).then_inc(r_copied, 1)
            for b in range(2):
                act.wait_ge(tile_spilled[b], 16 * 20)
            for group in (1, 2):
                squares(group)
            round_(DEC, False, False, True)

            def head_rstd(h, b):
                act.wait_ge(h_sum, h + 1)
                act.activation(sqs[b], ps[:, 0:2, :], ACT.Ln, bias=epsc[:, :], scale=1.0 / HD).then_inc(h_ln, 1)
                act.wait_ge(h_ln, h + 1)
                act.activation(sqs[b], sqs[b], ACT.Exp, scale=-0.5).then_inc(h_rs, 1)

            def head_rows(h, b, n):
                act.wait_ge(h_rowsF, h * 2 + (n + 1))
                if n == 0:
                    act.wait_ge(h_rowfree, h + 1)
                copy((vrow, krow)[n][b], ps[:, 3 - n, :]).then_inc(h_rowsC, 1)

            rstd64(s_sum, s_rs)
            head_rstd(0, 0)
            head_rstd(1, 1)
            act.wait_ge(s_e, 1)
            act.activation(tmp5[2], tmp5[2], ACT.Exp).then_inc(s_x, 1)
            act.activation(tmp5[3], tmp5[3], ACT.Exp).then_inc(s_x, 1)
            act.wait_ge(r_full, 5)
            act.wait_ge(n_sum, 24)
            copy(krs.rearrange("p (c n) -> p c n", c=2), ps[0:DEC, 2:4, :]).then_inc(r_copied, 1)
            act.wait_ge(r_full, 6)
            copy(vrs.rearrange("p (c n) -> p c n", c=2), ps[0:DEC, 4:6, :]).then_inc(r_copied, 1)
            head_rows(0, 0, 0)
            head_rows(0, 0, 1)

            act.sem_inc(h_done, 1)
            act.wait_ge(s_done, 1)

            def exps(h, i):
                act.wait_ge(h_t, h * 4 + (i + 1))
                act.activation(probs2[i], shifted[i], ACT.Exp, bias=nmax[:, i:i + 1],
                               accum_out=rsum[:, i:i + 1]).then_inc(h_e, 1)

            def head_step(h, b, more):
                if isinstance(h, int) and h == 0:
                    act.wait_ge(r_stored, 96)
                copy_probs(act, copy, h, 0)
                squared = not (isinstance(h, int) and h == 0)
                if squared:
                    act.wait_ge(h_done, h + 1)
                    act.wait_ge(n_sum, h + 22)
                exps(h, 2)
                if squared:
                    square(h + 7, stg[:, 1 - b:2 - b, :])
                copy_probs(act, copy, h, 1)
                if more:
                    head_rows(h + 1, 1 - b, 0)
                exps(h, 3)
                copy_probs(act, copy, h, 2)
                if more:
                    head_rows(h + 1, 1 - b, 1)
                copy_probs(act, copy, h, 3)
                if more:
                    exps(h + 1, 0)
                    exps(h + 1, 1)
                if more == 2:
                    head_rstd(h + 2, b)
                elif more:
                    rstds((1,))
                act.wait_ge(h_O, h + 1)
                copy(xT[:, bass.ds(h + 8, 1), 0:SEQ], ps[:, 3:4, :]).then_inc(h_done, 1)

            exps(0, 0)
            exps(0, 1)
            attention(act, head_step)
            act.wait_ge(h_done, HEADS + 1)
            act.wait_ge(n_sum, 30)
            square(KT - 1, stg[:, 1:2, :])
            for n in range(2):
                act.wait_ge(h_stored[n], 16 * HEADS)

            heads(1)
            rstds((2, 3))
            heads(2)
            heads(3)

            act.wait_ge(n_lo, 32)
            with act.Fori(0, 4) as i:
                for u in range(4):
                    for c in (2 * u, 2 * u + 1):
                        head(i * 8 + 4 * R_O, 4 + c)
                    act.wait_ge(x2_ready, i * 4 + (u + 2))
                    act.wait_ge(n_sum, i * 4 + (31 + u))
                    square(i * 4 + u, stg[:, u % 2:u % 2 + 1, :])
            act.wait_ge(g_tr, 1)
            copy(stfT[:, 0:11, :], ps[:, 6, 0:484].rearrange("p (s f) -> p s f", f=FT)).then_inc(g_stT, 1)
            copy(stfT[:, 11:16, :], ps[:, 7, 0:220].rearrange("p (s f) -> p s f", f=FT)).then_inc(g_stT, 1)
            rstds((4,))
            heads(4)

            def ffn(i, us, first_down):
                g = i * 24 + 4 * R_F
                for u in us:
                    for c in (2 * u, 2 * u + 1):
                        head(g, 4 + c, down=first_down is not None and 4 + c >= first_down)
                    act.wait_ge(w_used, g + (4 + 2 * u + 2))
                    pair, gate, n = u // 4, (u // 2) % 2, u % 2
                    if not gate:
                        act.wait_ge(g_cv, i * 4 + (2 * pair + n + 1))
                        act.activation(abuf[:, n, 2:2 + T].rearrange("p (c t) -> p c t", c=2),
                                       ps[:, 2 * n:2 * n + 2, 0:HALF], ACT.Copy).then_inc(acc_free[n], 1)
                    else:
                        tile = 2 * pair + n
                        act.wait_ge(g_cv, i * 4 + (tile + 3))
                        act.activation(cv[:, n, :], cv[:, n, :], ACT.Silu, bias=fcur[:, 3, tile:tile + 1])\
                           .then_inc(g_silu, 1)
                        act.wait_ge(g_h, i * 4 + (tile + 1))
                        copy(hh[:, tile, :], cv[:, n, :]).then_inc(g_hi, 1)
                if first_down == 20:
                    for c in range(8):
                        head(g, 24 + c, down=c < 4)
                elif first_down is not None:
                    act.wait_ge(z_ffn, 1)
                    for n, (lo, hi) in enumerate(((0, 4), (4, 8), (8, 10))):
                        copy(astrows[:, lo:hi, :], ps[0:FT, 4 + n, 0:(hi - lo) * P].rearrange("p (s n) -> p s n", n=P))\
                            .then_inc(z_act, 1)
                    for c in range(4):
                        head(g, first_down + 4 + c, down=True)
                    for q in range(4):
                        for n, j in out_pieces(q, 1):
                            copy_piece(act, copy, q, n, j, z_rows_act)

            ffn(0, (0, 1), None)
            with act.Fori(0, GROUPS - 1) as i:
                ffn(i, range(2, 10), 20)
            ffn(GROUPS - 1, range(2, 8), 16)

        @block.vector
        def _(dve):
            seq = Count(dve_seq)

            def tt(out, in0, in1, op):
                return dve.tensor_tensor(out, in0, in1, op)

            def fma(out, in0, scalar, in1):
                return dve.scalar_tensor_tensor(out, in0, scalar, in1, ALU.mult, ALU.add)

            dve.sem_inc(k_used, PRIME)
            dve.sem_inc(x2_ready, 1)
            dve.sem_inc(o_kept, 1)
            dve.sem_inc(g_cv, 2)
            for i in range(1, 16, 2):
                j, g = divmod(i, 4)
                dve.wait_ge(x_full, i + 2)
                dve.tensor_copy(xT[:, 4 * g:4 * g + 4, j * P:(j + 1) * P],
                                ps[:, i % 4, :].rearrange("p (k t) -> p k t", k=4)).then_inc(x_moved_dve, 1)

            def add_square(group, slot, n):
                dve.wait_ge(n_sq, n + 1)
                dve.wait_ge(n_sum, n)
                tt(sumsq[group], sumsq[group], stg[:, slot, :], ALU.add).then_inc(n_sum, 1)

            def sums(group):
                lo, hi, _, _ = norm_groups[group]
                n0 = norm_first[group]
                dve.wait_ge(n_sq, n0 + 1)
                if n0:
                    dve.wait_ge(n_sum, n0)
                dve.sem_inc(n_sum, 1)
                for n in range(n0 + 1, n0 + hi - lo):
                    add_square(group, n % 2, n)

            def norm(group):
                lo, hi, gcol, _ = norm_groups[group]
                n0 = norm_first[group]
                if group == 1:
                    dve.wait_ge(n_sum, 32)
                dve.wait_ge(n_rb, group + 1)

                def rest(t):
                    n = n0 + t - lo
                    dve.wait_ge(n_hi, n + 1)
                    tt(xl[:, t, :], stg[:, n % 2, :], xh[:, t, :].bitcast(F32), ALU.subtract).then_inc(n_lo, 1)

                for t in range(lo, hi):
                    n = n0 + t - lo
                    if t - lo >= 2 or group in (2, 3):
                        dve.wait_ge(n_lo, n - 1)
                        if group == 0:
                            dve.wait_ge(f_full, n - 1)
                    dve.scalar_tensor_tensor(stg[:, n % 2, :], xT[:, t, :], par[:, gcol + t - lo:gcol + t - lo + 1],
                                             rbs[group],
                                             ALU.mult, ALU.mult).then_inc(n_tmp, 1)
                    if t > lo:
                        rest(t - 1)
                rest(hi - 1)

            def raw_chunk(c, down):
                raw, q = wraw[:, (c // 4) % 2, :], c % 4
                if down:
                    return raw.rearrange("p (k n) -> p k n", k=FG)[:, :, q * 256:(q + 1) * 256]
                m, half = divmod(q, 2)
                return raw.rearrange("p (k n) -> p k n", k=KT)[:, half * 8:half * 8 + 8, m * P:(m + 1) * P]

            def blocks(buf, c, down):
                return buf[:, c % 4, :].rearrange("p (k n) -> p k n", k=FG if down else 8)

            def weight_rest(g, c, down=False):
                dve.wait_ge(w_hi, g + (c + 1))
                tt(blocks(wl, c, down), raw_chunk(c, down), blocks(wh, c, down).bitcast(F32),
                   ALU.subtract).then_inc(w_lo, 1)

            dve.wait_ge(par_ready, 1)
            dve.tensor_scalar(qgs[:, :], par[:, QG:QG + 1], SCALE, None, ALU.mult)
            dve.wait_ge(x_moved_act, 9)
            dve.wait_ge(x_moved_dve, 8)
            sums(0)
            for c in range(4):
                weight_rest(0, c)
            norm(0)

            dve.wait_ge(small_loaded, 48)
            dve.wait_ge(f_full, KT)
            step(dve, seq, dve.tensor_scalar(two(fz), ps[0:HEADS, 4:6, 0:HALF], bf[:, :], None, ALU.add))
            dve.scalar_tensor_tensor(fn, fz, -1.0, fz, ALU.mult, ALU.min).then_inc(f_nz, 1)
            dve.wait_ge(f_soft, 1)
            step(dve, seq, dve.scalar_tensor_tensor(lgv, fz, 0.0, fn, ALU.min, ALU.subtract))
            dve.tensor_tensor_scan(out=junk[0:HEADS, 0:SEQ], data0=lgv[:, 0:SEQ], data1=lgv[:, 0:SEQ], initial=0.0,
                                   op0=ALU.add, op1=ALU.bypass).then_inc(f_cum, 1)
            for c in range(16):
                if c == 3:
                    dve.wait_ge(e_loaded, 32)
                    lf4 = work[:, 0:2048].rearrange("p (c t h) -> p c t h", c=2, h=HEADS)
                    P4 = work[:, 2048:4096].rearrange("p (c t h) -> p c t h", c=2, h=HEADS)
                    for n in range(2):
                        for h in range(HEADS):
                            last = dve.tensor_tensor_scan(out=P4[:, n, :, h], data0=lf4[:, n, :, h],
                                                          data1=lf4[:, n, :, h], initial=0.0,
                                                          op0=ALU.add, op1=ALU.bypass)
                    last.then_inc(e_scan, 1)
                weight_rest(0, 4 + c)
                if c == 5:
                    dve.wait_ge(e_tail, 1)
                    step(dve, seq, dve.tensor_copy(tot[:, :, :], ps[:, 5, 0:16].rearrange("p (c h) -> p c h", c=2)))
                    for n in range(2):
                        for h in range(HEADS):
                            last = dve.tensor_scalar(lfE[:, n, h, :], P4[:, n, :, h], -1.0, tot[:, n, h:h + 1],
                                                     ALU.mult, ALU.add)
                    last.then_inc(e_bias, 1)
            dve.wait_ge(tile_kept, 8)
            tt(sm[:, :, :], projS[:, T_Q:T_Q + HEADS, :], projS[:, T_Q:T_Q + HEADS, :], ALU.mult).then_inc(q_sq, 1)
            dve.wait_ge(q_rs, 1)
            dve.scalar_tensor_tensor(qS[:, :, :], projS[:, T_Q:T_Q + HEADS, :], par[:, QG:QG + 1], sm[:, :, :],
                                     ALU.mult, ALU.mult).then_inc(q_n, 1)
            dve.wait_ge(q_rows, 1)
            dve.wait_ge(f_stored, 48)
            dve.wait_ge(e_kept, 4)

            def key_page(r, p):
                dve.wait_ge(k_loaded[p % RING], r * (16 * PAGES // RING) + 16 * (p // RING + 1))
                dve.wait_ge(k_used, r * PAGES + (p + PRIME))
                for h in range(HEADS):
                    last = dve.tensor_tensor_reduce(
                        out=junk[:, h * HD:(h + 1) * HD], in0=kring[:, p % RING, h * HD:(h + 1) * HD],
                        in1=qcur[:, h * HD:(h + 1) * HD], scale=SCALE, scalar=0.0, op0=ALU.mult, op1=ALU.add,
                        accum_out=S[:, p, h:h + 1])
                last.then_inc(k_used, 1)

            def pool_conv():
                dve.wait_ge(w_used, 4 * R_O + 4)
                dve.memset(ub[:, :, 0:16], 0.0)
                dve.memset(shA[:, 0:16], 0.0)
                step(dve, seq, dve.memset(shB[:, 0:16], 0.0))
                dve.wait_ge(p_loaded, 16)
                dve.wait_ge(p_stT, 2)
                n_mm = 0
                for g in range(POOL_G):
                    win = 2 << g
                    cur = ub[:, g, :]
                    for n in range(g + 1):
                        nxt = shA if n % 2 == 0 else shB
                        sh = 1 << n
                        step(dve, seq, tt(nxt[:, 16:528], cur[:, 16:528], cur[:, 16 - sh:528 - sh], ALU.add))
                        cur = nxt
                    if g:
                        dve.wait_ge(p_mm, g)
                    step(dve, seq, tt(pooled[:, 0:win], cur[:, 16:16 + win], rc[:, 0:win], ALU.mult))
                    step(dve, seq, tt(pooled[:, 0:win], pooled[:, 0:win], ub[:, g, 16:16 + win], ALU.subtract))
                    step(dve, seq, dve.scalar_tensor_tensor(pooled[:, win:SEQ], cur[:, 16 + win:528], 1.0 / win,
                                                            ub[:, g, 16 + win:528], ALU.mult, ALU.subtract))
                    old = stT[:, g, :].rearrange("p (b t) -> p b t", b=DEC)[:, :, POOL_STATE + 1 - win:POOL_STATE]
                    step(dve, seq, dve.tensor_reduce(pooled[:, SEQ:T], old, AX.X, ALU.add))
                    step(dve, seq, tt(pooled[:, SEQ:T], pooled[:, SEQ:T], projS[:, T_U + g, :], ALU.add))
                    dve.scalar_tensor_tensor(pooled[:, SEQ:T], pooled[:, SEQ:T], 1.0 / win, projS[:, T_U + g, :],
                                             ALU.mult, ALU.subtract).then_inc(p_pooled, 1)

                def tap(j, t):
                    return par[:, CW + 4 * j + t:CW + 4 * j + t + 1]

                step(dve, seq, dve.memset(cz[:, 0:2], 0.0))
                for t in range(CONV_T):
                    dve.wait_ge(v_in[t], 16)
                    cs = cstT[:, t, :].rearrange("p (b j) -> p b j", j=2)
                    zs = zs4[:, DEC * t:DEC * (t + 1)]
                    tt(zs, projS[:, T_C + t, :], projS[:, T_X + t, :], ALU.mult)
                    step(dve, seq, tt(cz[:, 2:514], c3[:, t, 1, :], c3[:, t, 2, :], ALU.mult))
                    dve.tensor_copy(zl4[:, 2 * t:2 * t + 2], cz[:, 512:514])
                    dve.tensor_scalar(ct[:, SEQ:T], cs[:, :, 0], tap(0, t), None, ALU.mult)
                    step(dve, seq, dve.tensor_scalar(ct[:, 0:SEQ], cz[:, 0:512], tap(0, t), None, ALU.mult))
                    fma(ct[:, SEQ:T], cs[:, :, 1], tap(1, t), ct[:, SEQ:T])
                    step(dve, seq, fma(ct[:, 0:SEQ], cz[:, 1:513], tap(1, t), ct[:, 0:SEQ]))
                    fma(ct[:, SEQ:T], zs, tap(2, t), ct[:, SEQ:T])
                    step(dve, seq, fma(ct[:, 0:SEQ], cz[:, 2:514], tap(2, t), ct[:, 0:SEQ]))
                    tt(xT[:, 4 + t, SEQ:T], ct[:, SEQ:T], projS[:, T_B + t, :], ALU.mult)
                    tt(xT[:, 4 + t, 0:SEQ], ct[:, 0:SEQ], c3[:, t, 0, :], ALU.mult).then_inc(v_done, 1)
                    dve.wait_ge(v_done, t + 1)

            def mask_q(s):
                if not (isinstance(s, int) and s == 0):
                    dve.wait_ge(q_bc, s * 2)
                dve.tensor_scalar(qmask, qrows, ident[0:DEC, bass.ds(s, 1)], None, ALU.mult).then_inc(q_mask, 1)

            def round_(r, keys, more, values):
                g = r * 8 + 4 * R_IN
                if values:
                    dve.wait_ge(c_p, r)
                    dve.tensor_reduce(ps8[:, :], pr[:, :, :].rearrange("p g h -> p h g"), AX.X, ALU.add).then_inc(c_ps, 1)
                if keys:
                    dve.wait_ge(q_cur, r * 2 + 2)
                p = 0
                for c in range(8):
                    if c == 5 and more:
                        mask_q(r + 1)
                    if c == 2 and values:
                        if not keys:
                            pool_conv()
                            sums(1)
                            sums(2)
                        dve.wait_ge(c_den, r)
                        dve.tensor_copy(denall[:, bass.ds(r - 1, 1), :], ps[:, 7:8, 136:144]).then_inc(c_dk, 1)
                    if c == 7 and keys:
                        dve.wait_ge(k_used, r * PAGES + (PAGES + PRIME))
                        if values:
                            dve.wait_ge(c_p, r)
                        tt(shifts, S[:, :, :], Eb[:, bass.ds(r * PAGES, PAGES), :], ALU.add).then_inc(c_se, 1)
                        dve.wait_ge(c_se, r + 1)
                        dve.tensor_reduce(mx8[:, :], shifts.rearrange("p g h -> p h g"), AX.X, ALU.max).then_inc(c_mx, 1)
                        dve.wait_ge(c_mT, r + 1)
                        dve.tensor_reduce(mx1[:, :], ps[0:HEADS, 7, 0:P], AX.X, ALU.max).then_inc(c_m1, 1)
                        dve.wait_ge(c_m1, r + 1)
                        dve.tensor_scalar(diag[:, :], ident[0:HEADS, 0:HEADS], mx1[:, :], None, ALU.mult).then_inc(c_dg, 1)
                    for _ in range(min(3, K_PER_CHUNK[c]) if keys else 0):
                        key_page(r, p)
                        p += 1
                    if keys:
                        weight_rest(g, 4 + c)
                    for _ in range(K_PER_CHUNK[c] - 3 if keys else 0):
                        key_page(r, p)
                        p += 1
                if keys:
                    dve.wait_ge(c_mb, r + 1)
                    dve.tensor_copy(mxb[:, :], ps[:, 7, P:P + HEADS]).then_inc(c_mk, 1)
                if values:
                    dve.wait_ge(o_cols, r)
                    dve.tensor_copy(ocomb[:, bass.ds(r - 1, 1), :], ps[:, 7:8, 144:152]).then_inc(o_kept, 1)
                if keys:
                    dve.wait_ge(c_mk, r + 1)
                    tt(shifts, shifts, mxb[:, :].unsqueeze(1).broadcast_to([P, PAGES, HEADS]),
                       ALU.subtract).then_inc(c_sub, 1)
                    dve.tensor_copy(maxall[:, bass.ds(r, 1), :], mxb[:, :].unsqueeze(1))

            mask_q(0)
            round_(0, True, True, False)
            with dve.Fori(1, DEC - 1) as r:
                round_(r, True, True, True)
            round_(DEC - 1, True, False, True)
            round_(DEC, False, False, True)

            def squares(h, b):
                dve.wait_ge(h_loaded[0], h * 16 + 16)
                dve.wait_ge(h_loaded[1], h * 16 + 16)
                tt(sqs[b], qkv[b][:, 0:2, :], qkv[b][:, 0:2, :], ALU.mult).then_inc(h_sq, 1)
                dve.tensor_copy(cqh[:, b, :], cqT[:, :, bass.ds(h, 1)].rearrange("p j a -> p (j a)")).then_inc(h_cq, 1)

            def qk_norm(h, b):
                dve.wait_ge(h_rs, h + 1)
                for n, g in enumerate((qgs[:, :], par[:, KG:KG + 1])):
                    last = dve.scalar_tensor_tensor(qk[b][:, n, :], qkv[b][:, n, :], g, sqs[b][:, n, :],
                                                    ALU.mult, ALU.mult)
                last.then_inc(h_qk, 1)

            def decays(h, b):
                dve.wait_ge(h_cq, h + 1)
                for i in range(4):
                    last = dve.tensor_scalar(shifted[i], cb[b][:, 0:(i + 1) * P], -1.0, cqh[:, b, i:i + 1],
                                             ALU.mult, ALU.add)
                last.then_inc(h_bias, 1)
                dve.wait_ge(h_bias, h * 2 + 1)
                for i in range(4):
                    d = shifted[i][:, i * P:(i + 1) * P]
                    last = tt(d, d, cmask[:, :], ALU.add)
                last.then_inc(h_bias, 1)
                dve.wait_ge(h_bias, h * 2 + 2)
                dve.wait_ge(h_rowsF, h * 2 + 2)
                dve.sem_inc(h_free, 1)

            squares(0, 0)
            squares(1, 1)
            kv = projS[:, T_K:T_K + HEADS, :]
            dve.wait_ge(tile_kept, 40)
            tt(sm[:, :, :], kv, kv, ALU.mult).then_inc(s_sq, 1)
            dve.wait_ge(s_rs, 1)
            dve.scalar_tensor_tensor(kSn[:, :, :], kv, par[:, KG:KG + 1], sm[:, :, :], ALU.mult, ALU.mult).then_inc(s_kn, 1)
            dve.wait_ge(s_kn, 1)
            t3 = [t.rearrange("p (h b) -> p h b", h=HEADS) for t in tmp5]
            hb = [t[:, :, :].rearrange("p b h -> p h b") for t in (maxall, denall, ocomb)]
            tt(t3[0], qS[:, :, :], kSn[:, :, :], ALU.mult).then_inc(s_pd, 1)
            qk_norm(0, 0)
            dve.wait_ge(s_sc, 1)
            own = ps[:, 6, 64:128].rearrange("p (h b) -> p h b", h=HEADS)
            dve.wait_ge(c_dk, DEC)
            step(dve, seq, dve.tensor_scalar(t3[4], own, SCALE, None, ALU.mult))
            step(dve, seq, tt(t3[1], t3[4], hb[0], ALU.max))
            tt(t3[2], hb[0], t3[1], ALU.subtract)
            tt(t3[3], t3[4], t3[1], ALU.subtract).then_inc(s_e, 1)
            dve.wait_ge(s_x, 2)
            step(dve, seq, tt(t3[0], hb[1], t3[2], ALU.mult))
            step(dve, seq, tt(t3[0], t3[0], t3[3], ALU.add))
            step(dve, seq, dve.reciprocal(t3[4], t3[0]))
            step(dve, seq, tt(t3[1], hb[2], t3[2], ALU.mult))
            step(dve, seq, tt(t3[3], t3[3], projS[:, T_V:T_V + HEADS, :], ALU.mult))
            step(dve, seq, tt(t3[1], t3[1], t3[3], ALU.add))
            tt(xT[:, 8:16, SEQ:T], t3[1], t3[4], ALU.mult).then_inc(s_done, 1)
            decays(0, 0)

            def head_step(h, b, more):
                def scores(i):
                    dve.wait_ge(h_S, h * 4 + (i + 1))
                    tt(shifted[i], ps[:, 4 + i % 2, 0:(i + 1) * P], shifted[i], ALU.add).then_inc(h_sc, 1)
                    dve.wait_ge(h_sc, h * 4 + (i + 1))
                    dve.tensor_reduce(rmax[:, i:i + 1], shifted[i], AX.X, ALU.max).then_inc(h_mx, 1)
                    dve.wait_ge(h_mx, h * 4 + (i + 1))
                    dve.tensor_scalar(nmax[:, i:i + 1], rmax[:, i:i + 1], -1.0, None, ALU.mult).then_inc(h_t, 1)

                scores(0)
                scores(1)
                normalize(dve, h, 0)
                normalize(dve, h, 1)
                scores(2)
                if more:
                    qk_norm(h + 1, 1 - b)
                scores(3)
                if not (isinstance(h, int) and h == 0):
                    add_square(3, 1 - b, h + 23)
                normalize(dve, h, 2)
                if more == 2:
                    squares(h + 2, b)
                normalize(dve, h, 3)
                if more:
                    decays(h + 1, 1 - b)

            step(dve, seq, dve.memset(sumsq[3], 0.0))
            attention(dve, head_step)
            add_square(3, 1, 31)

            for group in (1, 2, 3):
                norm(group)

            step(dve, seq, dve.memset(sumsq[4], 0.0))
            with dve.Fori(0, 4) as i:
                g = i * 8 + 4 * R_O
                for u in range(4):
                    for c in (2 * u, 2 * u + 1):
                        weight_rest(g, 4 + c)
                    dve.wait_ge(w_used, g + (4 + 2 * u + 2))
                    if u == 0:
                        dve.wait_ge(res_loaded, i * 16 + 16)
                    b = 2 * (u % 2)
                    tt(two(xres[:, u, :]), ps[:, b:b + 2, 0:HALF], two(xres[:, u, :]), ALU.add).then_inc(acc_free[u % 2], 1)
                    dve.wait_ge(acc_free[u % 2], i * 2 + (T_O // 2 + u // 2 + 2))
                    dve.tensor_copy(xT[:, bass.ds(i * 4 + u, 1), :], xres[:, u:u + 1, :]).then_inc(x2_ready, 1)
                    add_square(4, u % 2, i * 4 + (32 + u))
            dve.wait_ge(x2_ready, KT + 1)
            norm(4)

            fw = par[:, FW:FW + 4 * FT].rearrange("p (j f) -> p j f", j=4)
            dve.memset(abuf[:, :, 0:2], 0.0).then_inc(g_cur, 1)
            dve.wait_ge(g_stT, 2)

            def conv(i, tile, n, u):
                dve.wait_ge(acc_free[n], i * 12 + (T_FF // 2 + u // 2 + 2))
                A = abuf[:, n, :]
                at = tile % FG
                w = [fcur[:, j, at:at + 1] for j in range(3)]
                old = stcur.rearrange("p (b j) f -> p b j f", j=2)[:, :, :, at]
                dve.tensor_copy(ast[:, 0:DEC, bass.ds(i * 4 + tile, 1)], A[:, 514:522].unsqueeze(2))
                dve.tensor_copy(ast[:, DEC:DEC + 2, bass.ds(i * 4 + tile, 1)], A[:, 512:514].unsqueeze(2)).then_inc(g_kept, 1)
                dve.wait_ge(g_hi, i * 4 + (tile + 1))
                dve.wait_ge(g_lo_own, i * 4 + (tile + 1))
                C = cv[:, n, :]
                dve.tensor_scalar(C[:, SEQ:T], old[:, :, 0], w[0], None, ALU.mult)
                dve.tensor_scalar(C[:, 0:SEQ], A[:, 0:512], w[0], None, ALU.mult).then_inc(g_t0, 1)
                dve.wait_ge(g_t0, i * 4 + (tile + 1))
                fma(C[:, SEQ:T], old[:, :, 1], w[1], C[:, SEQ:T])
                fma(C[:, 0:SEQ], A[:, 1:513], w[1], C[:, 0:SEQ]).then_inc(g_t1, 1)
                dve.wait_ge(g_t1, i * 4 + (tile + 1))
                fma(C[:, SEQ:T], A[:, 514:522], w[2], C[:, SEQ:T])
                fma(C[:, 0:SEQ], A[:, 2:514], w[2], C[:, 0:SEQ]).then_inc(g_cv, 1)

            def group_constants(i):
                dve.tensor_copy(fcur, fw[:, :, bass.ds(i * FG, FG)])
                dve.tensor_copy(stcur, stfT[:, :, bass.ds(i * FG, FG)]).then_inc(g_cur, 1)
                dve.wait_ge(g_cur, i + 2)

            def ffn(i, us, first_down):
                g = i * 24 + 4 * R_F
                for u in us:
                    for c in (2 * u, 2 * u + 1):
                        weight_rest(g, 4 + c, down=first_down is not None and 4 + c >= first_down)
                    pair, gate, n = u // 4, (u // 2) % 2, u % 2
                    tile = 2 * pair + n
                    if u == 8:
                        group_constants(i + 1)
                    if not gate:
                        conv(i, tile, n, u)
                    else:
                        dve.wait_ge(w_used, g + (4 + 2 * u + 2))
                        dve.wait_ge(g_silu, i * 4 + (tile + 1))
                        dve.tensor_tensor(two(cv[:, n, :]), ps[:, 2 * n:2 * n + 2, 0:HALF], two(cv[:, n, :]),
                                          ALU.mult).then_inc(acc_free[n], 1)
                        dve.wait_ge(acc_free[n], i * 12 + (T_FF // 2 + u // 2 + 2))
                        dve.sem_inc(g_h, 1)
                        dve.wait_ge(g_hi, i * 4 + (tile + 3))
                        tt(hl[:, tile, :], cv[:, n, :], hh[:, tile, :].bitcast(F32), ALU.subtract).then_inc(g_lo, 1)
                        dve.wait_ge(g_lo, i * 4 + (tile + 1))
                        dve.sem_inc(g_lo_own, 1)
                for c in range(8 if first_down is not None else 0):
                    for m in range(2):
                        dve.wait_ge(*((g_half, i * 8 + (c + 1)) if m == 0 else (w_used, g + (4 + first_down + c + 1))))
                        y = two(xT[:, 2 * c + m, :])
                        tt(y, ps[:, 2 * m:2 * m + 2, 0:HALF], y, ALU.add).then_inc(acc_free[m], 1)
                    if c < 4:
                        weight_rest(g, first_down + 4 + c, down=True)
                    elif first_down == 20:
                        weight_rest(g, 24 + c)
                    if first_down == 16 and c in (2, 4, 6):
                        for n, j in out_pieces(c // 2 - 1, 0):
                            copy_piece(dve, dve.tensor_copy, c // 2 - 1, n, j, z_rows)

            dve.sem_inc(g_lo_own, 2)
            group_constants(0)
            ffn(0, (0, 1), None)
            with dve.Fori(0, GROUPS - 1) as i:
                ffn(i, range(2, 10), 20)
            ffn(GROUPS - 1, range(2, 8), 16)
            for n, j in out_pieces(3, 0):
                copy_piece(dve, dve.tensor_copy, 3, n, j, z_rows)


_OUTS = [("y_prompt", (1, SEQ, D_MODEL)), ("y_sample", (DEC, 1, D_MODEL)),
         ("k_prompt", (1, 1, SEQ, HEADS, HD)), ("v_prompt", (1, 1, SEQ, HEADS, HD)),
         ("logf_prompt", (1, 1, SEQ, HEADS)), ("pool_prompt", (1, 1, POOL_STATE, 512)),
         ("conv_prompt", (1, 1, 2, 512)), ("ffn_prompt", (1, 1, 2, D_FF)),
         ("k_sample", (1, DEC, 1, HEADS, HD)), ("v_sample", (1, DEC, 1, HEADS, HD)),
         ("logf_sample", (1, DEC, 1, HEADS)), ("pool_sample", (1, DEC, POOL_STATE, 512)),
         ("conv_sample", (1, DEC, 2, 512)), ("ffn_sample", (1, DEC, 2, D_FF))]


def kernel(**inputs):
    import concourse.bacc as bacc
    from concourse.bass_utils import run_bass_kernel_spmd

    nc = bacc.Bacc("TRN2", target_bir_lowering=False, num_devices=1)
    arrays, a, o = {}, {}, {}
    for name, value in inputs.items():
        v = np.ascontiguousarray(value)
        arrays[f"in_{name}"] = v
        a[name] = nc.dram_tensor(f"in_{name}", v.shape, mybir.dt.from_np(v.dtype), kind="ExternalInput").ap()
    for name, shape in _OUTS:
        o[name] = nc.dram_tensor(f"out_{name}", shape, F32, kind="ExternalOutput").ap()
    hybrid_layer_kernel(nc, a, o)
    r = run_bass_kernel_spmd(nc, [arrays], core_ids=[0])
    return tuple(r.results[0][f"out_{name}"] for name, _ in _OUTS)
```
